# Optimizing a Trainium2 kernel written in Bass

```python
import math
import jax, jax.numpy as jnp
from jax import lax
import numpy as np

'''Two layers of a hybrid diffusion / flow-matching backbone over latent tokens.

Inputs: x (BATCH, SEQ, D_MODEL) noisy latent tokens on a GRID_W-wide grid,
c (BATCH, D_MODEL) conditioning vector, ctx (BATCH, CTX_LEN, D_MODEL) context
prefix tokens, c_ctx (D_MODEL,) learned modulation vector for context tokens,
plus per-layer parameters stacked on a leading DEPTH axis.
Output: the latent stream (BATCH, SEQ, D_MODEL).

Each layer: adaLN-modulated token-mixing sublayer made of three parallel
branches (differential attention with 2-D axial rotary, grouped 2-D Fourier
mixing, bidirectional RWKV-7 time mixing) fed by one combined input projection,
merged by per-channel sigmoid gates, one output projection; then an
adaLN-modulated ConvGLU channel mixer. Both sublayers use DeepNorm
post-normalisation x <- LN(alpha * x + gate * f(x)).
'''

D_MODEL = 1024
BATCH = 1
SEQ = 512
DEPTH = 2

CTX_LEN = 256
GRID_W = 64

HA = 8
DH_A = 64
DV_A = 2 * DH_A
D_A = HA * DV_A
ROPE_BASE = 10000.0
Q_BLOCK = 128
F_GROUPS = 4
F_GROUP_W = 128
D_F = F_GROUPS * F_GROUP_W
HC = 8
HS_C = 64
D_C = HC * HS_C
LORA_W = 64
LORA_A = 64
LORA_G = 128
D_CS = 2 * D_C + 2 * LORA_W + 2 * LORA_A
D_CO = D_C + LORA_G
N_BRANCH = 3
D_FF = 2816
CONV_W = 3
LN_EPS = 1e-5
GN_EPS = HS_C * 1e-5
HEAD_NORM_EPS = 1e-5

IN_GROUPS = (('q', HA * 2 * DH_A), ('k', HA * 2 * DH_A), ('v', D_A), ('f', D_F),
             ('cs', D_CS), ('co', D_CO), ('gate', N_BRANCH * D_MODEL))
D_IN = 2 * HA * 2 * DH_A + D_A + D_F + D_CS + D_CO + N_BRANCH * D_MODEL

kernel_name = 'hybrid_diffattn_fnet_rwkv7_prefix_block'

def _ln_plain(x):
    xf = x.astype(jnp.float32)
    mu = jnp.mean(xf, axis=-1, keepdims=True)
    var = jnp.mean(jnp.square(xf - mu), axis=-1, keepdims=True)
    return ((xf - mu) * lax.rsqrt(var + LN_EPS)).astype(x.dtype)

def _layernorm(x, g, b):
    return _ln_plain(x) * g + b

def _modulate(x, shift, scale):
    return _ln_plain(x) * (1.0 + scale) + shift

def _in_proj(h, w_in, names=None):
    out, off = {}, 0
    for name, width in IN_GROUPS:
        if names is None or name in names:
            out[name] = h @ w_in[:, off:off + width]
        off += width
    return out

def _shift_prev(x):
    return jnp.pad(x, ((0, 0), (1, 0), (0, 0)))[:, :-1]

def _shift_next(x):
    return jnp.pad(x, ((0, 0), (0, 1), (0, 0)))[:, 1:]

def _token_shift(p, mu):
    return p + mu[0] * (_shift_prev(p) - p) + mu[1] * (_shift_next(p) - p)

def _dwconv3(x, w, b):
    return w[0] * _shift_prev(x) + w[1] * x + w[2] * _shift_next(x) + b

def _rope_angles(n_tokens):
    rows = n_tokens // GRID_W
    row = jnp.repeat(jnp.arange(rows), GRID_W).astype(jnp.float32)
    col = jnp.tile(jnp.arange(GRID_W), rows).astype(jnp.float32)
    n_freq = DH_A // 4
    inv = ROPE_BASE ** (-jnp.arange(n_freq, dtype=jnp.float32) / n_freq)
    ang = jnp.stack([row[:, None] * inv, col[:, None] * inv], axis=1)
    return jnp.cos(ang), jnp.sin(ang)

def _apply_rope(x, cos, sin):
    sh = x.shape
    xr = x.reshape(sh[:-1] + (2, 2, DH_A // 4))
    x1, x2 = xr[..., 0, :], xr[..., 1, :]
    c = cos[None, :, None, None].astype(x.dtype)
    s = sin[None, :, None, None].astype(x.dtype)
    return jnp.stack([x1 * c - x2 * s, x2 * c + x1 * s], axis=-2).reshape(sh)

def _diff_attend(parts, lam):
    scale = DH_A ** -0.5
    s = jnp.concatenate([jnp.einsum('bqhcd,bkhcd->bhcqk', q, k).astype(jnp.float32) for q, k, _ in parts], axis=-1) * scale
    p = jax.nn.softmax(s, axis=-1)
    a = (p[:, :, 0] - lam * p[:, :, 1]).astype(parts[0][2].dtype)
    out, off = None, 0
    for _, k, v in parts:
        n = k.shape[1]
        t = jnp.einsum('bhqk,bkhe->bqhe', a[..., off:off + n], v)
        out = t if out is None else out + t
        off += n
    return out

def _latent_diff_attn(q, k, v, kc, vc, cos, sin, lam):
    B, T = q.shape[:2]
    qr = _apply_rope(q, cos, sin)
    kr = _apply_rope(k, cos, sin)
    nb = T // Q_BLOCK

    def to_blocks(t):
        return jnp.moveaxis(t.reshape((B, nb, Q_BLOCK) + t.shape[2:]), 1, 0)

    def blk(qs):
        q_rot, q_plain = qs
        return _diff_attend([(q_rot, kr, v), (q_plain, kc, vc)], lam)

    o = lax.map(blk, (to_blocks(qr), to_blocks(q)))
    return jnp.moveaxis(o, 0, 1).reshape((B, T) + o.shape[3:])

def _diff_out(o, subln_g, lam_init):
    B, T = o.shape[:2]
    of = o.astype(jnp.float32)
    of = of * lax.rsqrt(jnp.mean(jnp.square(of), axis=-1, keepdims=True) + HEAD_NORM_EPS) * subln_g * (1.0 - lam_init)
    return of.reshape(B, T, D_A).astype(o.dtype)

def _fourier(pf):
    B, T, _ = pf.shape
    z = jnp.fft.fftn(pf.astype(jnp.float32).reshape(B, T, F_GROUPS, F_GROUP_W), axes=(1, 3), norm='ortho')
    return z.real.reshape(B, T, D_F).astype(pf.dtype)

def _heads(t):
    return t.reshape(t.shape[:-1] + (HC, HS_C))

def _l2norm_heads(t):
    th = _heads(t).astype(jnp.float32)
    th = th / jnp.maximum(jnp.sqrt(jnp.sum(jnp.square(th), axis=-1, keepdims=True)), 1e-12)
    return th.reshape(t.shape).astype(t.dtype)

def _two(t):
    return jnp.broadcast_to(t, (2,) + t.shape)

def _dir_stack(t):
    return _heads(jnp.stack([t[0], jnp.flip(t[1], axis=1)]))

def _wkv_scan(decay, kd, v, kk, b, s0, r=None):
    xs = [decay, kd, v, kk, b] + ([r] if r is not None else [])
    xs = tuple(jnp.moveaxis(t.astype(jnp.float32), 2, 0) for t in xs)

    def step(s, inp):
        w_t, k_t, v_t, kk_t, b_t = inp[:5]
        sk = jnp.einsum('dbhvk,dbhk->dbhv', s, kk_t)
        s = s * w_t[..., None, :] - sk[..., None] * b_t[..., None, :] + v_t[..., None] * k_t[..., None, :]
        y = jnp.einsum('dbhvk,dbhk->dbhv', s, inp[5]) if len(inp) == 6 else None
        return s, y

    s_fin, y = lax.scan(step, s0.astype(jnp.float32), xs)
    return s_fin, (None if y is None else jnp.moveaxis(y, 0, 2))

def _rwkv_state_inputs(cs, lp):
    B, T, _ = cs.shape
    k, v, wd, ad = jnp.split(cs, [D_C, 2 * D_C, 2 * D_C + 2 * LORA_W], axis=-1)
    wd = wd.reshape(B, T, 2, LORA_W)
    ad = ad.reshape(B, T, 2, LORA_A)
    wlog = -jax.nn.softplus(-(lp['w0'][:, None, None, :] + jnp.einsum('btdr,drc->dbtc', jnp.tanh(wd), lp['w2'])).astype(jnp.float32)) - 0.5
    decay = jnp.exp(-jnp.exp(wlog))
    a = jax.nn.sigmoid(lp['a0'][:, None, None, :] + jnp.einsum('btdr,drc->dbtc', ad, lp['a2']))
    kk = _l2norm_heads(k * lp['k_k'])
    kd = k * (1.0 + (a - 1.0) * lp['k_a'])
    b = kk * a
    return v, decay, kd, kk, b

def _rwkv_branch(cs, co, s0, lp, want_out):
    B, T, _ = cs.shape
    v, decay, kd, kk, b = _rwkv_state_inputs(cs, lp)
    scan_in = [_dir_stack(t) for t in (decay, kd, _two(v), _two(kk), b)]
    if not want_out:
        s_fin, _ = _wkv_scan(*scan_in, s0)
        return s_fin, None
    r, gd = jnp.split(co, [D_C], axis=-1)
    s_fin, y = _wkv_scan(*scan_in, s0, r=_dir_stack(_two(r)))
    y = y[0] + jnp.flip(y[1], axis=1)
    mu = jnp.mean(y, axis=-1, keepdims=True)
    var = jnp.mean(jnp.square(y - mu), axis=-1, keepdims=True)
    yn = (y - mu) * lax.rsqrt(var + GN_EPS) * _heads(lp['ln_w']) + _heads(lp['ln_b'])
    bonus = jnp.sum(_heads(r)[None] * _heads(kd) * lp['r_k'], axis=(0, -1))[..., None] * _heads(v)
    g = jax.nn.sigmoid(gd) @ lp['g2']
    return s_fin, (yn.astype(v.dtype) + bonus).reshape(B, T, D_C) * g

def _merge(gate_pre, o_a, o_f, o_c, lp):
    g = jax.nn.sigmoid(gate_pre).reshape(gate_pre.shape[:-1] + (N_BRANCH, D_MODEL))
    y = g[..., 0, :] * (o_a @ lp['w_pa']) + g[..., 1, :] * (o_f @ lp['w_pf']) + g[..., 2, :] * (o_c @ lp['w_pc'])
    return y @ lp['w_o']

def _ctx_mixer(hc, lp, lam, lam_init, want_out):
    B, L, _ = hc.shape
    P = _in_proj(hc, lp['w_in'], None if want_out else ('k', 'v', 'cs'))
    k = P['k'].reshape(B, L, HA, 2, DH_A)
    v = P['v'].reshape(B, L, HA, DV_A)
    cs = _token_shift(P['cs'], lp['mu'][:, :D_CS])
    s0 = jnp.zeros((2, B, HC, HS_C, HS_C), jnp.float32)
    if not want_out:
        s_fin, _ = _rwkv_branch(cs, None, s0, lp, False)
        return (k, v, s_fin), None
    co = _token_shift(P['co'], lp['mu'][:, D_CS:])
    s_fin, o_c = _rwkv_branch(cs, co, s0, lp, True)
    q = P['q'].reshape(B, L, HA, 2, DH_A)
    o_a = _diff_out(_diff_attend([(q, k, v)], lam), lp['subln'], lam_init)
    o_f = _fourier(P['f'])
    return (k, v, s_fin), _merge(P['gate'], o_a, o_f, o_c, lp)

def _latent_mixer(h, lp, lam, lam_init, cache, cos, sin):
    kc, vc, s_ctx = cache
    B, T, _ = h.shape
    P = _in_proj(h, lp['w_in'])
    q = P['q'].reshape(B, T, HA, 2, DH_A)
    k = P['k'].reshape(B, T, HA, 2, DH_A)
    v = P['v'].reshape(B, T, HA, DV_A)
    o_a = _diff_out(_latent_diff_attn(q, k, v, kc, vc, cos, sin, lam), lp['subln'], lam_init)
    o_f = _fourier(P['f'])
    cs = _token_shift(P['cs'], lp['mu'][:, :D_CS])
    co = _token_shift(P['co'], lp['mu'][:, D_CS:])
    _, o_c = _rwkv_branch(cs, co, s_ctx, lp, True)
    return _merge(P['gate'], o_a, o_f, o_c, lp)

def _conv_ffn(h, lp):
    u, g = jnp.split(h @ lp['ffn_up'], 2, axis=-1)
    g = _dwconv3(g, lp['ffn_conv'], lp['ffn_conv_b'])
    return (jax.nn.gelu(g, approximate=False) * u) @ lp['ffn_down']

def setup_inputs(seed: int = 0) -> dict:
    key = jax.random.key(seed)
    ks = iter(jax.random.split(key, 40))
    f32 = jnp.float32
    L, D = DEPTH, D_MODEL
    beta = (8.0 * DEPTH) ** -0.25

    def nrm(shape, scale):
        return scale * jax.random.normal(next(ks), shape, f32)

    def unif(shape, lo, hi):
        return jax.random.uniform(next(ks), shape, f32, lo, hi)

    return {
        'x': nrm((BATCH, SEQ, D), 1.0),
        'c': nrm((BATCH, D), 1.0),
        'ctx': nrm((BATCH, CTX_LEN, D), 1.0),
        'c_ctx': nrm((D,), 1.0),
        'ada_w': nrm((L, D, 6 * D), 0.5 * D ** -0.5),
        'ada_b': nrm((L, 6 * D), 0.01),
        'w_in': nrm((L, D, D_IN), D ** -0.5),
        'lam_qk': nrm((L, 4, DH_A), 0.1),
        'subln_g': 1.0 + nrm((L, DV_A), 0.02),
        'tshift_mu': unif((L, 2, D_CS + D_CO), 0.0, 0.5),
        'rw_w0': unif((L, 2, D_C), -5.0, 0.0),
        'rw_w2': nrm((L, 2, LORA_W, D_C), 0.5 * LORA_W ** -0.5),
        'rw_a0': nrm((L, 2, D_C), 0.5),
        'rw_a2': nrm((L, 2, LORA_A, D_C), 0.5 * LORA_A ** -0.5),
        'rw_g2': nrm((L, LORA_G, D_C), LORA_G ** -0.5),
        'rw_kk': 1.0 + nrm((L, D_C), 0.1),
        'rw_ka': 1.0 + nrm((L, D_C), 0.1),
        'rw_rk': nrm((L, HC, HS_C), 0.1),
        'rw_lnw': 1.0 + nrm((L, D_C), 0.02),
        'rw_lnb': nrm((L, D_C), 0.02),
        'w_pa': nrm((L, D_A, D), D_A ** -0.5),
        'w_pf': nrm((L, D_F, D), D_F ** -0.5),
        'w_pc': nrm((L, D_C, D), D_C ** -0.5),
        'w_o': nrm((L, D, D), beta * D ** -0.5),
        'ln1_g': 1.0 + nrm((L, D), 0.02),
        'ln1_b': nrm((L, D), 0.02),
        'ffn_up': nrm((L, D, 2 * D_FF), D ** -0.5),
        'ffn_conv': nrm((L, CONV_W, D_FF), CONV_W ** -0.5),
        'ffn_conv_b': nrm((L, D_FF), 0.02),
        'ffn_down': nrm((L, D_FF, D), beta * D_FF ** -0.5),
        'ln2_g': 1.0 + nrm((L, D), 0.02),
        'ln2_b': nrm((L, D), 0.02),
    }

def reference(x, c, ctx, c_ctx, ada_w, ada_b, w_in, lam_qk, subln_g, tshift_mu,
              rw_w0, rw_w2, rw_a0, rw_a2, rw_g2, rw_kk, rw_ka, rw_rk, rw_lnw, rw_lnb,
              w_pa, w_pf, w_pc, w_o, ln1_g, ln1_b, ffn_up, ffn_conv, ffn_conv_b, ffn_down,
              ln2_g, ln2_b):
    alpha = (2.0 * DEPTH) ** 0.25
    cos, sin = _rope_angles(x.shape[1])
    xc = ctx
    for i in range(DEPTH):
        last = i == DEPTH - 1
        lam_init = 0.8 - 0.6 * math.exp(-0.3 * i)
        lq = lam_qk[i].astype(jnp.float32)
        lam = jnp.exp(jnp.sum(lq[0] * lq[1])) - jnp.exp(jnp.sum(lq[2] * lq[3])) + lam_init
        lp = {'w_in': w_in[i], 'subln': subln_g[i], 'mu': tshift_mu[i],
              'w0': rw_w0[i], 'w2': rw_w2[i], 'a0': rw_a0[i], 'a2': rw_a2[i], 'g2': rw_g2[i],
              'k_k': rw_kk[i], 'k_a': rw_ka[i], 'r_k': rw_rk[i], 'ln_w': rw_lnw[i], 'ln_b': rw_lnb[i],
              'w_pa': w_pa[i], 'w_pf': w_pf[i], 'w_pc': w_pc[i], 'w_o': w_o[i],
              'ffn_up': ffn_up[i], 'ffn_conv': ffn_conv[i], 'ffn_conv_b': ffn_conv_b[i], 'ffn_down': ffn_down[i]}
        mod = [m[:, None, :] for m in jnp.split(jax.nn.silu(c) @ ada_w[i] + ada_b[i], 6, axis=-1)]
        mod_c = jnp.split(jax.nn.silu(c_ctx) @ ada_w[i] + ada_b[i], 6, axis=-1)
        cache, ctx_mix = _ctx_mixer(_modulate(xc, mod_c[0], mod_c[1]), lp, lam, lam_init, not last)
        lat_mix = _latent_mixer(_modulate(x, mod[0], mod[1]), lp, lam, lam_init, cache, cos, sin)
        x = _layernorm(alpha * x + mod[2] * lat_mix, ln1_g[i], ln1_b[i])
        x = _layernorm(alpha * x + mod[5] * _conv_ffn(_modulate(x, mod[3], mod[4]), lp), ln2_g[i], ln2_b[i])
        if not last:
            xc = _layernorm(alpha * xc + mod_c[2] * ctx_mix, ln1_g[i], ln1_b[i])
            xc = _layernorm(alpha * xc + mod_c[5] * _conv_ffn(_modulate(xc, mod_c[3], mod_c[4]), lp), ln2_g[i], ln2_b[i])
    return x


_drawn_inputs = setup_inputs


def setup_inputs(seed=0):
    import zlib

    import numpy as np

    out = dict(_drawn_inputs(seed))
    spreads = {}
    factors = {'ctx': 3.386,
     'ada_b': 8.0,
     'lam_qk': 8.0,
     'subln_g': 43.045,
     'rw_w2': 8.0,
     'rw_a0': 6.398,
     'rw_a2': 7.756,
     'rw_kk': 8.0,
     'rw_ka': 6.442,
     'rw_rk': 3.454,
     'rw_lnw': 64.0,
     'rw_lnb': 52.939,
     'ffn_conv_b': 21.412}
    for name, (base, spread) in spreads.items():
        noise = np.random.default_rng([zlib.crc32(name.encode()), seed]).standard_normal(out[name].shape)
        drawn = base * np.exp(spread * noise) if base else spread * noise
        out[name] = __import__('jax').numpy.asarray(drawn.astype(out[name].dtype))
    for name, factor in factors.items():
        out[name] = (out[name] * factor).astype(out[name].dtype)
    return out
```

```python
import math
from contextlib import ExitStack, contextmanager

import numpy as np
import concourse.bass as bass
from concourse import mybir

F32 = mybir.dt.float32
I32 = mybir.dt.int32
ALU = mybir.AluOpType
ACT = mybir.ActivationFunctionType
AX = mybir.AxisListType

P = 128
D_MODEL, SEQ, CTX_LEN, DEPTH, GRID_W = 1024, 512, 256, 2, 64
TOK = SEQ + CTX_LEN
KT = D_MODEL // P
LT, CT = SEQ // P, CTX_LEN // P
NT = LT + CT
HA, DH_A, DV = 8, 64, 128
F_GROUPS, F_GROUP_W = 4, 128
D_F = F_GROUPS * F_GROUP_W
HC, HS_C = 8, 64
D_C = HC * HS_C
CTILES = D_C // P
LORA_G = 128
D_CS = 2 * D_C + 4 * 64
D_CO = D_C + LORA_G
D_FF = 2816
FT = D_FF // P
LN_EPS, GN_EPS, HEAD_EPS = 1e-5, HS_C * 1e-5, 1e-5
ALPHA = (2.0 * DEPTH) ** 0.25
DECAY = math.exp(-0.5)
OFF_Q, OFF_K, OFF_V = 0, D_MODEL, 2 * D_MODEL
OFF_F = 3 * D_MODEL
OFF_C = OFF_F + D_F
OFF_G = OFF_C + D_CS + D_CO
C = 64
GCOL = CTILES * P

PA = dict(ada_b=0, mu0=48, mu1=63, w0=78, a0=86, kk=94, ka=98, rk=102, lnw=106, lnb=110, subln=114, end=115)
PB = dict(conv=0, conv_b=3 * FT, c=4 * FT, c_ctx=4 * FT + KT, end=4 * FT + 2 * KT)
LEVELS = (1, 2, 4, 8, 16, 32)
(M_ID, M_LO, M_UP, M_LOI, M_UPI, M_LO1, M_UP1) = range(7)


def tables():
    t = {}
    t["ident"] = np.eye(P, dtype=np.float32)
    blk = np.zeros((P, P), np.float32)
    blk[:64, :64] = blk[64:, 64:] = 1.0
    t["blkones"] = blk
    i = np.arange(C)
    row, col = np.meshgrid(i, i, indexing="ij")
    low = lambda b: (row // b == col // b + 1) & (row // b % 2 == 1)
    m = [row == col, row > col, row < col, row >= col, row <= col, low(1), low(1).T]
    t["masks"] = np.ascontiguousarray(np.concatenate([np.stack(m, 1)] * 2, 0).astype(np.float32))
    lv = [low(b) for b in LEVELS[1:]] + [low(b).T for b in LEVELS[1:]]
    t["lvmasks"] = np.ascontiguousarray(np.concatenate([np.stack(lv, 1)] * 2, 0).astype(np.int32))
    n_freq = DH_A // 4
    inv = (np.float32(10000.0) ** (-np.arange(n_freq, dtype=np.float32) / n_freq)).astype(np.float32)
    tok = np.arange(SEQ)
    pos = np.stack([tok // GRID_W, tok % GRID_W]).astype(np.float32)
    d = np.arange(P) % DH_A
    ang = pos[d // 32] * inv[d % 16][:, None]
    sign = np.where(d % 32 < 16, -1.0, 1.0)[:, None]
    t["rope"] = np.stack([np.cos(ang), np.sin(ang) * sign], 1).astype(np.float32)
    w = np.arange(F_GROUP_W)
    aw = 2 * np.pi * (np.outer(w, w) % F_GROUP_W) / F_GROUP_W
    t["dft_w"] = np.concatenate([np.cos(aw), np.sin(aw)], 1).astype(np.float32)
    for name, n in (("dft_lat", SEQ), ("dft_ctx", CTX_LEN)):
        k = np.arange(n)
        at = 2 * np.pi * (np.outer(k, k) % n) / n
        s = 1.0 / math.sqrt(n * F_GROUP_W)
        both = np.stack([np.cos(at) * s, -np.sin(at) * s])
        t[name] = np.ascontiguousarray(both.reshape(2, n // P, P, n).transpose(2, 0, 1, 3).astype(np.float32))
    return t


@contextmanager
def stage(nc, done=None):
    sems = {}

    def sem(name):
        if name not in sems:
            sems[name] = nc.alloc_semaphore(nc.get_next_instruction_name() + "_" + name)
        return sems[name]

    with nc.Block(no_gpsimd_drain=True) as block:
        yield block, sem
    if sems:
        nc.clear_and_free_semaphores(list(sems.values()))
        nc.all_engine_barrier(sem_only=True)


def bc(ap, n, axis=1):
    v = ap.unsqueeze(axis)
    shape = list(v.shape)
    shape[axis] = n
    return v.to_broadcast(shape)


def program(nc, A, out):
    with ExitStack() as top:
        def sb(scope, name, shape, dt=F32):
            return scope.enter_context(nc.sbuf_tensor(nc.get_next_instruction_name() + "_" + name, shape, dt))

        ps = top.enter_context(nc.psum_tensor("ps", [P, 4096], F32))
        bank = lambda b, n=512, o=0: ps[:, b * 512 + o:b * 512 + o + n]
        x_keep = nc.dram_tensor("x_keep", [P, NT, D_MODEL], F32).ap()

        x = sb(top, "x", [P, NT, D_MODEL])
        h = sb(top, "h", [P, KT, TOK])
        ident = sb(top, "ident", [P, P])
        ones = sb(top, "ones", [P, P])
        blkones = sb(top, "blkones", [P, P])
        pa = [sb(top, f"pa{l}", [P, PA["end"]]) for l in range(DEPTH)]
        pb = [sb(top, f"pb{l}", [P, PB["end"]]) for l in range(DEPTH)]
        mu_own = [sb(top, f"mu_own{l}", [P, 15]) for l in range(DEPTH)]
        nlam = [sb(top, f"nlam{l}", [P, 1]) for l in range(DEPTH)]
        subln = [sb(top, f"subln{l}", [P, 1]) for l in range(DEPTH)]
        mod = sb(top, "mod", [P, 48, 2])

        with ExitStack() as sc, stage(nc) as (block, sem):
            rows = [sb(sc, f"rows{i}", [P, P]) for i in range(2 * DEPTH)]
            lqk = sb(sc, "lqk", [P, DEPTH, 4, 64])
            lpr = sb(sc, "lpr", [P, DEPTH, 2, 64])
            ldot = sb(sc, "ldot", [P, DEPTH, 2])
            lexp = sb(sc, "lexp", [P, DEPTH, 2])
            row_src = []
            for l in range(DEPTH):
                ra, rb = rows[2 * l], rows[2 * l + 1]
                r = lambda ap: ap.rearrange("(t p) -> t p", p=P)
                r2 = lambda ap: ap.rearrange("a (t p) -> (a t) p", p=P)
                row_src += [
                    (ra, PA["ada_b"], 48, r(A["ada_b"][l])), (ra, PA["mu0"], 30, r2(A["tshift_mu"][l])),
                    (ra, PA["w0"], 8, r2(A["rw_w0"][l])), (ra, PA["a0"], 8, r2(A["rw_a0"][l])),
                    (ra, PA["kk"], 4, r(A["rw_kk"][l])), (ra, PA["ka"], 4, r(A["rw_ka"][l])),
                    (ra, PA["rk"], 4, A["rw_rk"][l].rearrange("(t a) k -> t (a k)", a=2)),
                    (ra, PA["lnw"], 4, r(A["rw_lnw"][l])), (ra, PA["lnb"], 4, r(A["rw_lnb"][l])),
                    (ra, PA["subln"], 1, r(A["subln_g"][l])),
                    (rb, PB["conv"], 3 * FT, r2(A["ffn_conv"][l])), (rb, PB["conv_b"], FT, r(A["ffn_conv_b"][l])),
                    (rb, PB["c"], KT, r2(A["c"])), (rb, PB["c_ctx"], KT, r(A["c_ctx"])),
                ]

            @block.sync
            def _(sp):
                for dst, at, n, src in row_src:
                    sp.dma_start(dst[at:at + n, :], src).then_inc(sem("rows_in"), 16)
                sp.dma_start(x[:, 0:LT, :], A["x"].rearrange("b (t p) d -> p (b t) d", p=P)).then_inc(sem("x_in"), 16)
                sp.dma_start(x[:, LT:NT, :], A["ctx"].rearrange("b (t p) d -> p (b t) d", p=P)).then_inc(sem("x_in"), 16)
                sp.wait_ge(sem("x_in"), 32)

            @block.scalar
            def _(act):
                act.dma_start(ident[:, :], A["ident"]).then_inc(sem("const_in"), 16)
                act.dma_start(blkones[:, :], A["blkones"]).then_inc(sem("const_in"), 16)
                act.dma_start(lqk[:, :, :, :], A["lam_qk"].partition_broadcast(P)).then_inc(sem("const_in"), 16)
                act.wait_ge(sem("dots"), 1)
                act.activation(lexp[:, :, :], ldot[:, :, :], ACT.Exp).then_inc(sem("lexp"), 1)

            @block.tensor
            def _(pe):
                pe.wait_ge(sem("rows_in"), 16 * len(row_src))
                pe.wait_ge(sem("const_in"), 48)
                for i, src in enumerate(rows):
                    n = (PA, PB)[i % 2]["end"]
                    pe.transpose(bank(i, n), src[0:n, :], ident[0:n, 0:n]).then_inc(sem("columns"), 1)

            @block.gpsimd
            def _(pool):
                pool.memset(ones[:, :], 1.0)

            @block.vector
            def _(dve):
                dve.wait_ge(sem("const_in"), 48)
                dve.tensor_tensor(lpr[:, :, :, :], lqk[:, :, 0:4:2, :], lqk[:, :, 1:4:2, :], ALU.mult).then_inc(sem("dve"), 1)
                dve.wait_ge(sem("dve"), 1)
                dve.reduce_sum(ldot[:, :, :], lpr[:, :, :, :], AX.X).then_inc(sem("dots"), 1)
                for i in range(2 * DEPTH):
                    dst, n = (pa, pb)[i % 2][i // 2], (PA, PB)[i % 2]["end"]
                    dve.wait_ge(sem("columns"), i + 1)
                    dve.tensor_copy(dst[:, :], bank(i, n)).then_inc(sem("dve"), 1)
                dve.wait_ge(sem("dve"), 1 + 2 * DEPTH)
                dve.wait_ge(sem("lexp"), 1)
                for l in range(DEPTH):
                    lam_init = 0.8 - 0.6 * math.exp(-0.3 * l)
                    a = pa[l]
                    dve.tensor_scalar(subln[l][:, :], a[:, PA["subln"]:PA["subln"] + 1], 1.0 - lam_init, None, ALU.mult)
                    dve.tensor_tensor(nlam[l][:, :], lexp[:, l, 1:2], lexp[:, l, 0:1], ALU.subtract).then_inc(sem("half"), 1)
                    dve.tensor_tensor(mu_own[l][:, :], a[:, PA["mu0"]:PA["mu0"] + 15], a[:, PA["mu1"]:PA["mu1"] + 15],
                                      ALU.add).then_inc(sem("half"), 1)
                    dve.wait_ge(sem("half"), 2 * l + 2)
                    dve.tensor_scalar(nlam[l][:, :], nlam[l][:, :], -lam_init, None, ALU.add)
                    dve.tensor_scalar(mu_own[l][:, :], mu_own[l][:, :], -1.0, 1.0, ALU.mult, ALU.add)

        def modulation(l):
            with ExitStack() as sc, stage(nc) as (block, sem):
                w = sb(sc, "ada_w", [P, 3, KT, 512])
                sg = sb(sc, "sig_c", [P, 2, KT])
                cc = sb(sc, "silu_c", [P, KT, 2])
                raw = pb[l][:, PB["c"]:PB["end"]].rearrange("p (s k) -> p s k", s=2)
                src = A["ada_w"][l].rearrange("(k p) n -> p k n", p=P)

                @block.sync
                def _(sp):
                    for n in range(12):
                        if n >= 3:
                            sp.wait_ge(sem("w_used"), n - 2)
                        sp.dma_start(w[:, n % 3, :, :], src[:, :, n * 512:(n + 1) * 512]).then_inc(sem(f"w_in{n % 3}"), 16)

                @block.scalar
                def _(act):
                    act.activation(sg[:, :, :], raw, ACT.Sigmoid).then_inc(sem("sig"), 1)

                @block.vector
                def _(dve):
                    dve.wait_ge(sem("sig"), 1)
                    dve.tensor_tensor(cc[:, :, :].rearrange("p k s -> p s k"), raw, sg[:, :, :], ALU.mult).then_inc(sem("silu"), 1)
                    dve.wait_ge(sem("w_used"), 12)
                    b = pa[l][:, PA["ada_b"]:PA["ada_b"] + 48]
                    dve.tensor_tensor(mod[:, :, :], bank(0, 96).rearrange("p (n s) -> p n s", s=2),
                                      bc(b, 2, 2), ALU.add).then_inc(sem("mod"), 1)
                    dve.wait_ge(sem("mod"), 1)
                    for i in (1, 4):
                        dve.tensor_scalar(mod[:, 8 * i:8 * i + 8, :], mod[:, 8 * i:8 * i + 8, :], 1.0, None, ALU.add)

                @block.tensor
                def _(pe):
                    pe.wait_ge(sem("silu"), 1)
                    for n in range(12):
                        pe.wait_ge(sem(f"w_in{n % 3}"), 16 * (n // 3 + 1))
                        for j in range(4):
                            for k in range(KT):
                                m = pe.matmul(bank(0, 2, 8 * n + 2 * j), w[:, n % 3, k, j * P:(j + 1) * P], cc[:, k, :],
                                              start=k == 0, stop=k == KT - 1)
                        m.then_inc(sem("w_used"), 1)

        def norm(l, i_shift, i_scale, nt):
            lat, ctx = LT, nt - LT
            with ExitStack() as sc, stage(nc) as (block, sem):
                xn = sb(sc, "xn", [P, NT, D_MODEL])
                st = sb(sc, "stats", [P, NT, 2, 6])
                mv = sb(sc, "mean_var", [P, NT, 2])
                rs = sb(sc, "rstd", [P, NT])
                sh = lambda j, s: mod[:, 8 * i_shift + j, s:s + 1]
                sl = lambda j, s: mod[:, 8 * i_scale + j, s:s + 1]

                @block.vector
                def _(dve):
                    for t in range(nt):
                        for f in range(2):
                            i = dve.bn_stats(st[:, t, f, :], x[:, t, f * 512:(f + 1) * 512])
                        i.then_inc(sem("stats"), 1)
                    for t in range(nt):
                        dve.wait_ge(sem("stats"), t + 1)
                        i = dve.bn_aggr(mv[:, t, :], st[:, t, :, :])
                    i.then_inc(sem("mv"), 1)
                    dve.wait_ge(sem("mv"), 1)
                    dve.tensor_scalar(rs[:, 0:nt], mv[:, 0:nt, 1], LN_EPS, None, ALU.add).then_inc(sem("var"), 1)
                    dve.wait_ge(sem("std"), 1)
                    dve.reciprocal(rs[:, 0:nt], rs[:, 0:nt]).then_inc(sem("rstd"), 1)
                    dve.wait_ge(sem("rstd"), 1)
                    for t in range(nt):
                        dve.tensor_scalar(xn[:, t, :], x[:, t, :], mv[:, t, 0:1], rs[:, t:t + 1],
                                          ALU.subtract, ALU.mult).then_inc(sem("xn"), 1)
                    if ctx:
                        for j in range(KT):
                            dve.wait_ge(sem("ctx_T"), j + 1)
                            dve.tensor_scalar(h[:, j, SEQ:TOK], bank(4 + j % 4, 256), sl(j, 1), sh(j, 1),
                                              ALU.mult, ALU.add).then_inc(sem("ctx_h"), 1)

                @block.tensor
                def _(pe):
                    pe.wait_ge(sem("xn"), nt)
                    for j in range(KT):
                        if j >= 4:
                            pe.wait_ge(sem("lat_h"), j - 3)
                        for t in range(lat):
                            m = pe.transpose(bank(j % 4, P, t * P), xn[:, t, j * P:(j + 1) * P], ident[:, :])
                        m.then_inc(sem("lat_T"), 1)
                        if ctx:
                            if j >= 4:
                                pe.wait_ge(sem("ctx_h"), j - 3)
                            for t in range(ctx):
                                m = pe.transpose(bank(4 + j % 4, P, t * P), xn[:, LT + t, j * P:(j + 1) * P], ident[:, :])
                            m.then_inc(sem("ctx_T"), 1)

                @block.scalar
                def _(act):
                    act.wait_ge(sem("var"), 1)
                    act.activation(rs[:, 0:nt], rs[:, 0:nt], ACT.Sqrt).then_inc(sem("std"), 1)
                    for j in range(KT):
                        act.wait_ge(sem("lat_T"), j + 1)
                        act.activation(h[:, j, 0:SEQ], bank(j % 4), ACT.Identity, bias=sh(j, 0), scale=sl(j, 0)).then_inc(sem("lat_h"), 1)

        def column_tiles(sp, sem, ring, n_slots, sources):
            for n, src in enumerate(sources):
                if n >= n_slots:
                    sp.wait_ge(sem("w_used"), n - n_slots + 1)
                sp.dma_start(ring[:, n % n_slots, 0:src.shape[1], :], src).then_inc(sem(f"w_in{n % n_slots}"), 16)

        def fm_product(pe, dst, w, act_fm, kt, widths):
            for k in range(kt):
                for at, n in widths:
                    m = pe.matmul(dst[:, at:at + n], w[:, k, :], act_fm[:, k, at:at + n], start=k == 0, stop=k == kt - 1)
            return m

        BOTH = ((0, SEQ), (SEQ, CTX_LEN))
        LAT = ((0, SEQ),)

        def rwkv(l, oc, last):
            S8 = 6
            with ExitStack() as sc:
                raw = sb(sc, "raw", [P, 15, TOK])
                kk = sb(sc, "kk", [P, CTILES, TOK])
                rkd = sb(sc, "rkd", [P, CTILES, TOK])
                kf, vf, wd, ad, rf, gd = raw[:, 0:4], raw[:, 4:8], raw[:, 8], raw[:, 9], raw[:, 10:14], raw[:, 14]

                with ExitStack() as s2, stage(nc) as (block, sem):
                    ring = sb(s2, "w_ring", [P, S8, KT, P])
                    sq = sb(s2, "sq", [P, TOK])
                    nrm = sb(s2, "nrm", [P, 2, TOK])
                    src = A["w_in"][l].rearrange("(k p) n -> p k n", p=P)
                    p_of = lambda t: ps[:, (t % 4) * 1024:(t % 4) * 1024 + TOK]
                    seqs = lambda t: LAT if (last and t >= 10) else BOTH
                    col = lambda name, t: pa[l][:, PA[name] + t:PA[name] + t + 1]

                    @block.sync
                    def _(sp):
                        column_tiles(sp, sem, ring, S8, [src[:, :, OFF_C + t * P:OFF_C + (t + 1) * P] for t in range(15)])

                    @block.tensor
                    def _(pe):
                        for t in range(15):
                            pe.wait_ge(sem(f"w_in{t % S8}"), 16 * (t // S8 + 1))
                            if t >= 4:
                                pe.wait_ge(sem("shifted"), t - 3)
                            fm_product(pe, p_of(t), ring[:, t % S8], h, KT, seqs(t)).then_inc(sem("w_used"), 1)
                        for t in range(CTILES):
                            pe.wait_ge(sem("kk_sq"), t + 1)
                            if t == 0:
                                pe.wait_ge(sem("shifted"), 15)
                            elif t >= 2:
                                pe.wait_ge(sem("norm"), t - 1)
                            for at, n in BOTH:
                                m = pe.matmul(p_of(t % 2)[:, at:at + n], blkones[:, :], sq[:, at:at + n], start=True, stop=True)
                            m.then_inc(sem("kk_ss"), 1)

                    @block.scalar
                    def _(act):
                        for t in range(15):
                            act.wait_ge(sem("w_used"), t + 1)
                            n = sum(w for _, w in seqs(t))
                            act.activation(raw[:, t, 0:n], p_of(t)[:, 0:n], ACT.Copy, scale=mu_own[l][:, t:t + 1]).then_inc(sem("own"), 1)
                        act.wait_ge(sem("shifted"), 15)
                        act.activation(wd, wd, ACT.Tanh)
                        act.activation(gd[:, 0:n], gd[:, 0:n], ACT.Sigmoid)
                        for t in range(CTILES):
                            act.wait_ge(sem("kk_raw"), t + 1)
                            if t:
                                act.wait_ge(sem("kk_ss"), t)
                            act.activation(sq[:, :], kk[:, t, :], ACT.Square).then_inc(sem("kk_sq"), 1)
                            act.wait_ge(sem("kk_ss"), t + 1)
                            if t >= 2:
                                act.wait_ge(sem("kk_done"), t - 1)
                            act.activation(nrm[:, t % 2, :], p_of(t % 2), ACT.Sqrt).then_inc(sem("norm"), 1)

                    @block.gpsimd
                    def _(pool):
                        pool.memset(rkd[:, :, :], 0.0)
                        pool.memset(oc[:, :, :], 0.0)

                    @block.vector
                    def _(dve):
                        for t in range(15):
                            dve.wait_ge(sem("own"), t + 1)
                            for i, (at, n) in enumerate(seqs(t)):
                                o, p = raw[:, t, at:at + n], p_of(t)[:, at:at + n]
                                dve.scalar_tensor_tensor(o[:, 1:n], p[:, 0:n - 1], pa[l][:, PA["mu0"] + t:PA["mu0"] + t + 1],
                                                         o[:, 1:n], ALU.mult, ALU.add).then_inc(sem(f"prev{i}"), 1)
                            for i, (at, n) in enumerate(seqs(t)):
                                o, p = raw[:, t, at:at + n], p_of(t)[:, at:at + n]
                                dve.wait_ge(sem(f"prev{i}"), t + 1)
                                m = dve.scalar_tensor_tensor(o[:, 0:n - 1], p[:, 1:n], pa[l][:, PA["mu1"] + t:PA["mu1"] + t + 1],
                                                             o[:, 0:n - 1], ALU.mult, ALU.add)
                            m.then_inc(sem("shifted"), 1)
                        dve.wait_ge(sem("shifted"), 15)
                        for t in range(CTILES):
                            dve.tensor_scalar(kk[:, t, :], kf[:, t, :], col("kk", t), None, ALU.mult).then_inc(sem("kk_raw"), 1)
                        for t in range(CTILES):
                            n = nrm[:, t % 2, :]
                            dve.wait_ge(sem("norm"), t + 1)
                            dve.tensor_scalar(n, n, 1e-12, None, ALU.max).then_inc(sem("kk_n"), 1)
                            dve.wait_ge(sem("kk_n"), 2 * t + 1)
                            dve.reciprocal(n, n).then_inc(sem("kk_n"), 1)
                            dve.wait_ge(sem("kk_n"), 2 * t + 2)
                            dve.tensor_tensor(kk[:, t, :], kk[:, t, :], n, ALU.mult).then_inc(sem("kk_done"), 1)

                with ExitStack() as s2:
                    rwkv_scan(l, s2, oc, rkd, kf, vf, wd, ad, rf, kk, last)

                rwkv_output(l, oc, rkd, vf, gd, last)

        def rwkv_scan(l, s2, oc, rkd, kf, vf, wd, ad, rf, kk, last):
            G = [P, GCOL]
            two = lambda name: [sb(s2, f"{name}{d}", G) for d in range(2)]
            masks = sb(s2, "masks", [P, 7, C])
            lvm = sb(s2, "lvmasks", [P, 10, C], I32)
            reset = sb(s2, "reset", [P, 2, GCOL])
            w2 = sb(s2, "w2", [P, 2, D_C])
            a2 = sb(s2, "a2", [P, 2, D_C])
            S = [sb(s2, f"S{i}", G) for i in range(3)]
            PC = sb(s2, "PC", [P, 2, 2, CTILES])
            Rt, W1T, Btm, Ktm, Vtm, QB, QK = (two(n) for n in ("Rt", "W1T", "Btm", "Ktm", "Vtm", "QB", "QK"))
            spare = x[:, :, :].rearrange("p t d -> p (t d)")
            Kttm, NAT, T, TT, Y, MT = ([spare[:, (2 * i + d) * GCOL:(2 * i + d + 1) * GCOL] for d in range(2)] for i in range(6))
            MV, U, W2s = Y, T, NAT
            sg, L, Lx, Lr, EN, a, kd, Bh, Bp, vg = (sb(s2, n, G) for n in ("sg", "L", "Lx", "Lr", "EN", "a", "kd", "Bh", "Bp", "vg"))
            g3 = lambda ap: ap.rearrange("p (t c) -> p t c", t=CTILES)
            g8 = lambda ap: ap.rearrange("p (g c) -> p g c", c=C)
            cols = lambda name, d: pa[l][:, PA[name] + 4 * d:PA[name] + 4 * d + 4]

            with stage(nc) as (block, sem):
                @block.sync
                def _(sp):
                    sp.dma_start(masks[:, :, :], A["masks"]).then_inc(sem("in"), 16)
                    sp.dma_start(lvm[:, :, :], A["lvmasks"]).then_inc(sem("in"), 16)
                    sp.wait_ge(sem("zero"), 1)
                    for d in range(2):
                        sp.dma_start(w2[64 * d:64 * d + 64, d, :], A["rw_w2"][l, d]).then_inc(sem("in"), 16)
                        sp.dma_start(a2[64 * d:64 * d + 64, d, :], A["rw_a2"][l, d]).then_inc(sem("in"), 16)
                    sp.wait_ge(sem("in"), 96)

                @block.gpsimd
                def _(pool):
                    pool.memset(w2[:, :, :], 0.0)
                    pool.memset(a2[:, :, :], 0.0).then_inc(sem("zero"), 1)
                    pool.memset(S[0][:, :], 0.0)

                @block.vector
                def _(dve):
                    dve.memset(reset[:, :, :], 1.0).then_inc(sem("one"), 1)
                    dve.wait_ge(sem("one"), 1)
                    dve.memset(g8(reset[:, 0, :])[:, :, 0:1], 0.0)
                    dve.memset(g8(reset[:, 1, :])[:, :, C - 1:C], 0.0)

            def groups(base, n, want_y):
                n_fm, n_pr = (6, 5) if want_y else (5, 3)
                with nc.Fori(0, n) as g, stage(nc) as (block, sem):
                    at = (base + g * P, base + (n - 1) * P - g * P)
                    sl = lambda ap, d: ap[:, :, bass.ds(at[d], P)]
                    chunk_of = lambda d, q: q if d == 0 else 1 - q
                    HT = [(hh, t) for t in range(CTILES) for hh in range(2)]
                    hc = lambda hh, t: (hh * CTILES + t) * C
                    tc = lambda t, i: t * P + i * C
                    rows = lambda i: slice(64 * i, 64 * i + 64)

                    @block.tensor
                    def _(pe):
                        for d in range(2):
                            if d:
                                pe.wait_ge(sem("sig"), d)
                                pe.wait_ge(sem("prod"), n_pr * d)
                            for b, w, lora in ((0, w2, wd), (1, a2, ad)):
                                for t in range(CTILES):
                                    m = pe.matmul(bank(b, P, t * P), w[:, d, t * P:(t + 1) * P], lora[:, bass.ds(at[d], P)],
                                                  start=True, stop=True)
                            m.then_inc(sem("z"), 1)
                            pe.wait_ge(sem("fm"), n_fm * (d + 1))

                            def product(b, o, stat, mov):
                                for t in range(CTILES):
                                    for i in range(2):
                                        for hh in range(2):
                                            m = pe.matmul(ps[rows(i), (b + hh) * 512 + o + t * C:(b + hh) * 512 + o + (t + 1) * C],
                                                          stat[rows(hh), tc(t, i):tc(t, i) + C], mov[rows(hh), tc(t, i):tc(t, i) + C],
                                                          start=True, stop=True)
                                m.then_inc(sem("pmm"), 1)
                            product(6, 0, Bh, Lx)
                            product(6, 256, Lx, Bh)
                            pe.wait_ge(sem("sig"), d + 1)
                            product(0, 0, EN, Lx)
                            if d:
                                pe.wait_ge(sem("tm"), 4 * d)
                            if want_y:
                                product(0, 256, Bh, Rt[d])
                                product(2, 0, EN, Rt[d])
                            pe.wait_ge(sem("vg"), d + 1)
                            pe.wait_ge(sem("prod"), n_pr * (d + 1))
                            for b, src in ((2, Lx), (3, Bp), (4, Lr), (5, vg)):
                                for t in range(CTILES):
                                    m = pe.transpose(bank(b, P, t * P), src[:, t * P:(t + 1) * P], ident[:, :])
                                m.then_inc(sem("tmm"), 1)
                        def diag(b, stat, mov, name):
                            for hh, t in HT:
                                for i in range(2):
                                    c0 = hc(hh, t)
                                    m = pe.matmul(ps[rows(i), b * 512 + c0:b * 512 + c0 + C], stat[rows(i), c0:c0 + C],
                                                  mov[rows(i), c0:c0 + C], start=True, stop=True)
                            m.then_inc(sem(name), 1)
                        pe.wait_ge(sem("tm"), 8)
                        for n_lv in range(5):
                            for d in range(2):
                                pe.wait_ge(sem(f"T{d}"), n_lv + 1)
                                diag(4 + d, NAT[d], T[d], f"Ymm{d}")
                            for d in range(2):
                                pe.wait_ge(sem(f"Y{d}"), n_lv + 1)
                                if n_lv < 4:
                                    diag(6 + d, TT[d], Y[d], f"off{d}")
                                diag(2 + d, Y[d], TT[d], f"offT{d}")
                        for d in range(2):
                            for hh, t in HT:
                                for i in range(2):
                                    m = pe.matmul(ps[rows(i), (6 + d) * 512 + hc(hh, t):(6 + d) * 512 + hc(hh, t) + C],
                                                  MT[d][rows(i), hc(hh, t):hc(hh, t) + C],
                                                  Vtm[d][rows(i), tc(t, hh):tc(t, hh) + C], start=True, stop=True)
                            m.then_inc(sem("MVmm"), 1)
                        for d in range(2):
                            pe.wait_ge(sem(f"T{d}"), 6)
                            if d:
                                pe.wait_ge(sem("W1"), d)
                            for t in range(CTILES):
                                for i in range(2):
                                    for hh in range(2):
                                        m = pe.matmul(ps[rows(hh), i * 512 + t * C:i * 512 + (t + 1) * C],
                                                      Kttm[d][rows(i), tc(t, hh):tc(t, hh) + C],
                                                      TT[d][rows(i), hc(hh, t):hc(hh, t) + C], start=True, stop=True)
                            m.then_inc(sem("W1mm"), 1)
                        for d in range(2):
                            pe.wait_ge(sem("MV"), d + 1)
                            diag(4 + d, TT[d], MV[d], "W2mm")
                        for q in range(2):
                            if q == 0:
                                pe.wait_ge(sem("W1"), 2)
                                pe.wait_ge(sem("W2"), 4)
                            else:
                                pe.wait_ge(sem("S"), 1)
                            for t in range(CTILES):
                                for d in range(2):
                                    i = chunk_of(d, q)
                                    for hh in range(2):
                                        m = pe.matmul(ps[rows(i), (2 + hh) * 512 + t * C:(2 + hh) * 512 + (t + 1) * C],
                                                      W1T[d][rows(hh), tc(t, i):tc(t, i) + C],
                                                      S[q][rows(hh), (d * CTILES + t) * C:(d * CTILES + t + 1) * C], start=True, stop=True)
                            m.then_inc(sem("Umm"), 1)
                            pe.wait_ge(sem("U"), q + 1)
                            for t in range(CTILES):
                                for d in range(2):
                                    i = chunk_of(d, q)
                                    for hh in range(2):
                                        o = ps[rows(hh), (6 + d) * 512 + t * C:(6 + d) * 512 + (t + 1) * C]
                                        pe.matmul(o, Btm[d][rows(i), tc(t, hh):tc(t, hh) + C],
                                                  U[q][rows(i), hc(hh, t):hc(hh, t) + C], start=True, stop=False)
                                        m = pe.matmul(o, Ktm[d][rows(i), tc(t, hh):tc(t, hh) + C],
                                                      Vtm[d][rows(i), tc(t, hh):tc(t, hh) + C], start=False, stop=True)
                            m.then_inc(sem("Smm"), 1)
                        if want_y:
                            for d in range(2):
                                for t in range(CTILES):
                                    for i in range(2):
                                        q = chunk_of(d, i)
                                        for hh in range(2):
                                            m = pe.matmul(ps[rows(hh), (4 + d) * 512 + tc(t, i):(4 + d) * 512 + tc(t, i) + C],
                                                          S[q][rows(hh), (d * CTILES + t) * C:(d * CTILES + t + 1) * C],
                                                          Rt[d][rows(hh), tc(t, i):tc(t, i) + C], start=True, stop=True)
                                m.then_inc(sem("YRmm"), 1)
                                for t in range(CTILES):
                                    for i in range(2):
                                        q = chunk_of(d, i)
                                        for hh in range(2):
                                            o = ps[rows(hh), (2 * d + i) * 512 + t * C:(2 * d + i) * 512 + (t + 1) * C]
                                            c0 = hc(hh, t)
                                            pe.matmul(o, U[q][rows(i), c0:c0 + C], QB[d][rows(i), c0:c0 + C], start=True, stop=False)
                                            m = pe.matmul(o, Vtm[d][rows(i), tc(t, hh):tc(t, hh) + C],
                                                          QK[d][rows(i), c0:c0 + C], start=False, stop=True)
                                m.then_inc(sem("YUmm"), 1)

                    @block.scalar
                    def _(act):
                        for d in range(2):
                            act.wait_ge(sem("z"), d + 1)
                            if d:
                                act.wait_ge(sem("fm"), n_fm * d)
                            for b, name, dst in ((0, "w0", sg), (1, "a0", a)):
                                for t in range(CTILES):
                                    m = act.activation(dst[:, t * P:(t + 1) * P], bank(b, P, t * P), ACT.Sigmoid,
                                                       bias=cols(name, d)[:, t:t + 1])
                            m.then_inc(sem("sig"), 1)
                            act.wait_ge(sem("sums"), 3 * d + 3)
                            act.activation(Lx[:, :], Lx[:, :], ACT.Exp, scale=-DECAY).then_inc(sem("exp"), 1)
                            act.activation(EN[:, :], L[:, :], ACT.Exp, scale=DECAY).then_inc(sem("exp"), 1)
                            last_t = C - 1 if d == 0 else 0
                            for q in range(2):
                                i = chunk_of(d, q)
                                act.activation(PC[:, q, d, :], g3(L[:, :])[:, :, i * C + last_t], ACT.Exp, scale=-DECAY)
                            act.activation(Lr[:, :], Lr[:, :], ACT.Exp, scale=-DECAY).then_inc(sem("exp"), 1)
                            act.wait_ge(sem("exp"), 4 * d + 3)
                            act.activation(L[:, :], L[:, :], ACT.Exp, scale=-DECAY).then_inc(sem("exp"), 1)
                            for n_tm, (b, dst) in enumerate(((2, Kttm), (3, Btm), (4, Ktm), (5, Vtm))):
                                act.wait_ge(sem("tmm"), 4 * d + n_tm + 1)
                                act.activation(dst[d][:, :], bank(b), ACT.Copy).then_inc(sem("tm"), 1)
                        for n_lv in range(5):
                            for d in range(2):
                                act.wait_ge(sem(f"Ymm{d}"), n_lv + 1)
                                if n_lv:
                                    act.wait_ge(sem(f"offT{d}"), n_lv)
                                elif want_y:
                                    act.wait_ge(sem("rk"), 2 * d + 2)
                                act.activation(Y[d][:, :], bank(4 + d), ACT.Copy).then_inc(sem(f"Y{d}"), 1)
                        for d in range(2):
                            act.wait_ge(sem("MVmm"), d + 1)
                            act.activation(MV[d][:, :], bank(6 + d), ACT.Copy).then_inc(sem("MV"), 1)
                        for d in range(2):
                            act.wait_ge(sem("W2mm"), d + 1)
                            for q in range(2):
                                r = rows(chunk_of(d, q))
                                act.activation(W2s[q][r, :], ps[r, (4 + d) * 512:(5 + d) * 512], ACT.Copy).then_inc(sem("W2"), 1)
                        if want_y:
                            for d in range(2):
                                act.wait_ge(sem("YRmm"), d + 1)
                                act.activation((sg, a)[d][:, :], bank(4 + d), ACT.Copy).then_inc(sem("YR"), 1)

                    @block.gpsimd
                    def _(pool):
                        for d in range(2):
                            if d:
                                pool.wait_ge(sem("tmm"), 4 * d)
                            pool.tensor_copy(g3(vg[:, :]), sl(vf, d)).then_inc(sem("vg"), 1)
                            if want_y:
                                pool.wait_ge(sem("kd"), 2 * d + 2)
                                pool.tensor_tensor(g3(Y[d][:, :]), sl(rf, d), g3(kd[:, :]), ALU.mult).then_inc(sem("rk"), 1)
                                pool.wait_ge(sem("rk"), 2 * d + 1)
                                pool.tensor_tensor(sl(rkd, d), sl(rkd, d), g3(Y[d][:, :]), ALU.add).then_inc(sem("rk"), 1)
                        for q in range(2):
                            if q:
                                pool.wait_ge(sem("S"), q)
                            else:
                                pool.wait_ge(sem("exp"), 8)
                            pool.tensor_tensor(S[q + 1][:, :].rearrange("p (g v) -> p g v", v=C),
                                               S[q][:, :].rearrange("p (g v) -> p g v", v=C),
                                               bc(PC[:, q].rearrange("p d t -> p (d t)"), C, 2), ALU.mult).then_inc(sem("SP"), 1)
                        if want_y:
                            for d in range(2):
                                pool.wait_ge(sem("Ysum"), d + 1)
                                pool.tensor_tensor(sl(oc, d), sl(oc, d), g3((sg, a)[d][:, :]), ALU.add).then_inc(sem("yacc"), 1)
                                pool.wait_ge(sem("yacc"), d + 1)
                        pool.wait_ge(sem("S"), 2)
                        if want_y:
                            pool.wait_ge(sem("YRmm"), 2)
                        else:
                            pool.wait_ge(sem("Smm"), 2)
                        pool.tensor_copy(S[0][:, :], S[2][:, :])

                    @block.vector
                    def _(dve):
                        for d in range(2):
                            rev = slice(None, None, -1) if d else slice(None)
                            tl = 0 if d else C - 1
                            dve.wait_ge(sem("sig"), d + 1)
                            if d:
                                dve.wait_ge(sem("pmm"), n_pr * d)
                                dve.wait_ge(sem("tmm"), 4 * d)
                            dve.tensor_tensor_scan(L[:, rev], reset[:, d, rev], sg[:, rev], 0.0, ALU.mult, ALU.add).then_inc(sem("sums"), 1)
                            dve.wait_ge(sem("sums"), 3 * d + 1)
                            dve.tensor_tensor(Lx[:, :], L[:, :], sg[:, :], ALU.subtract).then_inc(sem("sums"), 1)
                            dve.tensor_tensor(g8(Lr[:, :]), g8(L[:, :])[:, :, tl:tl + 1].to_broadcast([P, 8, C]), g8(L[:, :]),
                                              ALU.subtract).then_inc(sem("sums"), 1)
                            if d and want_y:
                                dve.wait_ge(sem("rk"), 2 * d - 1)
                            dve.scalar_tensor_tensor(g3(kd[:, :]), g3(a[:, :]), -1.0, bc(pa[l][:, PA["ka"]:PA["ka"] + 4], P, 2),
                                                     ALU.add, ALU.mult).then_inc(sem("kd"), 1)
                            dve.wait_ge(sem("kd"), 2 * d + 1)
                            dve.scalar_tensor_tensor(g3(kd[:, :]), g3(kd[:, :]), 1.0, sl(kf, d), ALU.add, ALU.mult).then_inc(sem("kd"), 1)
                            dve.scalar_tensor_tensor(g3(a[:, :]), sl(kk, d), -1.0, g3(a[:, :]), ALU.mult, ALU.mult).then_inc(sem("b"), 1)
                            dve.wait_ge(sem("exp"), 4 * d + 1)
                            dve.tensor_tensor(g3(Lx[:, :]), sl(kk, d), g3(Lx[:, :]), ALU.mult).then_inc(sem("fm"), 1)
                            dve.wait_ge(sem("exp"), 4 * d + 2)
                            dve.wait_ge(sem("b"), d + 1)
                            dve.tensor_tensor(Bh[:, :], a[:, :], EN[:, :], ALU.mult).then_inc(sem("fm"), 1)
                            dve.wait_ge(sem("kd"), 2 * d + 2)
                            dve.tensor_tensor(EN[:, :], kd[:, :], EN[:, :], ALU.mult).then_inc(sem("fm"), 1)
                            dve.wait_ge(sem("exp"), 4 * d + 3)
                            dve.tensor_tensor(Bp[:, :], a[:, :], Lr[:, :], ALU.mult).then_inc(sem("fm"), 1)
                            dve.tensor_tensor(Lr[:, :], kd[:, :], Lr[:, :], ALU.mult).then_inc(sem("fm"), 1)
                            if want_y:
                                dve.wait_ge(sem("exp"), 4 * d + 4)
                                dve.tensor_tensor(g3(Rt[d][:, :]), sl(rf, d), g3(L[:, :]), ALU.mult).then_inc(sem("fm"), 1)
                            pv = lambda b, o: ps[:, b * 512:(b + 2) * 512].rearrange("p (h c) -> p h c", h=2)[:, :, o:o + 256]\
                                .rearrange("p h (t c) -> p h t c", t=CTILES)
                            o4 = lambda ap: ap.rearrange("p (h t c) -> p h t c", h=2, t=CTILES)
                            mk = lambda m: masks[:, m, :].unsqueeze(1).unsqueeze(1).to_broadcast([P, 2, CTILES, C])
                            strict, incl = ((M_UP, M_UPI), (M_LO, M_LOI))[d]
                            lo1, up1 = ((M_LO1, M_UP1), (M_UP1, M_LO1))[d]
                            dve.wait_ge(sem("pmm"), n_pr * d + 2)
                            dve.tensor_tensor(o4(NAT[d][:, :]), pv(6, 0), mk(strict), ALU.mult).then_inc(sem("prod"), 1)
                            dve.tensor_tensor(o4(T[d][:, :]), pv(6, 256), mk(lo1), ALU.mult).then_inc(sem("prod"), 1)
                            dve.wait_ge(sem("pmm"), n_pr * d + min(n_pr, 4))
                            dve.tensor_tensor(o4(MT[d][:, :]), pv(0, 0), mk(strict), ALU.mult).then_inc(sem("prod"), 1)
                            if want_y:
                                dve.tensor_tensor(o4(QB[d][:, :]), pv(0, 256), mk(incl), ALU.mult).then_inc(sem("prod"), 1)
                                dve.wait_ge(sem("pmm"), n_pr * d + 5)
                                dve.tensor_tensor(o4(QK[d][:, :]), pv(2, 0), mk(incl), ALU.mult).then_inc(sem("prod"), 1)
                            m8 = lambda m: masks[:, m, :].unsqueeze(1).to_broadcast([P, 8, C])
                            dve.wait_ge(sem("prod"), n_pr * d + 2)
                            dve.tensor_tensor(g8(T[d][:, :]), g8(T[d][:, :]), m8(M_ID), ALU.add)
                            dve.tensor_tensor(g8(TT[d][:, :]), g8(NAT[d][:, :]), m8(up1), ALU.mult).then_inc(sem("TT1"), 1)
                            dve.wait_ge(sem("TT1"), d + 1)
                            dve.tensor_tensor(g8(TT[d][:, :]), g8(TT[d][:, :]), m8(M_ID), ALU.add).then_inc(sem(f"T{d}"), 1)
                        for n_lv in range(5):
                            for d in range(2):
                                lo, up = (n_lv, 5 + n_lv) if d == 0 else (5 + n_lv, n_lv)
                                lm = lambda m: lvm[:, m, :].unsqueeze(1).to_broadcast([P, 8, C])
                                if n_lv < 4:
                                    dve.wait_ge(sem(f"off{d}"), n_lv + 1)
                                    dve.copy_predicated(g8(T[d][:, :]), lm(lo), g8(bank(6 + d)))
                                dve.wait_ge(sem(f"offT{d}"), n_lv + 1)
                                dve.copy_predicated(g8(TT[d][:, :]), lm(up), g8(bank(2 + d))).then_inc(sem(f"T{d}"), 1)
                        for d in range(2):
                            dve.wait_ge(sem("W1mm"), d + 1)
                            dve.tensor_copy(W1T[d][:, :].rearrange("p (t i c) -> p i t c", t=CTILES, i=2),
                                            ps[:, 0:1024].rearrange("p (i c) -> p i c", i=2)[:, :, 0:256]
                                            .rearrange("p i (t c) -> p i t c", t=CTILES)).then_inc(sem("W1"), 1)
                        half = lambda b: ps[:, b * 512:(b + 2) * 512].rearrange("p (b c) -> p b c", b=2)[:, :, 0:256]
                        for q in range(2):
                            dve.wait_ge(sem("Umm"), q + 1)
                            if q == 0:
                                dve.wait_ge(sem("W2"), 4)
                            dve.tensor_tensor(U[q][:, :].rearrange("p (b c) -> p b c", b=2), half(2),
                                              W2s[q][:, :].rearrange("p (b c) -> p b c", b=2), ALU.add).then_inc(sem("U"), 1)
                            dve.wait_ge(sem("Smm"), q + 1)
                            dve.wait_ge(sem("SP"), q + 1)
                            s_n = S[q + 1][:, :].rearrange("p (b c) -> p b c", b=2)
                            dve.tensor_tensor(s_n, s_n, half(6), ALU.add).then_inc(sem("S"), 1)
                        if want_y:
                            for d in range(2):
                                dve.wait_ge(sem("YUmm"), d + 1)
                                dve.wait_ge(sem("YR"), d + 1)
                                y = (sg, a)[d][:, :].rearrange("p (t i c) -> p t i c", t=CTILES, i=2)
                                dve.tensor_tensor(y, y, half(2 * d).rearrange("p i (t c) -> p t i c", t=CTILES), ALU.add).then_inc(sem("Ysum"), 1)

            groups(SEQ, CTX_LEN // P, not last)
            groups(0, SEQ // P, True)

        def rwkv_output(l, oc, rkd, vf, gd, last):
            seqs = LAT if last else BOTH
            n_tok = SEQ if last else TOK
            with ExitStack() as sc, stage(nc) as (block, sem):
                g2 = sb(sc, "g2", [P, D_C])
                yc = sb(sc, "yc", [P, 2, TOK])
                sq = sb(sc, "ysq", [P, 2, TOK])
                pr = lambda i: ps[:, i * 1024:i * 1024 + n_tok]
                col = lambda name, t: pa[l][:, PA[name] + t:PA[name] + t + 1]

                @block.sync
                def _(sp):
                    sp.dma_start(g2[:, :], A["rw_g2"][l]).then_inc(sem("g2"), 16)

                @block.gpsimd
                def _(pool):
                    for t in range(CTILES):
                        pool.tensor_scalar(rkd[:, t, 0:n_tok], rkd[:, t, 0:n_tok], col("rk", t), None, ALU.mult).then_inc(sem("rk"), 1)

                @block.tensor
                def _(pe):
                    pe.wait_ge(sem("g2"), 16)
                    for t in range(CTILES):
                        def by(dst, stat, mov, name):
                            for at, n in seqs:
                                m = pe.matmul(dst[:, at:at + n], stat, mov[:, at:at + n], start=True, stop=True)
                            m.then_inc(sem(name), 1)
                        if t:
                            pe.wait_ge(sem("done"), t)
                        by(pr(0), blkones[:, :], oc[:, t, :], "mean")
                        by(pr(1), g2[:, t * P:(t + 1) * P], gd, "gate")
                        pe.wait_ge(sem("rk"), t + 1)
                        by(pr(2), blkones[:, :], rkd[:, t, :], "bonus")
                        pe.wait_ge(sem("sq"), t + 1)
                        by(pr(3), blkones[:, :], sq[:, t % 2, :], "var")

                @block.scalar
                def _(act):
                    for t in range(CTILES):
                        act.wait_ge(sem("yc"), t + 1)
                        act.activation(sq[:, t % 2, 0:n_tok], yc[:, t % 2, 0:n_tok], ACT.Square).then_inc(sem("sq"), 1)
                        act.wait_ge(sem("v"), t + 1)
                        act.activation(sq[:, t % 2, 0:n_tok], sq[:, t % 2, 0:n_tok], ACT.Sqrt).then_inc(sem("std"), 1)
                        act.wait_ge(sem("yn"), t + 1)
                        act.activation(yc[:, t % 2, 0:n_tok], yc[:, t % 2, 0:n_tok], ACT.Identity, bias=col("lnb", t),
                                       scale=col("lnw", t)).then_inc(sem("yl"), 1)

                @block.vector
                def _(dve):
                    steps = [0]

                    def link(ins):
                        steps[0] += 1
                        ins.then_inc(sem("dve"), 1)
                        dve.wait_ge(sem("dve"), steps[0])
                    for t in range(CTILES):
                        c, s, y = yc[:, t % 2, 0:n_tok], sq[:, t % 2, 0:n_tok], oc[:, t, 0:n_tok]
                        dve.wait_ge(sem("mean"), t + 1)
                        dve.scalar_tensor_tensor(c, pr(0), -1.0 / HS_C, y, ALU.mult, ALU.add).then_inc(sem("yc"), 1)
                        dve.wait_ge(sem("bonus"), t + 1)
                        dve.wait_ge(sem("yc"), t + 1)
                        link(dve.tensor_tensor(y, pr(2), vf[:, t, 0:n_tok], ALU.mult))
                        dve.wait_ge(sem("var"), t + 1)
                        dve.tensor_scalar(s, pr(3), 1.0 / HS_C, GN_EPS, ALU.mult, ALU.add).then_inc(sem("v"), 1)
                        dve.wait_ge(sem("std"), t + 1)
                        link(dve.reciprocal(s, s))
                        dve.tensor_tensor(c, c, s, ALU.mult).then_inc(sem("yn"), 1)
                        dve.wait_ge(sem("yl"), t + 1)
                        link(dve.tensor_tensor(y, y, c, ALU.add))
                        dve.wait_ge(sem("gate"), t + 1)
                        dve.tensor_tensor(y, y, pr(1), ALU.mult).then_inc(sem("done"), 1)

        def attention(l, oa, last):
            nq = LT if last else NT
            q_seqs = LAT if last else BOTH
            q_tok = SEQ if last else TOK
            SL = 6
            with ExitStack() as sc, stage(nc) as (block, sem):
                ring = sb(sc, "w_ring", [P, SL, KT, P])
                rope = sb(sc, "rope", [P, 2, SEQ])
                qp = sb(sc, "q_plain", [P, 2, TOK])
                kp = sb(sc, "k_plain", [P, 2, TOK])
                qr = sb(sc, "q_rot", [P, 2, SEQ])
                kr = sb(sc, "k_rot", [P, 2, SEQ])
                vt = sb(sc, "v_tm", [P, 2, NT, P])
                shuf = sb(sc, "shuf", [P, 2, SEQ])
                rcos = sb(sc, "rcos", [P, 2, SEQ])
                E = sb(sc, "E", [P, 2, 2, TOK])
                mx = sb(sc, "mx", [P, 2, 2])
                sm = sb(sc, "sm", [P, 2, 2])
                at = sb(sc, "a_T", [P, 2, TOK])
                swap = list(range(16, 32)) + list(range(16))
                src = A["w_in"][l].rearrange("(k p) n -> p k n", p=P)
                proj = lambda n: ps[:, 2048:2048 + n]
                s_view = lambda n: ps[:, 0:2048].rearrange("p (c n) -> p c n", c=2)[:, :, 0:n]
                n_keys = lambda u: TOK if u < LT else CTX_LEN
                k_tiles = lambda u: range(NT) if u < LT else range(LT, NT)

                @block.sync
                def _(sp):
                    sp.dma_start(rope[:, :, :], A["rope"]).then_inc(sem("rope"), 16)
                    column_tiles(sp, sem, ring, SL, [src[:, :, o + j * P:o + (j + 1) * P] for j in range(HA)
                                                     for o in (OFF_Q, OFF_K, OFF_V)])

                @block.tensor
                def _(pe):
                    def project(j, i):
                        n = 3 * j + i
                        w = ring[:, n % SL]
                        pe.wait_ge(sem(f"w_in{n % SL}"), 16 * (n // SL + 1))
                        if n:
                            pe.wait_ge(sem("proj_read"), n)
                        if i < 2:
                            m = fm_product(pe, proj(TOK), w, h, KT, q_seqs if i == 0 else BOTH)
                        else:
                            for t in range(NT):
                                for k in range(KT):
                                    m = pe.matmul(proj(TOK)[:, t * P:(t + 1) * P], h[:, k, t * P:(t + 1) * P], w[:, k, :],
                                                  start=k == 0, stop=k == KT - 1)
                        m.then_inc(sem("w_used"), 1)

                    def scores(j, u):
                        n = j * nq + u
                        if u == 0:
                            pe.wait_ge(sem("rot"), 2 * j + 2)
                            pe.wait_ge(sem("proj_read"), 3 * j + 3)
                        if n:
                            pe.wait_ge(sem("exp"), 2 * n)
                        qs = slice(u * P, (u + 1) * P)
                        for c in range(2):
                            r = slice(c * DH_A, (c + 1) * DH_A)
                            o = 0
                            if u < LT:
                                pe.matmul(ps[:, c * 1024:c * 1024 + SEQ], qr[r, j % 2, qs], kr[r, j % 2, :], start=True, stop=True)
                                o = SEQ
                            m = pe.matmul(ps[:, c * 1024 + o:c * 1024 + o + CTX_LEN], qp[r, j % 2, qs], kp[r, j % 2, SEQ:TOK],
                                          start=True, stop=True)
                        m.then_inc(sem("scores"), 1)

                    def values(j, u):
                        n = j * nq + u
                        pe.wait_ge(sem("a"), n + 1)
                        if n:
                            pe.wait_ge(sem("o_read"), n)
                        kts = list(k_tiles(u))
                        for i, kt in enumerate(kts):
                            m = pe.transpose(ps[:, 3072 + i * P:3072 + (i + 1) * P], E[:, n % 2, 1, i * P:(i + 1) * P], ident[:, :])
                        m.then_inc(sem("aT_mm"), 1)
                        pe.wait_ge(sem("aT"), n + 1)
                        for i, kt in enumerate(kts):
                            m = pe.matmul(bank(7, P, 384), vt[:, j % 2, kt, :], at[:, n % 2, i * P:(i + 1) * P],
                                          start=i == 0, stop=i == len(kts) - 1)
                        m.then_inc(sem("o"), 1)

                    pe.wait_ge(sem("rope"), 16)
                    for i in range(3):
                        project(0, i)
                    scores(0, 0)
                    for j in range(HA):
                        for u in range(nq):
                            if u < 3 and j + 1 < HA:
                                project(j + 1, u)
                            if u + 1 < nq:
                                scores(j, u + 1)
                            elif j + 1 < HA:
                                scores(j + 1, 0)
                            values(j, u)

                def order():
                    for i in range(3):
                        yield "proj", 0, i
                    yield "soft", 0, 0
                    for j in range(HA):
                        for u in range(nq):
                            if u < 3 and j + 1 < HA:
                                yield "proj", j + 1, u
                            yield "aT", j, u
                            if u + 1 < nq:
                                yield "soft", j, u + 1
                            elif j + 1 < HA:
                                yield "soft", j + 1, 0

                @block.scalar
                def _(act):
                    for what, j, u in order():
                        if what == "proj":
                            n = 3 * j + u
                            act.wait_ge(sem("w_used"), n + 1)
                            if j >= 2:
                                act.wait_ge(sem("o"), (j - 1) * nq)
                                act.wait_ge(sem("rot"), 2 * (j - 1))
                            if u == 2:
                                act.activation(vt[:, j % 2, :, :].rearrange("p t d -> p (t d)"), proj(TOK), ACT.Copy).then_inc(sem("proj_read"), 1)
                            else:
                                w = q_tok if u == 0 else TOK
                                act.activation((qp, kp)[u][:, j % 2, 0:w], proj(w), ACT.Copy).then_inc(sem("proj_read"), 1)
                        elif what == "soft":
                            n = j * nq + u
                            w = n_keys(u)
                            act.wait_ge(sem("max"), n + 1)
                            if n >= 2:
                                act.wait_ge(sem("aT_mm"), n - 1)
                            for c in range(2):
                                act.activation(E[:, n % 2, c, 0:w], ps[:, c * 1024:c * 1024 + w], ACT.Exp, bias=mx[:, n % 2, c:c + 1],
                                               scale=DH_A ** -0.5, accum_out=sm[:, n % 2, c:c + 1]).then_inc(sem("exp"), 1)
                        else:
                            n = j * nq + u
                            w = n_keys(u)
                            act.wait_ge(sem("aT_mm"), n + 1)
                            if n >= 2:
                                act.wait_ge(sem("o"), n - 1)
                            act.activation(at[:, n % 2, 0:w], ps[:, 3072:3072 + w], ACT.Copy).then_inc(sem("aT"), 1)
                            act.wait_ge(sem("o"), n + 1)
                            act.activation(oa[:, j, u * P:(u + 1) * P], bank(7, P, 384), ACT.Copy).then_inc(sem("o_read"), 1)

                @block.gpsimd
                def _(pool):
                    pool.wait_ge(sem("rope"), 16)
                    for j in range(HA):
                        for i in range(2):
                            pool.wait_ge(sem("proj_read"), 3 * j + i + 1)
                            if 2 * j + i >= 2:
                                pool.wait_ge(sem("rot"), 2 * j + i - 1)
                            pool.tensor_tensor(rcos[:, i, :], (qp, kp)[i][:, j % 2, 0:SEQ], rope[:, 0, :], ALU.mult).then_inc(sem("rcos"), 1)

                @block.vector
                def _(dve):
                    dve.wait_ge(sem("rope"), 16)
                    for what, j, u in order():
                        if what == "proj" and u < 2:
                            n = 2 * j + u
                            dve.wait_ge(sem("proj_read"), 3 * j + u + 1)
                            dve.stream_shuffle(shuf[:, u, :], (qp, kp)[u][:, j % 2, 0:SEQ], swap).then_inc(sem("shuf"), 1)
                            dve.wait_ge(sem("shuf"), 2 * n + 1)
                            dve.tensor_tensor(shuf[:, u, :], shuf[:, u, :], rope[:, 1, :], ALU.mult).then_inc(sem("shuf"), 1)
                            dve.wait_ge(sem("shuf"), 2 * n + 2)
                            dve.wait_ge(sem("rcos"), n + 1)
                            if j >= 2:
                                dve.wait_ge(sem("scores"), (j - 1) * nq)
                            dve.tensor_tensor((qr, kr)[u][:, j % 2, :], shuf[:, u, :], rcos[:, u, :], ALU.add).then_inc(sem("rot"), 1)
                        elif what == "soft":
                            n = j * nq + u
                            w = n_keys(u)
                            dve.wait_ge(sem("scores"), n + 1)
                            if n >= 2:
                                dve.wait_ge(sem("exp"), 2 * n - 2)
                            m = mx[:, n % 2, :]
                            dve.tensor_reduce(m, s_view(w), AX.X, ALU.max).then_inc(sem("mraw"), 1)
                            dve.wait_ge(sem("mraw"), n + 1)
                            dve.tensor_scalar(m, m, -DH_A ** -0.5, None, ALU.mult).then_inc(sem("max"), 1)
                            s = sm[:, n % 2, :]
                            dve.wait_ge(sem("exp"), 2 * n + 2)
                            dve.reciprocal(s, s).then_inc(sem("rec"), 1)
                            dve.wait_ge(sem("rec"), n + 1)
                            dve.tensor_scalar(E[:, n % 2, 0, 0:w], E[:, n % 2, 0, 0:w], s[:, 0:1], None, ALU.mult).then_inc(sem("p0"), 1)
                            dve.tensor_tensor(s[:, 1:2], s[:, 1:2], nlam[l][:, :], ALU.mult).then_inc(sem("p0"), 1)
                            dve.wait_ge(sem("p0"), 2 * n + 2)
                            dve.scalar_tensor_tensor(E[:, n % 2, 1, 0:w], E[:, n % 2, 1, 0:w], s[:, 1:2], E[:, n % 2, 0, 0:w],
                                                     ALU.mult, ALU.add).then_inc(sem("a"), 1)

            with ExitStack() as sc, stage(nc) as (block, sem):
                sq = sb(sc, "osq", [P, 2, TOK])
                rr = sb(sc, "orr", [P, 2, TOK])
                p_of = lambda j: ps[:, (j % 2) * 1024:(j % 2) * 1024 + q_tok]

                @block.scalar
                def _(act):
                    for j in range(HA):
                        if j >= 2:
                            act.wait_ge(sem("ss"), j - 1)
                        act.activation(sq[:, j % 2, 0:q_tok], oa[:, j, 0:q_tok], ACT.Square).then_inc(sem("sq"), 1)
                        if j:
                            act.wait_ge(sem("ms"), j)
                            act.activation(rr[:, (j - 1) % 2, 0:q_tok], rr[:, (j - 1) % 2, 0:q_tok], ACT.Sqrt).then_inc(sem("std"), 1)
                    act.wait_ge(sem("ms"), HA)
                    act.activation(rr[:, (HA - 1) % 2, 0:q_tok], rr[:, (HA - 1) % 2, 0:q_tok], ACT.Sqrt).then_inc(sem("std"), 1)

                @block.tensor
                def _(pe):
                    for j in range(HA):
                        pe.wait_ge(sem("sq"), j + 1)
                        if j >= 2:
                            pe.wait_ge(sem("ms"), j - 1)
                        for at_, n in q_seqs:
                            m = pe.matmul(p_of(j)[:, at_:at_ + n], ones[:, :], sq[:, j % 2, at_:at_ + n], start=True, stop=True)
                        m.then_inc(sem("ss"), 1)

                @block.vector
                def _(dve):
                    def mean(j):
                        dve.wait_ge(sem("ss"), j + 1)
                        dve.tensor_scalar(rr[:, j % 2, 0:q_tok], p_of(j), 1.0 / DV, HEAD_EPS, ALU.mult, ALU.add).then_inc(sem("ms"), 1)
                    mean(0)
                    for j in range(HA):
                        if j + 1 < HA:
                            mean(j + 1)
                        r = rr[:, j % 2, 0:q_tok]
                        dve.wait_ge(sem("std"), j + 1)
                        dve.reciprocal(r, r).then_inc(sem("rec"), 1)
                        dve.wait_ge(sem("rec"), j + 1)
                        dve.scalar_tensor_tensor(oa[:, j, 0:q_tok], oa[:, j, 0:q_tok], subln[l][:, :], r, ALU.mult, ALU.mult).then_inc(sem("oa"), 1)
                        dve.wait_ge(sem("oa"), j + 1)

        def fourier(l, of, last):
            seqs = LAT if last else BOTH
            n_tok = SEQ if last else TOK
            nt = n_tok // P
            with ExitStack() as sc, stage(nc) as (block, sem):
                ring = sb(sc, "w_ring", [P, F_GROUPS, KT, P])
                dw = sb(sc, "dft_w", [P, 2 * P])
                dl = sb(sc, "dft_lat", [P, 2, LT, SEQ])
                dc = sb(sc, "dft_ctx", [P, 2, CT, CTX_LEN])
                f = sb(sc, "f", [P, 2, TOK])
                z = sb(sc, "z", [P, 2, NT, 2 * P])
                src = A["w_in"][l].rearrange("(k p) n -> p k n", p=P)

                @block.sync
                def _(sp):
                    column_tiles(sp, sem, ring, F_GROUPS, [src[:, :, OFF_F + j * P:OFF_F + (j + 1) * P] for j in range(F_GROUPS)])
                    sp.dma_start(dw[:, :], A["dft_w"]).then_inc(sem("dft"), 16)
                    sp.dma_start(dl[:, :, :, :], A["dft_lat"]).then_inc(sem("dft"), 16)
                    sp.dma_start(dc[:, :, :, :], A["dft_ctx"]).then_inc(sem("dft"), 16)

                @block.tensor
                def _(pe):
                    def project(j):
                        pe.wait_ge(sem(f"w_in{j}"), 16)
                        if j:
                            pe.wait_ge(sem("f"), j)
                        fm_product(pe, ps[:, 0:TOK], ring[:, j], h, KT, seqs).then_inc(sem("w_used"), 1)
                    project(0)
                    pe.wait_ge(sem("dft"), 48)
                    for j in range(F_GROUPS):
                        pe.wait_ge(sem("f"), j + 1)
                        for t in range(nt):
                            if j and t % 2 == 0:
                                pe.wait_ge(sem("z"), 3 * (j - 1) + t // 2 + 1 if nt == 6 else 2 * (j - 1) + t // 2 + 1)
                            m = pe.matmul(ps[:, 1024 + t * 256:1280 + t * 256], f[:, j % 2, t * P:(t + 1) * P], dw[:, :],
                                          start=True, stop=True)
                            if t % 2:
                                m.then_inc(sem("zmm"), 1)
                        if j + 1 < F_GROUPS:
                            project(j + 1)
                        pe.wait_ge(sem("z"), (nt // 2) * (j + 1))
                        if j:
                            pe.wait_ge(sem("of"), j)
                        for i in range(2 * LT):
                            m = pe.matmul(bank(6), z[:, j % 2, i % LT, (i // LT) * P:(i // LT + 1) * P], dl[:, i // LT, i % LT, :],
                                          start=i == 0, stop=i == 2 * LT - 1)
                        if not last:
                            for i in range(2 * CT):
                                m = pe.matmul(bank(7, 256), z[:, j % 2, LT + i % CT, (i // CT) * P:(i // CT + 1) * P], dc[:, i // CT, i % CT, :],
                                              start=i == 0, stop=i == 2 * CT - 1)
                        m.then_inc(sem("ofmm"), 1)

                @block.vector
                def _(dve):
                    for j in range(F_GROUPS):
                        for i in range(nt // 2):
                            dve.wait_ge(sem("zmm"), j * (nt // 2) + i + 1)
                            if j >= 2:
                                dve.wait_ge(sem("ofmm"), j - 1)
                            dve.tensor_copy(z[:, j % 2, 2 * i:2 * i + 2, :].rearrange("p a b -> p (a b)"), bank(2 + i)).then_inc(sem("z"), 1)

                @block.scalar
                def _(act):
                    for j in range(F_GROUPS + 1):
                        if j < F_GROUPS:
                            act.wait_ge(sem("w_used"), j + 1)
                            if j >= 2:
                                act.wait_ge(sem("zmm"), (nt // 2) * (j - 1))
                            act.activation(f[:, j % 2, 0:n_tok], ps[:, 0:n_tok], ACT.Copy).then_inc(sem("f"), 1)
                        if j:
                            act.wait_ge(sem("ofmm"), j)
                            act.activation(of[:, j - 1, 0:n_tok], ps[:, 3072:3072 + n_tok], ACT.Copy).then_inc(sem("of"), 1)

        def merge(l, oa, of, oc, y, last):
            seqs = LAT if last else BOTH
            n_tok = SEQ if last else TOK
            SL = 8
            with ExitStack() as sc, stage(nc) as (block, sem):
                ring = sb(sc, "w_ring", [P, SL, KT, P])
                sgm = sb(sc, "gate", [P, 2, TOK])
                pr = sb(sc, "gated", [P, 2, TOK])
                kp_ = lambda ap: ap.rearrange("(k p) n -> p k n", p=P)
                win = kp_(A["w_in"][l])
                branches = [(0, kp_(A["w_pa"][l]), oa, HA), (1, kp_(A["w_pf"][l]), of, F_GROUPS), (2, kp_(A["w_pc"][l]), oc, CTILES)]
                order = [(j, b) for j in range(KT) for b in branches]
                p_of = lambda n, i: ps[:, (2 * (n % 2) + i) * 1024:(2 * (n % 2) + i) * 1024 + n_tok]

                @block.sync
                def _(sp):
                    srcs = []
                    for j, (b, w, _, _) in order:
                        srcs += [win[:, :, OFF_G + b * D_MODEL + j * P:OFF_G + b * D_MODEL + (j + 1) * P], w[:, :, j * P:(j + 1) * P]]
                    column_tiles(sp, sem, ring, SL, srcs)

                @block.tensor
                def _(pe):
                    for n, (j, (b, _, o, kt)) in enumerate(order):
                        for i, (act_fm, k) in enumerate(((h, KT), (o, kt))):
                            s = 2 * n + i
                            pe.wait_ge(sem(f"w_in{s % SL}"), 16 * (s // SL + 1))
                            if n >= 2:
                                pe.wait_ge(sem("gated"), n - 1)
                            fm_product(pe, p_of(n, i), ring[:, s % SL], act_fm, k, seqs).then_inc(sem("w_used"), 1)

                @block.scalar
                def _(act):
                    for n in range(len(order)):
                        act.wait_ge(sem("w_used"), 2 * n + 1)
                        if n >= 2:
                            act.wait_ge(sem("gated"), n - 1)
                        act.activation(sgm[:, n % 2, 0:n_tok], p_of(n, 0), ACT.Sigmoid).then_inc(sem("gate"), 1)

                @block.vector
                def _(dve):
                    for n, (j, (b, _, _, _)) in enumerate(order):
                        dve.wait_ge(sem("gate"), n + 1)
                        dve.wait_ge(sem("w_used"), 2 * n + 2)
                        if b == 0:
                            dst = y[:, j, 0:n_tok]
                        else:
                            dst = pr[:, b - 1, 0:n_tok]
                            if j:
                                dve.wait_ge(sem("sum"), 2 * (j - 1) + b)
                        dve.tensor_tensor(dst, sgm[:, n % 2, 0:n_tok], p_of(n, 1), ALU.mult).then_inc(sem("gated"), 1)

                @block.gpsimd
                def _(pool):
                    for n, (j, (b, _, _, _)) in enumerate(order):
                        if b:
                            pool.wait_ge(sem("gated"), n + 1)
                            if b == 2:
                                pool.wait_ge(sem("sum"), 2 * j + 1)
                            pool.tensor_tensor(y[:, j, 0:n_tok], y[:, j, 0:n_tok], pr[:, b - 1, 0:n_tok], ALU.add).then_inc(sem("sum"), 1)

        def gate_rows(sc, i_mod, streams):
            g = sb(sc, "gate_row", [P, 2, D_MODEL])
            with ExitStack() as s2, stage(nc) as (block, sem):
                diag = sb(s2, "diag", [P, 2 * KT, P])

                @block.vector
                def _(dve):
                    for s in range(streams):
                        for j in range(KT):
                            m = dve.tensor_scalar(diag[:, s * KT + j, :], ident[:, :], mod[:, 8 * i_mod + j, s:s + 1], None, ALU.mult)
                        m.then_inc(sem("diag"), 1)

                @block.tensor
                def _(pe):
                    for s in range(streams):
                        pe.wait_ge(sem("diag"), s + 1)
                        for j in range(0, KT, 4):
                            m = pe.matmul(bank(2 * s + j // 4), ones[:, :], diag[:, s * KT + j:s * KT + j + 4, :].rearrange("p a b -> p (a b)"),
                                          start=True, stop=True)
                        m.then_inc(sem("row"), 1)

                @block.scalar
                def _(act):
                    for s in range(streams):
                        act.wait_ge(sem("row"), s + 1)
                        act.activation(g[:, s, :], ps[:, s * 1024:(s + 1) * 1024], ACT.Copy)
            return g

        def post_norm(dve, act_sem, sem, nt, first, st, mv, rs):
            pass

        def residual(l, i_mod, g_name, b_name, nt, emit, n_halves_first, store):
            pass

        def out_proj(l, y, last):
            nt = LT if last else NT
            with ExitStack() as sc:
                gate = gate_rows(sc, 2, 1 if last else 2)
                with stage(nc) as (block, sem):
                    w = sb(sc, "w_o", [P, KT, D_MODEL])
                    lg = sb(sc, "ln_g", [P, D_MODEL])
                    lb = sb(sc, "ln_b", [P, D_MODEL])
                    tmp = sb(sc, "tmp", [P, 2, D_MODEL])

                    @block.sync
                    def _(sp):
                        sp.dma_start(w[:, :, :], A["w_o"][l].rearrange("(k p) n -> p k n", p=P)).then_inc(sem("w"), 16)
                        sp.dma_start(x[:, :, :], x_keep).then_inc(sem("x_back"), 16)
                        sp.dma_start(lg[:, :], A["ln1_g"][l].partition_broadcast(P)).then_inc(sem("ln"), 16)
                        sp.dma_start(lb[:, :], A["ln1_b"][l].partition_broadcast(P)).then_inc(sem("ln"), 16)

                    @block.tensor
                    def _(pe):
                        pe.wait_ge(sem("w"), 16)
                        for t in range(nt):
                            if t >= 4:
                                pe.wait_ge(sem("z1"), t - 3)
                            for n in range(2):
                                for k in range(KT):
                                    m = pe.matmul(bank(2 * (t % 4) + n), y[:, k, t * P:(t + 1) * P], w[:, k, n * 512:(n + 1) * 512],
                                                  start=k == 0, stop=k == KT - 1)
                            m.then_inc(sem("mm"), 1)

                    norm_tail(block, sem, sc, nt, lambda t: ps[:, (t % 4) * 1024:(t % 4) * 1024 + 1024], gate, tmp, lg, lb, "x_back")

        def norm_tail(block, sem, sc, nt, p_of, gate, tmp, lg, lb, wait_x):
            st = sb(sc, "stats", [P, NT, 2, 6])
            mv = sb(sc, "mean_var", [P, NT, 2])
            rs = sb(sc, "rstd", [P, NT])

            @block.vector
            def _(dve):
                if wait_x:
                    dve.wait_ge(sem(wait_x), 16)
                dve.wait_ge(sem("ln"), 32)

                def first(t):
                    dve.wait_ge(sem("mm"), t + 1)
                    if t >= 2:
                        dve.wait_ge(sem("z2"), t - 1)
                    dve.tensor_tensor(tmp[:, t % 2, :], p_of(t), gate[:, t // LT, :], ALU.mult).then_inc(sem("z1"), 1)
                    dve.wait_ge(sem("z1"), t + 1)
                    dve.scalar_tensor_tensor(x[:, t, :], x[:, t, :], ALPHA, tmp[:, t % 2, :], ALU.mult, ALU.add).then_inc(sem("z2"), 1)
                    dve.wait_ge(sem("z2"), t + 1)
                    for f in range(2):
                        i = dve.bn_stats(st[:, t, f, :], x[:, t, f * 512:(f + 1) * 512])
                    i.then_inc(sem("st"), 1)
                    dve.wait_ge(sem("st"), t + 1)
                    dve.bn_aggr(mv[:, t, :], st[:, t, :, :]).then_inc(sem("mv"), 1)
                    dve.wait_ge(sem("mv"), t + 1)
                    dve.tensor_scalar(rs[:, t:t + 1], mv[:, t, 1:2], LN_EPS, None, ALU.add).then_inc(sem("var"), 1)

                def second(t):
                    dve.wait_ge(sem("std"), t + 1)
                    dve.reciprocal(rs[:, t:t + 1], rs[:, t:t + 1]).then_inc(sem("rstd"), 1)
                    dve.wait_ge(sem("rstd"), t + 1)
                    dve.tensor_scalar(x[:, t, :], x[:, t, :], mv[:, t, 0:1], rs[:, t:t + 1], ALU.subtract, ALU.mult).then_inc(sem("xn"), 1)
                    dve.wait_ge(sem("xn"), t + 1)
                    dve.tensor_tensor(x[:, t, :], x[:, t, :], lg[:, :], ALU.mult).then_inc(sem("xg"), 1)

                first(0)
                for t in range(nt):
                    if t + 1 < nt:
                        first(t + 1)
                    second(t)

            @block.gpsimd
            def _(pool):
                for t in range(nt):
                    pool.wait_ge(sem("xg"), t + 1)
                    pool.tensor_tensor(x[:, t, :], x[:, t, :], lb[:, :], ALU.add)

            @block.scalar
            def _(act):
                for t in range(nt):
                    act.wait_ge(sem("var"), t + 1)
                    act.activation(rs[:, t:t + 1], rs[:, t:t + 1], ACT.Sqrt).then_inc(sem("std"), 1)

        def ffn(l, last):
            seqs = LAT if last else BOTH
            n_tok = SEQ if last else TOK
            nt = n_tok // P
            with ExitStack() as sc:
                hf = sb(sc, "hf", [P, FT, n_tok])
                with ExitStack() as s2, stage(nc) as (block, sem):
                    SL = 4
                    ring = sb(s2, "w_ring", [P, SL, KT, P])
                    cv = sb(s2, "conv", [P, 2, TOK])
                    src = A["ffn_up"][l].rearrange("(k p) n -> p k n", p=P)
                    p_of = lambda s: ps[:, (s % 4) * 1024:(s % 4) * 1024 + n_tok]
                    tap = lambda i, j: pb[l][:, PB["conv"] + i * FT + j:PB["conv"] + i * FT + j + 1]

                    @block.sync
                    def _(sp):
                        column_tiles(sp, sem, ring, SL, [src[:, :, o + j * P:o + (j + 1) * P] for j in range(FT) for o in (D_FF, 0)])

                    @block.tensor
                    def _(pe):
                        for s in range(2 * FT):
                            pe.wait_ge(sem(f"w_in{s % SL}"), 16 * (s // SL + 1))
                            if s >= 4:
                                pe.wait_ge(sem("hf"), s // 2 - 1)
                            fm_product(pe, p_of(s), ring[:, s % SL], h, KT, seqs).then_inc(sem("w_used"), 1)

                    @block.scalar
                    def _(act):
                        def own(j):
                            act.wait_ge(sem("w_used"), 2 * j + 1)
                            if j >= 2:
                                act.wait_ge(sem("hf"), j - 1)
                            act.activation(cv[:, j % 2, 0:n_tok], p_of(2 * j), ACT.Copy, scale=tap(1, j)).then_inc(sem("own"), 1)
                        own(0)
                        for j in range(FT):
                            if j + 1 < FT:
                                own(j + 1)
                            act.wait_ge(sem("conv"), j + 1)
                            act.activation(cv[:, j % 2, 0:n_tok], cv[:, j % 2, 0:n_tok], ACT.Gelu,
                                           bias=pb[l][:, PB["conv_b"] + j:PB["conv_b"] + j + 1]).then_inc(sem("gelu"), 1)

                    @block.vector
                    def _(dve):
                        def conv(j):
                            dve.wait_ge(sem("own"), j + 1)
                            for i, (at, n) in enumerate(seqs):
                                o, p = cv[:, j % 2, at:at + n], p_of(2 * j)[:, at:at + n]
                                dve.scalar_tensor_tensor(o[:, 1:n], p[:, 0:n - 1], tap(0, j), o[:, 1:n], ALU.mult, ALU.add).then_inc(sem(f"prev{i}"), 1)
                            for i, (at, n) in enumerate(seqs):
                                o, p = cv[:, j % 2, at:at + n], p_of(2 * j)[:, at:at + n]
                                dve.wait_ge(sem(f"prev{i}"), j + 1)
                                m = dve.scalar_tensor_tensor(o[:, 0:n - 1], p[:, 1:n], tap(2, j), o[:, 0:n - 1], ALU.mult, ALU.add)
                            m.then_inc(sem("conv"), 1)
                        conv(0)
                        for j in range(FT):
                            dve.wait_ge(sem("gelu"), j + 1)
                            dve.wait_ge(sem("w_used"), 2 * j + 2)
                            dve.tensor_tensor(hf[:, j, :], cv[:, j % 2, 0:n_tok], p_of(2 * j + 1), ALU.mult).then_inc(sem("hf"), 1)
                            if j + 1 < FT:
                                conv(j + 1)

                gate = gate_rows(sc, 5, 1 if last else 2)
                with stage(nc) as (block, sem):
                    KG, SL = 2, 8
                    ring = sb(sc, "w_down", [P, SL, KG, 512])
                    lg = sb(sc, "ln_g", [P, D_MODEL])
                    lb = sb(sc, "ln_b", [P, D_MODEL])
                    part = sb(sc, "part", [P, 2, 512])
                    src = A["ffn_down"][l].rearrange("(g k p) n -> g p k n", p=P, k=KG)
                    NG = FT // KG
                    st = sb(sc, "stats", [P, NT, 2, 6])
                    mv = sb(sc, "mean_var", [P, NT, 2])
                    rs = sb(sc, "rstd", [P, NT])

                    @block.sync
                    def _(sp):
                        sp.dma_start(lg[:, :], A["ln2_g"][l].partition_broadcast(P)).then_inc(sem("ln"), 16)
                        sp.dma_start(lb[:, :], A["ln2_b"][l].partition_broadcast(P)).then_inc(sem("ln"), 16)
                        for n in range(2):
                            for g in range(NG):
                                i = n * NG + g
                                if i >= SL:
                                    sp.wait_ge(sem("w_used"), i - SL + 1)
                                sp.dma_start(ring[:, i % SL, :, :], src[g, :, :, n * 512:(n + 1) * 512]).then_inc(sem(f"w_in{i % SL}"), 16)

                    @block.tensor
                    def _(pe):
                        for n in range(2):
                            for g in range(NG):
                                i = n * NG + g
                                pe.wait_ge(sem(f"w_in{i % SL}"), 16 * (i // SL + 1))
                                for t in range(nt):
                                    if n and g == 0:
                                        pe.wait_ge(sem("z1"), t + 1)
                                    for k in range(KG):
                                        m = pe.matmul(bank(t), hf[:, g * KG + k, t * P:(t + 1) * P], ring[:, i % SL, k, :],
                                                      start=g == 0 and k == 0, stop=g == NG - 1 and k == KG - 1)
                                    if g == NG - 1 and t < nt - 1:
                                        m.then_inc(sem("mm"), 1)
                                if g == NG - 1:
                                    m.then_inc(sem("mm"), 1)
                                else:
                                    m.then_inc(sem("w_used"), 1)
                                if g == NG - 1 and n == 0:
                                    pass

                    @block.vector
                    def _(dve):
                        dve.wait_ge(sem("ln"), 32)
                        for n in range(2):
                            c = slice(n * 512, (n + 1) * 512)
                            for t in range(nt):
                                i = n * nt + t
                                dve.wait_ge(sem("mm"), i + 1)
                                if i >= 2:
                                    dve.wait_ge(sem("z2"), i - 1)
                                dve.tensor_tensor(part[:, i % 2, :], bank(t), gate[:, t // LT, c], ALU.mult).then_inc(sem("z1"), 1)
                                dve.wait_ge(sem("z1"), i + 1)
                                dve.scalar_tensor_tensor(x[:, t, c], x[:, t, c], ALPHA, part[:, i % 2, :], ALU.mult, ALU.add).then_inc(sem("z2"), 1)
                                dve.wait_ge(sem("z2"), i + 1)
                                dve.bn_stats(st[:, t, n, :], x[:, t, c]).then_inc(sem("st"), 1)
                        for t in range(nt):
                            dve.wait_ge(sem("st"), nt + t + 1)
                            m = dve.bn_aggr(mv[:, t, :], st[:, t, :, :])
                        m.then_inc(sem("mv"), 1)
                        dve.wait_ge(sem("mv"), 1)
                        dve.tensor_scalar(rs[:, 0:nt], mv[:, 0:nt, 1], LN_EPS, None, ALU.add).then_inc(sem("var"), 1)
                        dve.wait_ge(sem("std"), 1)
                        dve.reciprocal(rs[:, 0:nt], rs[:, 0:nt]).then_inc(sem("rstd"), 1)
                        dve.wait_ge(sem("rstd"), 1)
                        for t in range(nt):
                            dve.tensor_scalar(x[:, t, :], x[:, t, :], mv[:, t, 0:1], rs[:, t:t + 1], ALU.subtract, ALU.mult).then_inc(sem("xn"), 1)
                            dve.wait_ge(sem("xn"), t + 1)
                            dve.tensor_tensor(x[:, t, :], x[:, t, :], lg[:, :], ALU.mult).then_inc(sem("xg"), 1)

                    @block.scalar
                    def _(act):
                        act.wait_ge(sem("var"), 1)
                        act.activation(rs[:, 0:nt], rs[:, 0:nt], ACT.Sqrt).then_inc(sem("std"), 1)

                    @block.gpsimd
                    def _(pool):
                        for t in range(nt):
                            pool.wait_ge(sem("xg"), t + 1)
                            pool.tensor_tensor(x[:, t, :], x[:, t, :], lb[:, :], ALU.add)

        def keep_x():
            with stage(nc) as (block, sem):
                @block.sync
                def _(sp):
                    sp.dma_start(x_keep, x[:, :, :]).then_inc(sem("kept"), 16)
                    sp.wait_ge(sem("kept"), 16)

        for l in range(DEPTH):
            last = l == DEPTH - 1
            modulation(l)
            norm(l, 0, 1, NT)
            with ExitStack() as sc:
                oc = sb(sc, "oc", [P, CTILES, TOK])
                keep_x()
                rwkv(l, oc, last)
                oa = sb(sc, "oa", [P, HA, TOK])
                of = sb(sc, "of", [P, F_GROUPS, TOK])
                attention(l, oa, last)
                fourier(l, of, last)
                with ExitStack() as s2:
                    y = sb(s2, "y", [P, KT, TOK])
                    merge(l, oa, of, oc, y, last)
                    out_proj(l, y, last)
            norm(l, 3, 4, LT if last else NT)
            ffn(l, last)
        with stage(nc) as (block, sem):
            @block.sync
            def _(sp):
                sp.dma_start(out.rearrange("b (t p) d -> p (b t) d", p=P), x[:, 0:LT, :]).then_inc(sem("out"), 16)
                sp.wait_ge(sem("out"), 16)


_INS = ["x", "c", "ctx", "c_ctx", "ada_w", "ada_b", "w_in", "lam_qk", "subln_g", "tshift_mu", "rw_w0", "rw_w2", "rw_a0",
        "rw_a2", "rw_g2", "rw_kk", "rw_ka", "rw_rk", "rw_lnw", "rw_lnb", "w_pa", "w_pf", "w_pc", "w_o", "ln1_g", "ln1_b",
        "ffn_up", "ffn_conv", "ffn_conv_b", "ffn_down", "ln2_g", "ln2_b"]


def kernel(**inputs):
    import numpy as _np
    import concourse.bacc as _bacc
    from concourse import mybir as _mybir
    from concourse.bass_utils import run_bass_kernel_spmd as _run

    nc = _bacc.Bacc("TRN2", target_bir_lowering=False, num_devices=1)
    arrays, aps = {}, {}
    for name, a in [(n, inputs[n]) for n in _INS] + list(tables().items()):
        a = _np.ascontiguousarray(a)
        arrays[f"in_{name}"] = a
        aps[name] = nc.dram_tensor(f"in_{name}", a.shape, _mybir.dt.from_np(a.dtype), kind="ExternalInput").ap()
    out = nc.dram_tensor("out_0", (1, SEQ, D_MODEL), _mybir.dt.float32, kind="ExternalOutput").ap()
    program(nc, aps, out)
    r = _run(nc, [arrays], core_ids=[0])
    return r.results[0]["out_0"]
```

```python
import math
from contextlib import ExitStack, contextmanager

import numpy as np
import concourse.bass as bass
from concourse import mybir

F32 = mybir.dt.float32
I32 = mybir.dt.int32
F32R = mybir.dt.float32r
ALU = mybir.AluOpType
ACT = mybir.ActivationFunctionType
AX = mybir.AxisListType

P = 128
D_MODEL, SEQ, CTX_LEN, DEPTH, GRID_W = 1024, 512, 256, 2, 64
TOK = SEQ + CTX_LEN
KT = D_MODEL // P
LT, CT = SEQ // P, CTX_LEN // P
NT = LT + CT
HA, DH_A, DV = 8, 64, 128
F_GROUPS, F_GROUP_W = 4, 128
D_F = F_GROUPS * F_GROUP_W
HC, HS_C = 8, 64
D_C = HC * HS_C
CTILES = D_C // P
LORA_G = 128
D_CS = 2 * D_C + 4 * 64
D_CO = D_C + LORA_G
D_FF = 2816
FT = D_FF // P
LN_EPS, GN_EPS, HEAD_EPS = 1e-5, HS_C * 1e-5, 1e-5
ALPHA = (2.0 * DEPTH) ** 0.25
DECAY = math.exp(-0.5)
OFF_Q, OFF_K, OFF_V = 0, D_MODEL, 2 * D_MODEL
OFF_F = 3 * D_MODEL
OFF_C = OFF_F + D_F
OFF_G = OFF_C + D_CS + D_CO
C = 64
GCOL = CTILES * P

PA = dict(ada_b=0, mu0=48, mu1=63, w0=78, a0=86, kk=94, ka=98, rk=102, lnw=106, lnb=110, subln=114, end=115)
PB = dict(conv=0, conv_b=3 * FT, c=4 * FT, c_ctx=4 * FT + KT, end=4 * FT + 2 * KT)
J_V, J_F, J_G, J_Q, J_K, N_PROJ = 0, 8, 12, 36, 44, 52
LEVELS = (1, 2, 4, 8, 16, 32)
(M_ID, M_LO, M_UP, M_LOI, M_UPI, M_LO1, M_UP1) = range(7)


def tables():
    t = {}
    t["ident"] = np.eye(P, dtype=np.float32)
    blk = np.zeros((P, P), np.float32)
    blk[:64, :64] = blk[64:, 64:] = 1.0
    t["blkones"] = blk
    i = np.arange(C)
    row, col = np.meshgrid(i, i, indexing="ij")
    low = lambda b: (row // b == col // b + 1) & (row // b % 2 == 1)
    m = [row == col, row > col, row < col, row >= col, row <= col, low(1), low(1).T]
    t["masks"] = np.ascontiguousarray(np.concatenate([np.stack(m, 1)] * 2, 0).astype(np.float32))
    lv = [low(b) for b in LEVELS[1:]] + [low(b).T for b in LEVELS[1:]]
    t["lvmasks"] = np.ascontiguousarray(np.concatenate([np.stack(lv, 1)] * 2, 0).astype(np.int32))
    n_freq = DH_A // 4
    inv = (np.float32(10000.0) ** (-np.arange(n_freq, dtype=np.float32) / n_freq)).astype(np.float32)
    tok = np.arange(SEQ)
    pos = np.stack([tok // GRID_W, tok % GRID_W]).astype(np.float32)
    d = np.arange(P) % DH_A
    ang = pos[d // 32] * inv[d % 16][:, None]
    sign = np.where(d % 32 < 16, -1.0, 1.0)[:, None]
    t["rope"] = np.stack([np.cos(ang), np.sin(ang) * sign], 1).astype(np.float32)
    w = np.arange(F_GROUP_W)
    aw = 2 * np.pi * (np.outer(w, w) % F_GROUP_W) / F_GROUP_W
    t["dft_w"] = np.concatenate([np.cos(aw), np.sin(aw)], 1).astype(np.float32)
    for name, n in (("dft_lat", SEQ), ("dft_ctx", CTX_LEN)):
        k = np.arange(n)
        at = 2 * np.pi * (np.outer(k, k) % n) / n
        s = 1.0 / math.sqrt(n * F_GROUP_W)
        both = np.stack([np.cos(at) * s, -np.sin(at) * s])
        t[name] = np.ascontiguousarray(both.reshape(2, n // P, P, n).transpose(2, 0, 1, 3).astype(np.float32))
    return t


@contextmanager
def stage(nc, done=None):
    sems = {}

    def sem(name):
        if name not in sems:
            sems[name] = nc.alloc_semaphore(nc.get_next_instruction_name() + "_" + name)
        return sems[name]

    with nc.Block(no_gpsimd_drain=True) as block:
        yield block, sem
    if sems:
        nc.clear_and_free_semaphores(list(sems.values()))
        nc.all_engine_barrier(sem_only=True)


def bc(ap, n, axis=1):
    v = ap.unsqueeze(axis)
    shape = list(v.shape)
    shape[axis] = n
    return v.to_broadcast(shape)


def program(nc, A, out):
    with ExitStack() as top:
        def sb(scope, name, shape, dt=F32):
            return scope.enter_context(nc.sbuf_tensor(nc.get_next_instruction_name() + "_" + name, shape, dt))

        ps = top.enter_context(nc.psum_tensor("ps", [P, 4096], F32))
        bank = lambda b, n=512, o=0: ps[:, b * 512 + o:b * 512 + o + n]
        x_keep = nc.dram_tensor("x_keep", [P, NT, D_MODEL], F32).ap()
        proj_d = nc.dram_tensor("proj_d", [N_PROJ, P, TOK], F32).ap()

        x = sb(top, "x", [P, NT, D_MODEL])
        ident = sb(top, "ident", [P, P])
        ones = sb(top, "ones", [P, P])
        blkones = sb(top, "blkones", [P, P])
        pa = [sb(top, f"pa{l}", [P, PA["end"]]) for l in range(DEPTH)]
        pb = [sb(top, f"pb{l}", [P, PB["end"]]) for l in range(DEPTH)]
        mu_own = [sb(top, f"mu_own{l}", [P, 15]) for l in range(DEPTH)]
        nlam = [sb(top, f"nlam{l}", [P, 1]) for l in range(DEPTH)]
        subln = [sb(top, f"subln{l}", [P, 1]) for l in range(DEPTH)]
        mod = sb(top, "mod", [P, 48, 2])

        with ExitStack() as sc, stage(nc) as (block, sem):
            rows = [sb(sc, f"rows{i}", [P, P]) for i in range(2 * DEPTH)]
            lqk = sb(sc, "lqk", [P, DEPTH, 4, 64])
            lpr = sb(sc, "lpr", [P, DEPTH, 2, 64])
            ldot = sb(sc, "ldot", [P, DEPTH, 2])
            lexp = sb(sc, "lexp", [P, DEPTH, 2])
            row_src = []
            for l in range(DEPTH):
                ra, rb = rows[2 * l], rows[2 * l + 1]
                r = lambda ap: ap.rearrange("(t p) -> t p", p=P)
                r2 = lambda ap: ap.rearrange("a (t p) -> (a t) p", p=P)
                row_src += [
                    (ra, PA["ada_b"], 48, r(A["ada_b"][l])), (ra, PA["mu0"], 30, r2(A["tshift_mu"][l])),
                    (ra, PA["w0"], 8, r2(A["rw_w0"][l])), (ra, PA["a0"], 8, r2(A["rw_a0"][l])),
                    (ra, PA["kk"], 4, r(A["rw_kk"][l])), (ra, PA["ka"], 4, r(A["rw_ka"][l])),
                    (ra, PA["rk"], 4, A["rw_rk"][l].rearrange("(t a) k -> t (a k)", a=2)),
                    (ra, PA["lnw"], 4, r(A["rw_lnw"][l])), (ra, PA["lnb"], 4, r(A["rw_lnb"][l])),
                    (ra, PA["subln"], 1, r(A["subln_g"][l])),
                    (rb, PB["conv"], 3 * FT, r2(A["ffn_conv"][l])), (rb, PB["conv_b"], FT, r(A["ffn_conv_b"][l])),
                    (rb, PB["c"], KT, r2(A["c"])), (rb, PB["c_ctx"], KT, r(A["c_ctx"])),
                ]

            @block.sync
            def _(sp):
                for dst, at, n, src in row_src:
                    sp.dma_start(dst[at:at + n, :], src).then_inc(sem("rows_in"), 16)
                sp.dma_start(x[:, 0:LT, :], A["x"].rearrange("b (t p) d -> p (b t) d", p=P)).then_inc(sem("x_in"), 16)
                sp.dma_start(x[:, LT:NT, :], A["ctx"].rearrange("b (t p) d -> p (b t) d", p=P)).then_inc(sem("x_in"), 16)
                sp.wait_ge(sem("x_in"), 32)

            @block.scalar
            def _(act):
                act.dma_start(ident[:, :], A["ident"]).then_inc(sem("const_in"), 16)
                act.dma_start(blkones[:, :], A["blkones"]).then_inc(sem("const_in"), 16)
                act.dma_start(lqk[:, :, :, :], A["lam_qk"].partition_broadcast(P)).then_inc(sem("const_in"), 16)
                act.wait_ge(sem("dots"), 1)
                act.activation(lexp[:, :, :], ldot[:, :, :], ACT.Exp).then_inc(sem("lexp"), 1)

            @block.tensor
            def _(pe):
                pe.wait_ge(sem("rows_in"), 16 * len(row_src))
                pe.wait_ge(sem("const_in"), 48)
                for i, src in enumerate(rows):
                    n = (PA, PB)[i % 2]["end"]
                    pe.transpose(bank(i, n), src[0:n, :], ident[0:n, 0:n]).then_inc(sem("columns"), 1)

            @block.gpsimd
            def _(pool):
                pool.memset(ones[:, :], 1.0)

            @block.vector
            def _(dve):
                dve.wait_ge(sem("const_in"), 48)
                dve.tensor_tensor(lpr[:, :, :, :], lqk[:, :, 0:4:2, :], lqk[:, :, 1:4:2, :], ALU.mult).then_inc(sem("dve"), 1)
                dve.wait_ge(sem("dve"), 1)
                dve.reduce_sum(ldot[:, :, :], lpr[:, :, :, :], AX.X).then_inc(sem("dots"), 1)
                for i in range(2 * DEPTH):
                    dst, n = (pa, pb)[i % 2][i // 2], (PA, PB)[i % 2]["end"]
                    dve.wait_ge(sem("columns"), i + 1)
                    dve.tensor_copy(dst[:, :], bank(i, n)).then_inc(sem("dve"), 1)
                dve.wait_ge(sem("dve"), 1 + 2 * DEPTH)
                dve.wait_ge(sem("lexp"), 1)
                for l in range(DEPTH):
                    lam_init = 0.8 - 0.6 * math.exp(-0.3 * l)
                    a = pa[l]
                    dve.tensor_scalar(subln[l][:, :], a[:, PA["subln"]:PA["subln"] + 1], 1.0 - lam_init, None, ALU.mult)
                    dve.tensor_tensor(nlam[l][:, :], lexp[:, l, 1:2], lexp[:, l, 0:1], ALU.subtract).then_inc(sem("half"), 1)
                    dve.tensor_tensor(mu_own[l][:, :], a[:, PA["mu0"]:PA["mu0"] + 15], a[:, PA["mu1"]:PA["mu1"] + 15],
                                      ALU.add).then_inc(sem("half"), 1)
                    dve.wait_ge(sem("half"), 2 * l + 2)
                    dve.tensor_scalar(nlam[l][:, :], nlam[l][:, :], -lam_init, None, ALU.add)
                    dve.tensor_scalar(mu_own[l][:, :], mu_own[l][:, :], -1.0, 1.0, ALU.mult, ALU.add)

        def modulation(l):
            with ExitStack() as sc, stage(nc) as (block, sem):
                NC, SL = 12, 4
                w = sb(sc, "ada_w", [P, SL, KT, 512])
                sg = sb(sc, "sig_c", [P, 2, KT])
                cc = sb(sc, "silu_c", [P, KT, 2])
                row = sb(sc, "mod_row", [2, NC, 512])
                raw = pb[l][:, PB["c"]:PB["end"]].rearrange("p (s k) -> p s k", s=2)
                src = A["ada_w"][l].rearrange("(k p) n -> p k n", p=P)

                @block.sync
                def _(sp):
                    for n in range(NC):
                        if n >= SL:
                            sp.wait_ge(sem("w_used"), n - SL + 1)
                        sp.dma_start(w[:, n % SL, :, :], src[:, :, n * 512:(n + 1) * 512]).then_inc(sem(f"w_in{n % SL}"), 16)

                @block.scalar
                def _(act):
                    act.activation(sg[:, :, :], raw, ACT.Sigmoid).then_inc(sem("sig"), 1)
                    for n in range(NC):
                        act.wait_ge(sem("w_used"), n + 1)
                        act.activation(row[:, n, :], ps[0:2, (n % 4) * 512:(n % 4 + 1) * 512], ACT.Copy).then_inc(sem("row"), 1)

                @block.vector
                def _(dve):
                    dve.wait_ge(sem("sig"), 1)
                    dve.tensor_tensor(cc[:, :, :].rearrange("p k s -> p s k"), raw, sg[:, :, :], ALU.mult).then_inc(sem("silu"), 1)
                    dve.wait_ge(sem("column"), 1)
                    b = pa[l][:, PA["ada_b"]:PA["ada_b"] + 48]
                    dve.tensor_tensor(mod[:, :, :], bank(4, 96).rearrange("p (n s) -> p n s", s=2),
                                      bc(b, 2, 2), ALU.add).then_inc(sem("mod"), 1)
                    dve.wait_ge(sem("mod"), 1)
                    for i in (1, 4):
                        dve.tensor_scalar(mod[:, 8 * i:8 * i + 8, :], mod[:, 8 * i:8 * i + 8, :], 1.0, None, ALU.add)

                @block.tensor
                def _(pe):
                    pe.wait_ge(sem("silu"), 1)
                    for n in range(NC):
                        pe.wait_ge(sem(f"w_in{n % SL}"), 16 * (n // SL + 1))
                        if n >= 4:
                            pe.wait_ge(sem("row"), n - 3)
                        for k in range(KT):
                            m = pe.matmul(ps[0:2, (n % 4) * 512:(n % 4 + 1) * 512], cc[:, k, :], w[:, n % SL, k, :],
                                          start=k == 0, stop=k == KT - 1)
                        m.then_inc(sem("w_used"), 1)
                    pe.wait_ge(sem("row"), NC)
                    for n in range(48):
                        m = pe.transpose(bank(4, 2, 2 * n), row[:, n // 4, (n % 4) * P:(n % 4 + 1) * P], ident[0:2, 0:2])
                    m.then_inc(sem("column"), 1)

        def norm(l, i_shift, i_scale, nt, h):
            lat, ctx = LT, nt - LT
            n_tok = nt * P
            with ExitStack() as sc, stage(nc) as (block, sem):
                xn = sb(sc, "xn", [P, NT, D_MODEL])
                hf = sb(sc, "h_f32", [P, 3, TOK])
                st = sb(sc, "stats", [P, NT, 2, 6])
                mv = sb(sc, "mean_var", [P, NT, 2])
                rs = sb(sc, "rstd", [P, NT])
                sh = lambda j, s: mod[:, 8 * i_shift + j, s:s + 1]
                sl = lambda j, s: mod[:, 8 * i_scale + j, s:s + 1]

                @block.vector
                def _(dve):
                    for t in range(nt):
                        for f in range(2):
                            i = dve.bn_stats(st[:, t, f, :], x[:, t, f * 512:(f + 1) * 512])
                        i.then_inc(sem("stats"), 1)
                    for t in range(nt):
                        dve.wait_ge(sem("stats"), t + 1)
                        i = dve.bn_aggr(mv[:, t, :], st[:, t, :, :])
                    i.then_inc(sem("mv"), 1)
                    dve.wait_ge(sem("mv"), 1)
                    dve.tensor_scalar(rs[:, 0:nt], mv[:, 0:nt, 1], LN_EPS, None, ALU.add).then_inc(sem("var"), 1)
                    dve.wait_ge(sem("std"), 1)
                    dve.reciprocal(rs[:, 0:nt], rs[:, 0:nt]).then_inc(sem("rstd"), 1)
                    dve.wait_ge(sem("rstd"), 1)
                    for t in range(nt):
                        dve.tensor_scalar(xn[:, t, :], x[:, t, :], mv[:, t, 0:1], rs[:, t:t + 1],
                                          ALU.subtract, ALU.mult).then_inc(sem("xn"), 1)
                    for j in range(KT):
                        dve.wait_ge(sem("hi"), j + 1)
                        dve.tensor_tensor(h[1][:, j, 0:n_tok], hf[:, j % 3, 0:n_tok], h[0][:, j, 0:n_tok].bitcast(F32),
                                          ALU.subtract).then_inc(sem("lo"), 1)

                @block.tensor
                def _(pe):
                    pe.wait_ge(sem("xn"), nt)
                    for j in range(KT):
                        if j >= 4:
                            pe.wait_ge(sem("h"), j - 3)
                        for t in range(nt):
                            m = pe.transpose(bank(2 * (j % 4), P, t * P), xn[:, t, j * P:(j + 1) * P], ident[:, :])
                        m.then_inc(sem("T"), 1)

                @block.scalar
                def _(act):
                    act.wait_ge(sem("var"), 1)
                    act.activation(rs[:, 0:nt], rs[:, 0:nt], ACT.Sqrt).then_inc(sem("std"), 1)
                    for j in range(KT):
                        act.wait_ge(sem("T"), j + 1)
                        if j >= 3:
                            act.wait_ge(sem("lo"), j - 2)
                        for s, (at, n) in enumerate(BOTH if ctx else LAT):
                            m = act.activation(hf[:, j % 3, at:at + n], bank(2 * (j % 4), n, at), ACT.Identity, bias=sh(j, s), scale=sl(j, s))
                        m.then_inc(sem("h"), 1)

                @block.gpsimd
                def _(pool):
                    for j in range(KT):
                        pool.wait_ge(sem("h"), j + 1)
                        pool.tensor_copy(h[0][:, j, 0:n_tok], hf[:, j % 3, 0:n_tok]).then_inc(sem("hi"), 1)

        def weight_rings(sc, n_raw, n_split):
            return (sb(sc, "w_raw", [P, n_raw, KT, P]), sb(sc, "w_hi", [P, n_split, KT, P], F32R),
                    sb(sc, "w_lo", [P, n_split, KT, P], F32R))

        def activation_pair(sc):
            return sb(sc, "h_hi", [P, KT, TOK], F32R), sb(sc, "h_lo", [P, KT, TOK], F32R)

        def load_weights(sp, sem, rings, n, src):
            n_raw = rings[0].shape[1]
            if n >= n_raw:
                sp.wait_ge(sem("w_lo"), n - n_raw + 1)
            sp.dma_start(rings[0][:, n % n_raw, 0:src.shape[1], :], src).then_inc(sem(f"w_in{n % n_raw}"), 16)

        def split_hi(act, sem, rings, n, kt=KT):
            n_raw, n_split = rings[0].shape[1], rings[1].shape[1]
            act.wait_ge(sem(f"w_in{n % n_raw}"), 16 * (n // n_raw + 1))
            if n >= n_split:
                act.wait_ge(sem("w_used"), n - n_split + 1)
            act.activation(rings[1][:, n % n_split, 0:kt, :], rings[0][:, n % n_raw, 0:kt, :], ACT.Copy).then_inc(sem("w_hi"), 1)

        def split_lo(eng, sem, rings, n, kt=KT):
            n_raw, n_split = rings[0].shape[1], rings[1].shape[1]
            eng.wait_ge(sem("w_hi"), n + 1)
            eng.tensor_tensor(rings[2][:, n % n_split, 0:kt, :], rings[0][:, n % n_raw, 0:kt, :],
                              rings[1][:, n % n_split, 0:kt, :].bitcast(F32), ALU.subtract).then_inc(sem("w_lo"), 1)

        def fm_product(pe, dst, w, a, ks, kt, widths):
            for k in ks:
                for i, (wi, ai) in enumerate(((0, 0), (0, 1), (1, 0))):
                    for at, n in widths:
                        m = pe.matmul(dst[:, at:at + n], w[wi][:, k, :], a[ai][:, k, at:at + n],
                                      start=k == 0 and i == 0, stop=k == kt - 1 and i == 2)
            return m

        def slot(rings, n):
            n_split = rings[1].shape[1]
            return rings[1][:, n % n_split], rings[2][:, n % n_split]

        BOTH = ((0, SEQ), (SEQ, CTX_LEN))
        LAT = ((0, SEQ),)

        def rwkv_inputs(l, h, raw, kk, rkd, oc, last):
            kf, wd, gd = raw[:, 0:4], raw[:, 8], raw[:, 14]
            if True:
                with ExitStack() as s2, stage(nc) as (block, sem):
                    rings = weight_rings(s2, 3, 2)
                    sq = sb(s2, "sq", [P, TOK])
                    nrm = sb(s2, "nrm", [P, 2, TOK])
                    src = A["w_in"][l].rearrange("(k p) n -> p k n", p=P)
                    p_of = lambda t: ps[:, (t % 4) * 1024:(t % 4) * 1024 + TOK]
                    seqs = lambda t: LAT if (last and t >= 10) else BOTH
                    col = lambda name, t: pa[l][:, PA[name] + t:PA[name] + t + 1]

                    @block.sync
                    def _(sp):
                        for t in range(15):
                            load_weights(sp, sem, rings, t, src[:, :, OFF_C + t * P:OFF_C + (t + 1) * P])

                    @block.tensor
                    def _(pe):
                        for t in range(15):
                            pe.wait_ge(sem("w_lo"), t + 1)
                            if t >= 4:
                                pe.wait_ge(sem("shifted"), t - 3)
                            fm_product(pe, p_of(t), slot(rings, t), h, range(KT), KT, seqs(t)).then_inc(sem("w_used"), 1)
                        for t in range(CTILES):
                            pe.wait_ge(sem("kk_sq"), t + 1)
                            if t == 0:
                                pe.wait_ge(sem("shifted"), 15)
                            elif t >= 2:
                                pe.wait_ge(sem("norm"), t - 1)
                            for at, n in BOTH:
                                m = pe.matmul(p_of(t % 2)[:, at:at + n], blkones[:, :], sq[:, at:at + n], start=True, stop=True)
                            m.then_inc(sem("kk_ss"), 1)

                    @block.scalar
                    def _(act):
                        split_hi(act, sem, rings, 0)
                        for t in range(15):
                            if t + 1 < 15:
                                split_hi(act, sem, rings, t + 1)
                            act.wait_ge(sem("w_used"), t + 1)
                            n = sum(w for _, w in seqs(t))
                            act.activation(raw[:, t, 0:n], p_of(t)[:, 0:n], ACT.Copy, scale=mu_own[l][:, t:t + 1]).then_inc(sem("own"), 1)
                        act.wait_ge(sem("shifted"), 15)
                        act.activation(wd, wd, ACT.Tanh)
                        act.activation(gd[:, 0:n], gd[:, 0:n], ACT.Sigmoid)
                        for t in range(CTILES):
                            act.wait_ge(sem("kk_raw"), t + 1)
                            if t:
                                act.wait_ge(sem("kk_ss"), t)
                            act.activation(sq[:, :], kk[:, t, :], ACT.Square).then_inc(sem("kk_sq"), 1)
                            act.wait_ge(sem("kk_ss"), t + 1)
                            if t >= 2:
                                act.wait_ge(sem("kk_done"), t - 1)
                            act.activation(nrm[:, t % 2, :], p_of(t % 2), ACT.Sqrt).then_inc(sem("norm"), 1)

                    @block.gpsimd
                    def _(pool):
                        pool.memset(rkd[:, :, :], 0.0)
                        pool.memset(oc[:, :, :], 0.0)
                        for t in range(15):
                            split_lo(pool, sem, rings, t)

                    @block.vector
                    def _(dve):
                        for t in range(15):
                            dve.wait_ge(sem("own"), t + 1)
                            for i, (at, n) in enumerate(seqs(t)):
                                o, p = raw[:, t, at:at + n], p_of(t)[:, at:at + n]
                                dve.scalar_tensor_tensor(o[:, 1:n], p[:, 0:n - 1], pa[l][:, PA["mu0"] + t:PA["mu0"] + t + 1],
                                                         o[:, 1:n], ALU.mult, ALU.add).then_inc(sem(f"prev{i}"), 1)
                            for i, (at, n) in enumerate(seqs(t)):
                                o, p = raw[:, t, at:at + n], p_of(t)[:, at:at + n]
                                dve.wait_ge(sem(f"prev{i}"), t + 1)
                                m = dve.scalar_tensor_tensor(o[:, 0:n - 1], p[:, 1:n], pa[l][:, PA["mu1"] + t:PA["mu1"] + t + 1],
                                                             o[:, 0:n - 1], ALU.mult, ALU.add)
                            m.then_inc(sem("shifted"), 1)
                        dve.wait_ge(sem("shifted"), 15)
                        for t in range(CTILES):
                            dve.tensor_scalar(kk[:, t, :], kf[:, t, :], col("kk", t), None, ALU.mult).then_inc(sem("kk_raw"), 1)
                        for t in range(CTILES):
                            n = nrm[:, t % 2, :]
                            dve.wait_ge(sem("norm"), t + 1)
                            dve.tensor_scalar(n, n, 1e-12, None, ALU.max).then_inc(sem("kk_n"), 1)
                            dve.wait_ge(sem("kk_n"), 2 * t + 1)
                            dve.reciprocal(n, n).then_inc(sem("kk_n"), 1)
                            dve.wait_ge(sem("kk_n"), 2 * t + 2)
                            dve.tensor_tensor(kk[:, t, :], kk[:, t, :], n, ALU.mult).then_inc(sem("kk_done"), 1)

        def project_rest(l, h, last):
            tiles = [(J_V + j, OFF_V + j * P, BOTH) for j in range(HA)]
            tiles += [(J_F + j, OFF_F + j * P, LAT if last else BOTH) for j in range(F_GROUPS)]
            tiles += [(J_G + j, OFF_G + j * P, LAT if last else BOTH) for j in range(3 * KT)]
            tiles += [(J_Q + j, OFF_Q + j * P, LAT if last else BOTH) for j in range(HA)]
            tiles += [(J_K + j, OFF_K + j * P, BOTH) for j in range(HA)]
            n_of = lambda widths: sum(n for _, n in widths)
            with ExitStack() as sc, stage(nc) as (block, sem):
                rings = weight_rings(sc, 3, 2)
                res = sb(sc, "result", [P, 3, TOK])
                src = A["w_in"][l].rearrange("(k p) n -> p k n", p=P)
                p_of = lambda i: ps[:, (i % 4) * 1024:(i % 4) * 1024 + TOK]

                def store(act, i):
                    j, _, widths = tiles[i]
                    act.wait_ge(sem("result"), i + 1)
                    act.dma_start(proj_d[j, :, 0:n_of(widths)], res[:, i % 3, 0:n_of(widths)]).then_inc(sem(f"stored{i % 3}"), 16)

                @block.sync
                def _(sp):
                    for i in range(len(tiles)):
                        load_weights(sp, sem, rings, i, src[:, :, tiles[i][1]:tiles[i][1] + P])

                @block.tensor
                def _(pe):
                    for i, (_, _, widths) in enumerate(tiles):
                        pe.wait_ge(sem("w_lo"), i + 1)
                        if i >= 4:
                            pe.wait_ge(sem("result"), i - 3)
                        fm_product(pe, p_of(i), slot(rings, i), h, range(KT), KT, widths).then_inc(sem("w_used"), 1)

                @block.scalar
                def _(act):
                    for i in range(len(tiles)):
                        split_hi(act, sem, rings, i)
                        if i:
                            store(act, i - 1)
                    store(act, len(tiles) - 1)
                    for i in range(len(tiles) - 3, len(tiles)):
                        act.wait_ge(sem(f"stored{i % 3}"), 16 * (i // 3 + 1))

                @block.gpsimd
                def _(pool):
                    for i in range(len(tiles)):
                        split_lo(pool, sem, rings, i)

                @block.vector
                def _(dve):
                    for i, (_, _, widths) in enumerate(tiles):
                        dve.wait_ge(sem("w_used"), i + 1)
                        if i >= 3:
                            dve.wait_ge(sem(f"stored{i % 3}"), 16 * (i // 3))
                        dve.tensor_copy(res[:, i % 3, 0:n_of(widths)], p_of(i)[:, 0:n_of(widths)]).then_inc(sem("result"), 1)

        def rwkv_scan(l, s2, oc, rkd, kf, vf, wd, ad, rf, kk, last):
            G = [P, GCOL]
            two = lambda name: [sb(s2, f"{name}{d}", G) for d in range(2)]
            masks = sb(s2, "masks", [P, 7, C])
            lvm = sb(s2, "lvmasks", [P, 10, C], I32)
            reset = sb(s2, "reset", [P, 2, GCOL])
            w2 = sb(s2, "w2", [P, 2, D_C])
            a2 = sb(s2, "a2", [P, 2, D_C])
            S = [sb(s2, f"S{i}", G) for i in range(3)]
            PC = sb(s2, "PC", [P, 2, 2, CTILES])
            Rt, W1T, Btm, Ktm, Vtm, QB, QK = (two(n) for n in ("Rt", "W1T", "Btm", "Ktm", "Vtm", "QB", "QK"))
            spare = x[:, :, :].rearrange("p t d -> p (t d)")
            Kttm, NAT, T, TT, Y, MT = ([spare[:, (2 * i + d) * GCOL:(2 * i + d + 1) * GCOL] for d in range(2)] for i in range(6))
            MV, U, W2s = Y, T, NAT
            sg, L, Lx, Lr, EN, a, kd, Bh, Bp, vg = (sb(s2, n, G) for n in ("sg", "L", "Lx", "Lr", "EN", "a", "kd", "Bh", "Bp", "vg"))
            g3 = lambda ap: ap.rearrange("p (t c) -> p t c", t=CTILES)
            g8 = lambda ap: ap.rearrange("p (g c) -> p g c", c=C)
            cols = lambda name, d: pa[l][:, PA[name] + 4 * d:PA[name] + 4 * d + 4]

            with stage(nc) as (block, sem):
                @block.sync
                def _(sp):
                    sp.dma_start(masks[:, :, :], A["masks"]).then_inc(sem("in"), 16)
                    sp.dma_start(lvm[:, :, :], A["lvmasks"]).then_inc(sem("in"), 16)
                    sp.wait_ge(sem("zero"), 1)
                    for d in range(2):
                        sp.dma_start(w2[64 * d:64 * d + 64, d, :], A["rw_w2"][l, d]).then_inc(sem("in"), 16)
                        sp.dma_start(a2[64 * d:64 * d + 64, d, :], A["rw_a2"][l, d]).then_inc(sem("in"), 16)
                    sp.wait_ge(sem("in"), 96)

                @block.gpsimd
                def _(pool):
                    pool.memset(w2[:, :, :], 0.0)
                    pool.memset(a2[:, :, :], 0.0).then_inc(sem("zero"), 1)
                    pool.memset(S[0][:, :], 0.0)

                @block.vector
                def _(dve):
                    dve.memset(reset[:, :, :], 1.0).then_inc(sem("one"), 1)
                    dve.wait_ge(sem("one"), 1)
                    dve.memset(g8(reset[:, 0, :])[:, :, 0:1], 0.0)
                    dve.memset(g8(reset[:, 1, :])[:, :, C - 1:C], 0.0)

            def groups(base, n, want_y):
                n_fm, n_pr = (6, 5) if want_y else (5, 3)
                with nc.Fori(0, n) as g, stage(nc) as (block, sem):
                    at = (base + g * P, base + (n - 1) * P - g * P)
                    sl = lambda ap, d: ap[:, :, bass.ds(at[d], P)]
                    chunk_of = lambda d, q: q if d == 0 else 1 - q
                    HT = [(hh, t) for t in range(CTILES) for hh in range(2)]
                    hc = lambda hh, t: (hh * CTILES + t) * C
                    tc = lambda t, i: t * P + i * C
                    rows = lambda i: slice(64 * i, 64 * i + 64)

                    @block.tensor
                    def _(pe):
                        for d in range(2):
                            if d:
                                pe.wait_ge(sem("sig"), d)
                                pe.wait_ge(sem("prod"), n_pr * d)
                            for b, w, lora in ((0, w2, wd), (1, a2, ad)):
                                for t in range(CTILES):
                                    m = pe.matmul(bank(b, P, t * P), w[:, d, t * P:(t + 1) * P], lora[:, bass.ds(at[d], P)],
                                                  start=True, stop=True)
                            m.then_inc(sem("z"), 1)
                            pe.wait_ge(sem("fm"), n_fm * (d + 1))

                            def product(b, o, stat, mov):
                                for t in range(CTILES):
                                    for i in range(2):
                                        for hh in range(2):
                                            m = pe.matmul(ps[rows(i), (b + hh) * 512 + o + t * C:(b + hh) * 512 + o + (t + 1) * C],
                                                          stat[rows(hh), tc(t, i):tc(t, i) + C], mov[rows(hh), tc(t, i):tc(t, i) + C],
                                                          start=True, stop=True)
                                m.then_inc(sem("pmm"), 1)
                            product(6, 0, Bh, Lx)
                            product(6, 256, Lx, Bh)
                            pe.wait_ge(sem("sig"), d + 1)
                            product(0, 0, EN, Lx)
                            if d:
                                pe.wait_ge(sem("tm"), 4 * d)
                            if want_y:
                                product(0, 256, Bh, Rt[d])
                                product(2, 0, EN, Rt[d])
                            pe.wait_ge(sem("vg"), d + 1)
                            pe.wait_ge(sem("prod"), n_pr * (d + 1))
                            for b, src in ((2, Lx), (3, Bp), (4, Lr), (5, vg)):
                                for t in range(CTILES):
                                    m = pe.transpose(bank(b, P, t * P), src[:, t * P:(t + 1) * P], ident[:, :])
                                m.then_inc(sem("tmm"), 1)
                        def diag(b, stat, mov, name):
                            for hh, t in HT:
                                for i in range(2):
                                    c0 = hc(hh, t)
                                    m = pe.matmul(ps[rows(i), b * 512 + c0:b * 512 + c0 + C], stat[rows(i), c0:c0 + C],
                                                  mov[rows(i), c0:c0 + C], start=True, stop=True)
                            m.then_inc(sem(name), 1)
                        pe.wait_ge(sem("tm"), 8)
                        for n_lv in range(5):
                            for d in range(2):
                                pe.wait_ge(sem(f"T{d}"), n_lv + 1)
                                diag(4 + d, NAT[d], T[d], f"Ymm{d}")
                            for d in range(2):
                                pe.wait_ge(sem(f"Y{d}"), n_lv + 1)
                                if n_lv < 4:
                                    diag(6 + d, TT[d], Y[d], f"off{d}")
                                diag(2 + d, Y[d], TT[d], f"offT{d}")
                        for d in range(2):
                            for hh, t in HT:
                                for i in range(2):
                                    m = pe.matmul(ps[rows(i), (6 + d) * 512 + hc(hh, t):(6 + d) * 512 + hc(hh, t) + C],
                                                  MT[d][rows(i), hc(hh, t):hc(hh, t) + C],
                                                  Vtm[d][rows(i), tc(t, hh):tc(t, hh) + C], start=True, stop=True)
                            m.then_inc(sem("MVmm"), 1)
                        for d in range(2):
                            pe.wait_ge(sem(f"T{d}"), 6)
                            if d:
                                pe.wait_ge(sem("W1"), d)
                            for t in range(CTILES):
                                for i in range(2):
                                    for hh in range(2):
                                        m = pe.matmul(ps[rows(hh), i * 512 + t * C:i * 512 + (t + 1) * C],
                                                      Kttm[d][rows(i), tc(t, hh):tc(t, hh) + C],
                                                      TT[d][rows(i), hc(hh, t):hc(hh, t) + C], start=True, stop=True)
                            m.then_inc(sem("W1mm"), 1)
                        for d in range(2):
                            pe.wait_ge(sem("MV"), d + 1)
                            diag(4 + d, TT[d], MV[d], "W2mm")
                        for q in range(2):
                            if q == 0:
                                pe.wait_ge(sem("W1"), 2)
                                pe.wait_ge(sem("W2"), 4)
                            else:
                                pe.wait_ge(sem("S"), 1)
                            for t in range(CTILES):
                                for d in range(2):
                                    i = chunk_of(d, q)
                                    for hh in range(2):
                                        m = pe.matmul(ps[rows(i), (2 + hh) * 512 + t * C:(2 + hh) * 512 + (t + 1) * C],
                                                      W1T[d][rows(hh), tc(t, i):tc(t, i) + C],
                                                      S[q][rows(hh), (d * CTILES + t) * C:(d * CTILES + t + 1) * C], start=True, stop=True)
                            m.then_inc(sem("Umm"), 1)
                            pe.wait_ge(sem("U"), q + 1)
                            for t in range(CTILES):
                                for d in range(2):
                                    i = chunk_of(d, q)
                                    for hh in range(2):
                                        o = ps[rows(hh), (6 + d) * 512 + t * C:(6 + d) * 512 + (t + 1) * C]
                                        pe.matmul(o, Btm[d][rows(i), tc(t, hh):tc(t, hh) + C],
                                                  U[q][rows(i), hc(hh, t):hc(hh, t) + C], start=True, stop=False)
                                        m = pe.matmul(o, Ktm[d][rows(i), tc(t, hh):tc(t, hh) + C],
                                                      Vtm[d][rows(i), tc(t, hh):tc(t, hh) + C], start=False, stop=True)
                            m.then_inc(sem("Smm"), 1)
                        if want_y:
                            for d in range(2):
                                for t in range(CTILES):
                                    for i in range(2):
                                        q = chunk_of(d, i)
                                        for hh in range(2):
                                            m = pe.matmul(ps[rows(hh), (4 + d) * 512 + tc(t, i):(4 + d) * 512 + tc(t, i) + C],
                                                          S[q][rows(hh), (d * CTILES + t) * C:(d * CTILES + t + 1) * C],
                                                          Rt[d][rows(hh), tc(t, i):tc(t, i) + C], start=True, stop=True)
                                m.then_inc(sem("YRmm"), 1)
                                for t in range(CTILES):
                                    for i in range(2):
                                        q = chunk_of(d, i)
                                        for hh in range(2):
                                            o = ps[rows(hh), (2 * d + i) * 512 + t * C:(2 * d + i) * 512 + (t + 1) * C]
                                            c0 = hc(hh, t)
                                            pe.matmul(o, U[q][rows(i), c0:c0 + C], QB[d][rows(i), c0:c0 + C], start=True, stop=False)
                                            m = pe.matmul(o, Vtm[d][rows(i), tc(t, hh):tc(t, hh) + C],
                                                          QK[d][rows(i), c0:c0 + C], start=False, stop=True)
                                m.then_inc(sem("YUmm"), 1)

                    @block.scalar
                    def _(act):
                        for d in range(2):
                            act.wait_ge(sem("z"), d + 1)
                            if d:
                                act.wait_ge(sem("fm"), n_fm * d)
                            for b, name, dst in ((0, "w0", sg), (1, "a0", a)):
                                for t in range(CTILES):
                                    m = act.activation(dst[:, t * P:(t + 1) * P], bank(b, P, t * P), ACT.Sigmoid,
                                                       bias=cols(name, d)[:, t:t + 1])
                            m.then_inc(sem("sig"), 1)
                            act.wait_ge(sem("sums"), 3 * d + 3)
                            act.activation(Lx[:, :], Lx[:, :], ACT.Exp, scale=-DECAY).then_inc(sem("exp"), 1)
                            act.activation(EN[:, :], L[:, :], ACT.Exp, scale=DECAY).then_inc(sem("exp"), 1)
                            last_t = C - 1 if d == 0 else 0
                            for q in range(2):
                                i = chunk_of(d, q)
                                act.activation(PC[:, q, d, :], g3(L[:, :])[:, :, i * C + last_t], ACT.Exp, scale=-DECAY)
                            act.activation(Lr[:, :], Lr[:, :], ACT.Exp, scale=-DECAY).then_inc(sem("exp"), 1)
                            act.wait_ge(sem("exp"), 4 * d + 3)
                            act.activation(L[:, :], L[:, :], ACT.Exp, scale=-DECAY).then_inc(sem("exp"), 1)
                            for n_tm, (b, dst) in enumerate(((2, Kttm), (3, Btm), (4, Ktm), (5, Vtm))):
                                act.wait_ge(sem("tmm"), 4 * d + n_tm + 1)
                                act.activation(dst[d][:, :], bank(b), ACT.Copy).then_inc(sem("tm"), 1)
                        for n_lv in range(5):
                            for d in range(2):
                                act.wait_ge(sem(f"Ymm{d}"), n_lv + 1)
                                if n_lv:
                                    act.wait_ge(sem(f"offT{d}"), n_lv)
                                elif want_y:
                                    act.wait_ge(sem("rk"), 2 * d + 2)
                                act.activation(Y[d][:, :], bank(4 + d), ACT.Copy).then_inc(sem(f"Y{d}"), 1)
                        for d in range(2):
                            act.wait_ge(sem("MVmm"), d + 1)
                            act.activation(MV[d][:, :], bank(6 + d), ACT.Copy).then_inc(sem("MV"), 1)
                        for d in range(2):
                            act.wait_ge(sem("W2mm"), d + 1)
                            for q in range(2):
                                r = rows(chunk_of(d, q))
                                act.activation(W2s[q][r, :], ps[r, (4 + d) * 512:(5 + d) * 512], ACT.Copy).then_inc(sem("W2"), 1)
                        if want_y:
                            for d in range(2):
                                act.wait_ge(sem("YRmm"), d + 1)
                                act.activation((sg, a)[d][:, :], bank(4 + d), ACT.Copy).then_inc(sem("YR"), 1)

                    @block.gpsimd
                    def _(pool):
                        for d in range(2):
                            if d:
                                pool.wait_ge(sem("tmm"), 4 * d)
                            pool.tensor_copy(g3(vg[:, :]), sl(vf, d)).then_inc(sem("vg"), 1)
                            if want_y:
                                pool.wait_ge(sem("kd"), 2 * d + 2)
                                pool.tensor_tensor(g3(Y[d][:, :]), sl(rf, d), g3(kd[:, :]), ALU.mult).then_inc(sem("rk"), 1)
                                pool.wait_ge(sem("rk"), 2 * d + 1)
                                pool.tensor_tensor(sl(rkd, d), sl(rkd, d), g3(Y[d][:, :]), ALU.add).then_inc(sem("rk"), 1)
                        for q in range(2):
                            if q:
                                pool.wait_ge(sem("S"), q)
                            else:
                                pool.wait_ge(sem("exp"), 8)
                            pool.tensor_tensor(S[q + 1][:, :].rearrange("p (g v) -> p g v", v=C),
                                               S[q][:, :].rearrange("p (g v) -> p g v", v=C),
                                               bc(PC[:, q].rearrange("p d t -> p (d t)"), C, 2), ALU.mult).then_inc(sem("SP"), 1)
                        if want_y:
                            for d in range(2):
                                pool.wait_ge(sem("Ysum"), d + 1)
                                pool.tensor_tensor(sl(oc, d), sl(oc, d), g3((sg, a)[d][:, :]), ALU.add).then_inc(sem("yacc"), 1)
                                pool.wait_ge(sem("yacc"), d + 1)
                        pool.wait_ge(sem("S"), 2)
                        if want_y:
                            pool.wait_ge(sem("YRmm"), 2)
                        else:
                            pool.wait_ge(sem("Smm"), 2)
                        pool.tensor_copy(S[0][:, :], S[2][:, :])

                    @block.vector
                    def _(dve):
                        for d in range(2):
                            rev = slice(None, None, -1) if d else slice(None)
                            tl = 0 if d else C - 1
                            dve.wait_ge(sem("sig"), d + 1)
                            if d:
                                dve.wait_ge(sem("pmm"), n_pr * d)
                                dve.wait_ge(sem("tmm"), 4 * d)
                            dve.tensor_tensor_scan(L[:, rev], reset[:, d, rev], sg[:, rev], 0.0, ALU.mult, ALU.add).then_inc(sem("sums"), 1)
                            dve.wait_ge(sem("sums"), 3 * d + 1)
                            dve.tensor_tensor(Lx[:, :], L[:, :], sg[:, :], ALU.subtract).then_inc(sem("sums"), 1)
                            dve.tensor_tensor(g8(Lr[:, :]), g8(L[:, :])[:, :, tl:tl + 1].to_broadcast([P, 8, C]), g8(L[:, :]),
                                              ALU.subtract).then_inc(sem("sums"), 1)
                            if d and want_y:
                                dve.wait_ge(sem("rk"), 2 * d - 1)
                            dve.scalar_tensor_tensor(g3(kd[:, :]), g3(a[:, :]), -1.0, bc(pa[l][:, PA["ka"]:PA["ka"] + 4], P, 2),
                                                     ALU.add, ALU.mult).then_inc(sem("kd"), 1)
                            dve.wait_ge(sem("kd"), 2 * d + 1)
                            dve.scalar_tensor_tensor(g3(kd[:, :]), g3(kd[:, :]), 1.0, sl(kf, d), ALU.add, ALU.mult).then_inc(sem("kd"), 1)
                            dve.scalar_tensor_tensor(g3(a[:, :]), sl(kk, d), -1.0, g3(a[:, :]), ALU.mult, ALU.mult).then_inc(sem("b"), 1)
                            dve.wait_ge(sem("exp"), 4 * d + 1)
                            dve.tensor_tensor(g3(Lx[:, :]), sl(kk, d), g3(Lx[:, :]), ALU.mult).then_inc(sem("fm"), 1)
                            dve.wait_ge(sem("exp"), 4 * d + 2)
                            dve.wait_ge(sem("b"), d + 1)
                            dve.tensor_tensor(Bh[:, :], a[:, :], EN[:, :], ALU.mult).then_inc(sem("fm"), 1)
                            dve.wait_ge(sem("kd"), 2 * d + 2)
                            dve.tensor_tensor(EN[:, :], kd[:, :], EN[:, :], ALU.mult).then_inc(sem("fm"), 1)
                            dve.wait_ge(sem("exp"), 4 * d + 3)
                            dve.tensor_tensor(Bp[:, :], a[:, :], Lr[:, :], ALU.mult).then_inc(sem("fm"), 1)
                            dve.tensor_tensor(Lr[:, :], kd[:, :], Lr[:, :], ALU.mult).then_inc(sem("fm"), 1)
                            if want_y:
                                dve.wait_ge(sem("exp"), 4 * d + 4)
                                dve.tensor_tensor(g3(Rt[d][:, :]), sl(rf, d), g3(L[:, :]), ALU.mult).then_inc(sem("fm"), 1)
                            pv = lambda b, o: ps[:, b * 512:(b + 2) * 512].rearrange("p (h c) -> p h c", h=2)[:, :, o:o + 256]\
                                .rearrange("p h (t c) -> p h t c", t=CTILES)
                            o4 = lambda ap: ap.rearrange("p (h t c) -> p h t c", h=2, t=CTILES)
                            mk = lambda m: masks[:, m, :].unsqueeze(1).unsqueeze(1).to_broadcast([P, 2, CTILES, C])
                            strict, incl = ((M_UP, M_UPI), (M_LO, M_LOI))[d]
                            lo1, up1 = ((M_LO1, M_UP1), (M_UP1, M_LO1))[d]
                            dve.wait_ge(sem("pmm"), n_pr * d + 2)
                            dve.tensor_tensor(o4(NAT[d][:, :]), pv(6, 0), mk(strict), ALU.mult).then_inc(sem("prod"), 1)
                            dve.tensor_tensor(o4(T[d][:, :]), pv(6, 256), mk(lo1), ALU.mult).then_inc(sem("prod"), 1)
                            dve.wait_ge(sem("pmm"), n_pr * d + min(n_pr, 4))
                            dve.tensor_tensor(o4(MT[d][:, :]), pv(0, 0), mk(strict), ALU.mult).then_inc(sem("prod"), 1)
                            if want_y:
                                dve.tensor_tensor(o4(QB[d][:, :]), pv(0, 256), mk(incl), ALU.mult).then_inc(sem("prod"), 1)
                                dve.wait_ge(sem("pmm"), n_pr * d + 5)
                                dve.tensor_tensor(o4(QK[d][:, :]), pv(2, 0), mk(incl), ALU.mult).then_inc(sem("prod"), 1)
                            m8 = lambda m: masks[:, m, :].unsqueeze(1).to_broadcast([P, 8, C])
                            dve.wait_ge(sem("prod"), n_pr * d + 2)
                            dve.tensor_tensor(g8(T[d][:, :]), g8(T[d][:, :]), m8(M_ID), ALU.add)
                            dve.tensor_tensor(g8(TT[d][:, :]), g8(NAT[d][:, :]), m8(up1), ALU.mult).then_inc(sem("TT1"), 1)
                            dve.wait_ge(sem("TT1"), d + 1)
                            dve.tensor_tensor(g8(TT[d][:, :]), g8(TT[d][:, :]), m8(M_ID), ALU.add).then_inc(sem(f"T{d}"), 1)
                        for n_lv in range(5):
                            for d in range(2):
                                lo, up = (n_lv, 5 + n_lv) if d == 0 else (5 + n_lv, n_lv)
                                lm = lambda m: lvm[:, m, :].unsqueeze(1).to_broadcast([P, 8, C])
                                if n_lv < 4:
                                    dve.wait_ge(sem(f"off{d}"), n_lv + 1)
                                    dve.copy_predicated(g8(T[d][:, :]), lm(lo), g8(bank(6 + d)))
                                dve.wait_ge(sem(f"offT{d}"), n_lv + 1)
                                dve.copy_predicated(g8(TT[d][:, :]), lm(up), g8(bank(2 + d))).then_inc(sem(f"T{d}"), 1)
                        for d in range(2):
                            dve.wait_ge(sem("W1mm"), d + 1)
                            dve.tensor_copy(W1T[d][:, :].rearrange("p (t i c) -> p i t c", t=CTILES, i=2),
                                            ps[:, 0:1024].rearrange("p (i c) -> p i c", i=2)[:, :, 0:256]
                                            .rearrange("p i (t c) -> p i t c", t=CTILES)).then_inc(sem("W1"), 1)
                        half = lambda b: ps[:, b * 512:(b + 2) * 512].rearrange("p (b c) -> p b c", b=2)[:, :, 0:256]
                        for q in range(2):
                            dve.wait_ge(sem("Umm"), q + 1)
                            if q == 0:
                                dve.wait_ge(sem("W2"), 4)
                            dve.tensor_tensor(U[q][:, :].rearrange("p (b c) -> p b c", b=2), half(2),
                                              W2s[q][:, :].rearrange("p (b c) -> p b c", b=2), ALU.add).then_inc(sem("U"), 1)
                            dve.wait_ge(sem("Smm"), q + 1)
                            dve.wait_ge(sem("SP"), q + 1)
                            s_n = S[q + 1][:, :].rearrange("p (b c) -> p b c", b=2)
                            dve.tensor_tensor(s_n, s_n, half(6), ALU.add).then_inc(sem("S"), 1)
                        if want_y:
                            for d in range(2):
                                dve.wait_ge(sem("YUmm"), d + 1)
                                dve.wait_ge(sem("YR"), d + 1)
                                y = (sg, a)[d][:, :].rearrange("p (t i c) -> p t i c", t=CTILES, i=2)
                                dve.tensor_tensor(y, y, half(2 * d).rearrange("p i (t c) -> p t i c", t=CTILES), ALU.add).then_inc(sem("Ysum"), 1)

            groups(SEQ, CTX_LEN // P, not last)
            groups(0, SEQ // P, True)

        def rwkv_output(l, oc, rkd, vf, gd, last):
            seqs = LAT if last else BOTH
            n_tok = SEQ if last else TOK
            with ExitStack() as sc, stage(nc) as (block, sem):
                g2 = sb(sc, "g2", [P, D_C])
                yc = sb(sc, "yc", [P, 2, TOK])
                sq = sb(sc, "ysq", [P, 2, TOK])
                pr = lambda i: ps[:, i * 1024:i * 1024 + n_tok]
                col = lambda name, t: pa[l][:, PA[name] + t:PA[name] + t + 1]

                @block.sync
                def _(sp):
                    sp.dma_start(g2[:, :], A["rw_g2"][l]).then_inc(sem("g2"), 16)

                @block.gpsimd
                def _(pool):
                    for t in range(CTILES):
                        pool.tensor_scalar(rkd[:, t, 0:n_tok], rkd[:, t, 0:n_tok], col("rk", t), None, ALU.mult).then_inc(sem("rk"), 1)

                @block.tensor
                def _(pe):
                    pe.wait_ge(sem("g2"), 16)
                    for t in range(CTILES):
                        def by(dst, stat, mov, name):
                            for at, n in seqs:
                                m = pe.matmul(dst[:, at:at + n], stat, mov[:, at:at + n], start=True, stop=True)
                            m.then_inc(sem(name), 1)
                        if t:
                            pe.wait_ge(sem("done"), t)
                        by(pr(0), blkones[:, :], oc[:, t, :], "mean")
                        by(pr(1), g2[:, t * P:(t + 1) * P], gd, "gate")
                        pe.wait_ge(sem("rk"), t + 1)
                        by(pr(2), blkones[:, :], rkd[:, t, :], "bonus")
                        pe.wait_ge(sem("sq"), t + 1)
                        by(pr(3), blkones[:, :], sq[:, t % 2, :], "var")

                @block.scalar
                def _(act):
                    for t in range(CTILES):
                        act.wait_ge(sem("yc"), t + 1)
                        act.activation(sq[:, t % 2, 0:n_tok], yc[:, t % 2, 0:n_tok], ACT.Square).then_inc(sem("sq"), 1)
                        act.wait_ge(sem("v"), t + 1)
                        act.activation(sq[:, t % 2, 0:n_tok], sq[:, t % 2, 0:n_tok], ACT.Sqrt).then_inc(sem("std"), 1)
                        act.wait_ge(sem("yn"), t + 1)
                        act.activation(yc[:, t % 2, 0:n_tok], yc[:, t % 2, 0:n_tok], ACT.Identity, bias=col("lnb", t),
                                       scale=col("lnw", t)).then_inc(sem("yl"), 1)

                @block.vector
                def _(dve):
                    steps = [0]

                    def link(ins):
                        steps[0] += 1
                        ins.then_inc(sem("dve"), 1)
                        dve.wait_ge(sem("dve"), steps[0])
                    for t in range(CTILES):
                        c, s, y = yc[:, t % 2, 0:n_tok], sq[:, t % 2, 0:n_tok], oc[:, t, 0:n_tok]
                        dve.wait_ge(sem("mean"), t + 1)
                        dve.scalar_tensor_tensor(c, pr(0), -1.0 / HS_C, y, ALU.mult, ALU.add).then_inc(sem("yc"), 1)
                        dve.wait_ge(sem("bonus"), t + 1)
                        dve.wait_ge(sem("yc"), t + 1)
                        link(dve.tensor_tensor(y, pr(2), vf[:, t, 0:n_tok], ALU.mult))
                        dve.wait_ge(sem("var"), t + 1)
                        dve.tensor_scalar(s, pr(3), 1.0 / HS_C, GN_EPS, ALU.mult, ALU.add).then_inc(sem("v"), 1)
                        dve.wait_ge(sem("std"), t + 1)
                        link(dve.reciprocal(s, s))
                        dve.tensor_tensor(c, c, s, ALU.mult).then_inc(sem("yn"), 1)
                        dve.wait_ge(sem("yl"), t + 1)
                        link(dve.tensor_tensor(y, y, c, ALU.add))
                        dve.wait_ge(sem("gate"), t + 1)
                        dve.tensor_tensor(y, y, pr(1), ALU.mult).then_inc(sem("done"), 1)

        def attention(l, oa, last):
            nq = LT if last else NT
            q_seqs = LAT if last else BOTH
            q_tok = SEQ if last else TOK
            units = [(j, u) for j in range(HA) for u in range(nq)]
            N = len(units)
            users = []
            for n, (j, u) in enumerate(units):
                if u == 0:
                    users.append(("v", j))
                users += [("s", n, 0), ("s", n, 1)]
            place = {who: i for i, who in enumerate(users)}
            buf = lambda who, w: ps[:, (place[who] % 3) * 1024:(place[who] % 3) * 1024 + w]
            with ExitStack() as sc, stage(nc) as (block, sem):
                rope = sb(sc, "rope", [P, 2, SEQ])
                qp = sb(sc, "q_plain", [P, 2, TOK])
                kp = sb(sc, "k_plain", [P, 2, TOK])
                vp = sb(sc, "v_fm", [P, 2, TOK])
                qr = sb(sc, "q_rot", [P, 2, SEQ])
                kr = sb(sc, "k_rot", [P, 2, SEQ])
                vt = sb(sc, "v_tm", [P, 2, NT, P])
                shuf = sb(sc, "shuf", [P, 2, SEQ])
                rcos = sb(sc, "rcos", [P, 2, SEQ])
                E = sb(sc, "E", [P, 3, 2, TOK])
                mx = sb(sc, "mx", [P, 3, 2])
                sm = sb(sc, "sm", [P, 3, 2])
                ratio = sb(sc, "ratio", [P, 3])
                diag = sb(sc, "diag", [P, 3, P])
                at = sb(sc, "a_T", [P, 2, TOK])
                swap = list(range(16, 32)) + list(range(16))
                n_keys = lambda u: TOK if u < LT else CTX_LEN
                k_tiles = lambda u: range(NT) if u < LT else range(LT, NT)

                def wait_free(pe, who):
                    i = place[who] - 3
                    if i >= 0:
                        if users[i][0] == "v":
                            pe.wait_ge(sem("vt"), users[i][1] + 1)
                        else:
                            pe.wait_ge(sem(f"exp{users[i][2]}"), users[i][1] + 1)

                @block.sync
                def _(sp):
                    sp.dma_start(rope[:, :, :], A["rope"]).then_inc(sem("rope"), 16)
                    for j in range(HA):
                        if j >= 2:
                            sp.wait_ge(sem("s1_mm"), (j - 1) * nq)
                            sp.wait_ge(sem("v_mm"), j - 1)
                            sp.wait_ge(sem("rot"), 2 * (j - 1))
                        sp.dma_start(vp[:, j % 2, :], proj_d[J_V + j]).then_inc(sem(f"v_in{j % 2}"), 16)
                        sp.dma_start(qp[:, j % 2, 0:q_tok], proj_d[J_Q + j, :, 0:q_tok]).then_inc(sem(f"q_in{j % 2}"), 16)
                        sp.dma_start(kp[:, j % 2, :], proj_d[J_K + j]).then_inc(sem(f"k_in{j % 2}"), 16)

                @block.tensor
                def _(pe):
                    def scores(n):
                        j, u = units[n]
                        if u == 0:
                            pe.wait_ge(sem(f"v_in{j % 2}"), 16 * (j // 2 + 1))
                            wait_free(pe, ("v", j))
                            for t in range(NT):
                                m = pe.transpose(buf(("v", j), TOK)[:, t * P:(t + 1) * P], vp[:, j % 2, t * P:(t + 1) * P], ident[:, :])
                            m.then_inc(sem("v_mm"), 1)
                            pe.wait_ge(sem("rot"), 2 * j + 2)
                            pe.wait_ge(sem(f"q_in{j % 2}"), 16 * (j // 2 + 1))
                            pe.wait_ge(sem(f"k_in{j % 2}"), 16 * (j // 2 + 1))
                        qs = slice(u * P, (u + 1) * P)
                        for c in range(2):
                            wait_free(pe, ("s", n, c))
                            o = buf(("s", n, c), TOK)
                            r = slice(c * DH_A, (c + 1) * DH_A)
                            k0 = 0
                            if u < LT:
                                pe.matmul(o[:, 0:SEQ], qr[r, j % 2, qs], kr[r, j % 2, :], start=True, stop=True)
                                k0 = SEQ
                            pe.matmul(o[:, k0:k0 + CTX_LEN], qp[r, j % 2, qs], kp[r, j % 2, SEQ:TOK],
                                      start=True, stop=True).then_inc(sem(f"s{c}_mm"), 1)

                    def values(n):
                        j, u = units[n]
                        pe.wait_ge(sem("a"), n + 1)
                        pe.wait_ge(sem("diag"), n + 1)
                        if n:
                            pe.wait_ge(sem("o_read"), n)
                        kts = list(k_tiles(u))
                        for i, kt in enumerate(kts):
                            m = pe.matmul(ps[:, 3072 + i * P:3072 + (i + 1) * P], E[:, n % 3, 1, i * P:(i + 1) * P], diag[:, n % 3, :],
                                          start=True, stop=True)
                        m.then_inc(sem("aT_mm"), 1)
                        pe.wait_ge(sem("aT"), n + 1)
                        for i, kt in enumerate(kts):
                            m = pe.matmul(bank(7, P, 384), vt[:, j % 2, kt, :], at[:, n % 2, i * P:(i + 1) * P],
                                          start=i == 0, stop=i == len(kts) - 1)
                        m.then_inc(sem("o"), 1)

                    pe.wait_ge(sem("rope"), 16)
                    scores(0)
                    scores(1)
                    for n in range(N):
                        if n + 2 < N:
                            scores(n + 2)
                        values(n)

                @block.scalar
                def _(act):
                    def soft(n):
                        j, u = units[n]
                        if u == 0:
                            act.wait_ge(sem("v_mm"), j + 1)
                            if j >= 2:
                                act.wait_ge(sem("o"), (j - 1) * nq)
                            act.activation(vt[:, j % 2, :, :].rearrange("p t d -> p (t d)"), buf(("v", j), TOK), ACT.Copy).then_inc(sem("vt"), 1)
                        w = n_keys(u)
                        if n >= 3:
                            act.wait_ge(sem("aT_mm"), n - 2)
                            act.wait_ge(sem("rec"), n - 2)
                        for c in range(2):
                            act.wait_ge(sem(f"max{c}"), n + 1)
                            act.activation(E[:, n % 3, c, 0:w], buf(("s", n, c), w), ACT.Exp, bias=mx[:, n % 3, c:c + 1],
                                           scale=DH_A ** -0.5, accum_out=sm[:, n % 3, c:c + 1]).then_inc(sem(f"exp{c}"), 1)
                    soft(0)
                    for n, (j, u) in enumerate(units):
                        if n + 1 < N:
                            soft(n + 1)
                        w = n_keys(u)
                        act.wait_ge(sem("aT_mm"), n + 1)
                        if n >= 2:
                            act.wait_ge(sem("o"), n - 1)
                        act.activation(at[:, n % 2, 0:w], ps[:, 3072:3072 + w], ACT.Copy).then_inc(sem("aT"), 1)
                        act.wait_ge(sem("o"), n + 1)
                        act.activation(oa[:, j, u * P:(u + 1) * P], bank(7, P, 384), ACT.Copy).then_inc(sem("o_read"), 1)

                @block.gpsimd
                def _(pool):
                    pool.wait_ge(sem("rope"), 16)
                    for j in range(HA):
                        for i in range(2):
                            n = 2 * j + i
                            pool.wait_ge(sem(f"{'qk'[i]}_in{j % 2}"), 16 * (j // 2 + 1))
                            if n >= 2:
                                pool.wait_ge(sem("rot"), n - 1)
                            pool.tensor_tensor(rcos[:, i, :], (qp, kp)[i][:, j % 2, 0:SEQ], rope[:, 0, :], ALU.mult).then_inc(sem("rcos"), 1)
                            pool.wait_ge(sem("rcos"), n + 1)
                            pool.wait_ge(sem("shuf"), n + 1)
                            pool.tensor_tensor(shuf[:, i, :], shuf[:, i, :], rope[:, 1, :], ALU.mult).then_inc(sem("rsin"), 1)
                            pool.wait_ge(sem("rsin"), n + 1)
                            if j >= 2:
                                pool.wait_ge(sem("s1_mm"), (j - 1) * nq)
                            pool.tensor_tensor((qr, kr)[i][:, j % 2, :], shuf[:, i, :], rcos[:, i, :], ALU.add).then_inc(sem("rot"), 1)

                @block.vector
                def _(dve):
                    def shuffle(j):
                        for i in range(2):
                            n = 2 * j + i
                            dve.wait_ge(sem(f"{'qk'[i]}_in{j % 2}"), 16 * (j // 2 + 1))
                            if n >= 2:
                                dve.wait_ge(sem("rot"), n - 1)
                            dve.stream_shuffle(shuf[:, i, :], (qp, kp)[i][:, j % 2, 0:SEQ], swap).then_inc(sem("shuf"), 1)

                    def maxima(n):
                        w = n_keys(units[n][1])
                        if n >= 3:
                            dve.wait_ge(sem("exp1"), n - 2)
                        for c in range(2):
                            m = mx[:, n % 3, c:c + 1]
                            dve.wait_ge(sem(f"s{c}_mm"), n + 1)
                            dve.tensor_reduce(m, buf(("s", n, c), w), AX.X, ALU.max).then_inc(sem(f"mraw{c}"), 1)
                            dve.wait_ge(sem(f"mraw{c}"), n + 1)
                            dve.tensor_scalar(m, m, -DH_A ** -0.5, None, ALU.mult).then_inc(sem(f"max{c}"), 1)

                    def combine(n):
                        w = n_keys(units[n][1])
                        s, q = sm[:, n % 3, :], ratio[:, n % 3:n % 3 + 1]
                        dve.wait_ge(sem("exp0"), n + 1)
                        dve.wait_ge(sem("exp1"), n + 1)
                        if n >= 3:
                            dve.wait_ge(sem("aT_mm"), n - 2)
                        dve.tensor_tensor(q, s[:, 0:1], nlam[l][:, :], ALU.mult).then_inc(sem("q"), 1)
                        dve.wait_ge(sem("q"), 2 * n + 1)
                        dve.reciprocal(s, s).then_inc(sem("rec"), 1)
                        dve.wait_ge(sem("rec"), n + 1)
                        dve.tensor_tensor(q, q, s[:, 1:2], ALU.mult).then_inc(sem("q"), 1)
                        dve.tensor_scalar(diag[:, n % 3, :], ident[:, :], s[:, 0:1], None, ALU.mult).then_inc(sem("diag"), 1)
                        dve.wait_ge(sem("q"), 2 * n + 2)
                        dve.scalar_tensor_tensor(E[:, n % 3, 1, 0:w], E[:, n % 3, 1, 0:w], q, E[:, n % 3, 0, 0:w],
                                                 ALU.mult, ALU.add).then_inc(sem("a"), 1)

                    dve.wait_ge(sem("rope"), 16)
                    shuffle(0)
                    maxima(0)
                    for n in range(N):
                        if n + 1 < N:
                            if units[n + 1][1] == 1 and units[n + 1][0] + 1 < HA:
                                shuffle(units[n + 1][0] + 1)
                            maxima(n + 1)
                        combine(n)

            with ExitStack() as sc, stage(nc) as (block, sem):
                sq = sb(sc, "osq", [P, 2, TOK])
                rr = sb(sc, "orr", [P, 2, TOK])
                p_of = lambda j: ps[:, (j % 2) * 1024:(j % 2) * 1024 + q_tok]

                @block.scalar
                def _(act):
                    for j in range(HA):
                        if j >= 2:
                            act.wait_ge(sem("ss"), j - 1)
                        act.activation(sq[:, j % 2, 0:q_tok], oa[:, j, 0:q_tok], ACT.Square).then_inc(sem("sq"), 1)
                        if j:
                            act.wait_ge(sem("ms"), j)
                            act.activation(rr[:, (j - 1) % 2, 0:q_tok], rr[:, (j - 1) % 2, 0:q_tok], ACT.Sqrt).then_inc(sem("std"), 1)
                    act.wait_ge(sem("ms"), HA)
                    act.activation(rr[:, (HA - 1) % 2, 0:q_tok], rr[:, (HA - 1) % 2, 0:q_tok], ACT.Sqrt).then_inc(sem("std"), 1)

                @block.tensor
                def _(pe):
                    for j in range(HA):
                        pe.wait_ge(sem("sq"), j + 1)
                        if j >= 2:
                            pe.wait_ge(sem("ms"), j - 1)
                        for at_, n in q_seqs:
                            m = pe.matmul(p_of(j)[:, at_:at_ + n], ones[:, :], sq[:, j % 2, at_:at_ + n], start=True, stop=True)
                        m.then_inc(sem("ss"), 1)

                @block.vector
                def _(dve):
                    def mean(j):
                        dve.wait_ge(sem("ss"), j + 1)
                        dve.tensor_scalar(rr[:, j % 2, 0:q_tok], p_of(j), 1.0 / DV, HEAD_EPS, ALU.mult, ALU.add).then_inc(sem("ms"), 1)
                    mean(0)
                    for j in range(HA):
                        if j + 1 < HA:
                            mean(j + 1)
                        r = rr[:, j % 2, 0:q_tok]
                        dve.wait_ge(sem("std"), j + 1)
                        dve.reciprocal(r, r).then_inc(sem("rec"), 1)
                        dve.wait_ge(sem("rec"), j + 1)
                        dve.scalar_tensor_tensor(oa[:, j, 0:q_tok], oa[:, j, 0:q_tok], subln[l][:, :], r, ALU.mult, ALU.mult).then_inc(sem("oa"), 1)
                        dve.wait_ge(sem("oa"), j + 1)

        def fourier(l, of, last):
            seqs = LAT if last else BOTH
            n_tok = SEQ if last else TOK
            nt = n_tok // P
            with ExitStack() as sc, stage(nc) as (block, sem):
                dw = sb(sc, "dft_w", [P, 2 * P])
                dl = sb(sc, "dft_lat", [P, 2, LT, SEQ])
                dc = sb(sc, "dft_ctx", [P, 2, CT, CTX_LEN])
                f = sb(sc, "f", [P, F_GROUPS, TOK])
                z = sb(sc, "z", [P, 2, NT, 2 * P])

                @block.sync
                def _(sp):
                    sp.dma_start(f[:, :, 0:n_tok], proj_d[J_F:J_F + F_GROUPS, :, 0:n_tok].rearrange("j p n -> p j n")).then_inc(sem("f"), 16)
                    sp.dma_start(dw[:, :], A["dft_w"]).then_inc(sem("dft"), 16)
                    sp.dma_start(dl[:, :, :, :], A["dft_lat"]).then_inc(sem("dft"), 16)
                    sp.dma_start(dc[:, :, :, :], A["dft_ctx"]).then_inc(sem("dft"), 16)

                @block.tensor
                def _(pe):
                    pe.wait_ge(sem("f"), 16)
                    pe.wait_ge(sem("dft"), 48)
                    for j in range(F_GROUPS):
                        for t in range(nt):
                            if j and t % 2 == 0:
                                pe.wait_ge(sem("z"), 3 * (j - 1) + t // 2 + 1 if nt == 6 else 2 * (j - 1) + t // 2 + 1)
                            m = pe.matmul(ps[:, 1024 + t * 256:1280 + t * 256], f[:, j, t * P:(t + 1) * P], dw[:, :],
                                          start=True, stop=True)
                            if t % 2:
                                m.then_inc(sem("zmm"), 1)
                        pe.wait_ge(sem("z"), (nt // 2) * (j + 1))
                        if j:
                            pe.wait_ge(sem("of"), j)
                        for i in range(2 * LT):
                            m = pe.matmul(bank(6), z[:, j % 2, i % LT, (i // LT) * P:(i // LT + 1) * P], dl[:, i // LT, i % LT, :],
                                          start=i == 0, stop=i == 2 * LT - 1)
                        if not last:
                            for i in range(2 * CT):
                                m = pe.matmul(bank(7, 256), z[:, j % 2, LT + i % CT, (i // CT) * P:(i // CT + 1) * P], dc[:, i // CT, i % CT, :],
                                              start=i == 0, stop=i == 2 * CT - 1)
                        m.then_inc(sem("ofmm"), 1)

                @block.vector
                def _(dve):
                    for j in range(F_GROUPS):
                        for i in range(nt // 2):
                            dve.wait_ge(sem("zmm"), j * (nt // 2) + i + 1)
                            if j >= 2:
                                dve.wait_ge(sem("ofmm"), j - 1)
                            dve.tensor_copy(z[:, j % 2, 2 * i:2 * i + 2, :].rearrange("p a b -> p (a b)"), bank(2 + i)).then_inc(sem("z"), 1)

                @block.scalar
                def _(act):
                    for j in range(F_GROUPS):
                        act.wait_ge(sem("ofmm"), j + 1)
                        act.activation(of[:, j, 0:n_tok], ps[:, 3072:3072 + n_tok], ACT.Copy).then_inc(sem("of"), 1)

        def merge(l, b, w_name, o, kt, y, last):
            seqs = LAT if last else BOTH
            n_tok = SEQ if last else TOK
            with ExitStack() as sc, stage(nc) as (block, sem):
                rings = weight_rings(sc, 3, 2)
                pair = sb(sc, "o_hi", [P, kt, TOK], F32R), sb(sc, "o_lo", [P, kt, TOK], F32R)
                gt = sb(sc, "gate", [P, 3, TOK])
                pr = sb(sc, "gated", [P, 2, TOK])
                src = A[w_name][l].rearrange("(k p) n -> p k n", p=P)
                p_of = lambda j: ps[:, (j % 4) * 1024:(j % 4) * 1024 + n_tok]
                out_of = (lambda j: y[:, j, 0:n_tok]) if b == 0 else (lambda j: pr[:, j % 2, 0:n_tok])

                @block.sync
                def _(sp):
                    for j in range(KT):
                        load_weights(sp, sem, rings, j, src[:, :, j * P:(j + 1) * P])
                        if j >= 3:
                            sp.wait_ge(sem("gated"), j - 2)
                        sp.dma_start(gt[:, j % 3, 0:n_tok], proj_d[J_G + b * KT + j, :, 0:n_tok]).then_inc(sem(f"gate_in{j % 3}"), 16)

                @block.tensor
                def _(pe):
                    for j in range(KT):
                        pe.wait_ge(sem("w_lo"), j + 1)
                        if j >= 4:
                            pe.wait_ge(sem("gated"), j - 3)
                        for k in range(kt):
                            if j == 0:
                                pe.wait_ge(sem("o_lo"), k + 1)
                            m = fm_product(pe, p_of(j), slot(rings, j), pair, (k,), kt, seqs)
                        m.then_inc(sem("w_used"), 1)

                @block.scalar
                def _(act):
                    split_hi(act, sem, rings, 0, kt)
                    for k in range(kt):
                        act.activation(pair[0][:, k, 0:n_tok], o[:, k, 0:n_tok], ACT.Copy).then_inc(sem("o_hi"), 1)
                    for j in range(KT):
                        if j + 1 < KT:
                            split_hi(act, sem, rings, j + 1, kt)
                        act.wait_ge(sem(f"gate_in{j % 3}"), 16 * (j // 3 + 1))
                        g = gt[:, j % 3, 0:n_tok]
                        act.activation(g, g, ACT.Sigmoid).then_inc(sem("gate"), 1)

                @block.vector
                def _(dve):
                    for k in range(kt):
                        dve.wait_ge(sem("o_hi"), k + 1)
                        dve.tensor_tensor(pair[1][:, k, 0:n_tok], o[:, k, 0:n_tok], pair[0][:, k, 0:n_tok].bitcast(F32),
                                          ALU.subtract).then_inc(sem("o_lo"), 1)
                    for j in range(KT):
                        dve.wait_ge(sem("w_used"), j + 1)
                        dve.wait_ge(sem("gate"), j + 1)
                        if b and j >= 2:
                            dve.wait_ge(sem("sum"), j - 1)
                        dve.tensor_tensor(out_of(j), gt[:, j % 3, 0:n_tok], p_of(j), ALU.mult).then_inc(sem("gated"), 1)
                        if b:
                            dve.wait_ge(sem("gated"), j + 1)
                            dve.tensor_tensor(y[:, j, 0:n_tok], y[:, j, 0:n_tok], out_of(j), ALU.add).then_inc(sem("sum"), 1)

                @block.gpsimd
                def _(pool):
                    for j in range(KT):
                        split_lo(pool, sem, rings, j, kt)

        def gate_rows(sc, i_mod, streams):
            g = sb(sc, "gate_row", [P, 2, D_MODEL])
            with ExitStack() as s2, stage(nc) as (block, sem):
                diag = sb(s2, "diag", [P, 2 * KT, P])

                @block.vector
                def _(dve):
                    for s in range(streams):
                        for j in range(KT):
                            m = dve.tensor_scalar(diag[:, s * KT + j, :], ident[:, :], mod[:, 8 * i_mod + j, s:s + 1], None, ALU.mult)
                        m.then_inc(sem("diag"), 1)

                @block.tensor
                def _(pe):
                    for s in range(streams):
                        pe.wait_ge(sem("diag"), s + 1)
                        for j in range(0, KT, 4):
                            m = pe.matmul(bank(2 * s + j // 4), ones[:, :], diag[:, s * KT + j:s * KT + j + 4, :].rearrange("p a b -> p (a b)"),
                                          start=True, stop=True)
                        m.then_inc(sem("row"), 1)

                @block.scalar
                def _(act):
                    for s in range(streams):
                        act.wait_ge(sem("row"), s + 1)
                        act.activation(g[:, s, :], ps[:, s * 1024:(s + 1) * 1024], ACT.Copy)
            return g

        def out_proj(l, y, last):
            nt = LT if last else NT
            with ExitStack() as sc:
                gate = gate_rows(sc, 2, 1 if last else 2)
                with stage(nc) as (block, sem):
                    w = sb(sc, "w_o", [P, KT, D_MODEL])
                    lg = sb(sc, "ln_g", [P, D_MODEL])
                    lb = sb(sc, "ln_b", [P, D_MODEL])
                    tmp = sb(sc, "tmp", [P, 2, D_MODEL])

                    @block.sync
                    def _(sp):
                        sp.dma_start(w[:, :, :], A["w_o"][l].rearrange("(k p) n -> p k n", p=P)).then_inc(sem("w"), 16)
                        sp.dma_start(x[:, :, :], x_keep).then_inc(sem("x_back"), 16)
                        sp.dma_start(lg[:, :], A["ln1_g"][l].partition_broadcast(P)).then_inc(sem("ln"), 16)
                        sp.dma_start(lb[:, :], A["ln1_b"][l].partition_broadcast(P)).then_inc(sem("ln"), 16)

                    @block.tensor
                    def _(pe):
                        pe.wait_ge(sem("w"), 16)
                        for t in range(nt):
                            if t >= 4:
                                pe.wait_ge(sem("z1"), t - 3)
                            for n in range(2):
                                for k in range(KT):
                                    m = pe.matmul(bank(2 * (t % 4) + n), y[:, k, t * P:(t + 1) * P], w[:, k, n * 512:(n + 1) * 512],
                                                  start=k == 0, stop=k == KT - 1)
                            m.then_inc(sem("mm"), 1)

                    norm_tail(block, sem, sc, nt, lambda t: ps[:, (t % 4) * 1024:(t % 4) * 1024 + 1024], gate, tmp, lg, lb, "x_back")

        def norm_tail(block, sem, sc, nt, p_of, gate, tmp, lg, lb, wait_x):
            st = sb(sc, "stats", [P, NT, 2, 6])
            mv = sb(sc, "mean_var", [P, NT, 2])
            rs = sb(sc, "rstd", [P, NT])

            @block.vector
            def _(dve):
                if wait_x:
                    dve.wait_ge(sem(wait_x), 16)
                dve.wait_ge(sem("ln"), 32)

                def first(t):
                    dve.wait_ge(sem("mm"), t + 1)
                    if t >= 2:
                        dve.wait_ge(sem("z2"), t - 1)
                    dve.tensor_tensor(tmp[:, t % 2, :], p_of(t), gate[:, t // LT, :], ALU.mult).then_inc(sem("z1"), 1)
                    dve.wait_ge(sem("z1"), t + 1)
                    dve.scalar_tensor_tensor(x[:, t, :], x[:, t, :], ALPHA, tmp[:, t % 2, :], ALU.mult, ALU.add).then_inc(sem("z2"), 1)
                    dve.wait_ge(sem("z2"), t + 1)
                    for f in range(2):
                        i = dve.bn_stats(st[:, t, f, :], x[:, t, f * 512:(f + 1) * 512])
                    i.then_inc(sem("st"), 1)
                    dve.wait_ge(sem("st"), t + 1)
                    dve.bn_aggr(mv[:, t, :], st[:, t, :, :]).then_inc(sem("mv"), 1)
                    dve.wait_ge(sem("mv"), t + 1)
                    dve.tensor_scalar(rs[:, t:t + 1], mv[:, t, 1:2], LN_EPS, None, ALU.add).then_inc(sem("var"), 1)

                def second(t):
                    dve.wait_ge(sem("std"), t + 1)
                    dve.reciprocal(rs[:, t:t + 1], rs[:, t:t + 1]).then_inc(sem("rstd"), 1)
                    dve.wait_ge(sem("rstd"), t + 1)
                    dve.tensor_scalar(x[:, t, :], x[:, t, :], mv[:, t, 0:1], rs[:, t:t + 1], ALU.subtract, ALU.mult).then_inc(sem("xn"), 1)
                    dve.wait_ge(sem("xn"), t + 1)
                    dve.tensor_tensor(x[:, t, :], x[:, t, :], lg[:, :], ALU.mult).then_inc(sem("xg"), 1)

                first(0)
                for t in range(nt):
                    if t + 1 < nt:
                        first(t + 1)
                    second(t)

            @block.gpsimd
            def _(pool):
                for t in range(nt):
                    pool.wait_ge(sem("xg"), t + 1)
                    pool.tensor_tensor(x[:, t, :], x[:, t, :], lb[:, :], ALU.add)

            @block.scalar
            def _(act):
                for t in range(nt):
                    act.wait_ge(sem("var"), t + 1)
                    act.activation(rs[:, t:t + 1], rs[:, t:t + 1], ACT.Sqrt).then_inc(sem("std"), 1)

        def ffn(l, hf, h, last):
            seqs = LAT if last else BOTH
            n_tok = SEQ if last else TOK
            nt = n_tok // P
            if True:
                with ExitStack() as s2, stage(nc) as (block, sem):
                    rings = weight_rings(s2, 3, 2)
                    cv = sb(s2, "conv", [P, 2, TOK])
                    src = A["ffn_up"][l].rearrange("(k p) n -> p k n", p=P)
                    p_of = lambda s: ps[:, (s % 4) * 1024:(s % 4) * 1024 + n_tok]
                    tap = lambda i, j: pb[l][:, PB["conv"] + i * FT + j:PB["conv"] + i * FT + j + 1]

                    @block.sync
                    def _(sp):
                        for s in range(2 * FT):
                            o = (D_FF, 0)[s % 2] + s // 2 * P
                            load_weights(sp, sem, rings, s, src[:, :, o:o + P])

                    @block.tensor
                    def _(pe):
                        for s in range(2 * FT):
                            pe.wait_ge(sem("w_lo"), s + 1)
                            if s >= 4:
                                pe.wait_ge(sem("hf"), s // 2 - 1)
                            fm_product(pe, p_of(s), slot(rings, s), h, range(KT), KT, seqs).then_inc(sem("w_used"), 1)

                    @block.scalar
                    def _(act):
                        def own(j):
                            act.wait_ge(sem("w_used"), 2 * j + 1)
                            if j >= 2:
                                act.wait_ge(sem("hf"), j - 1)
                            act.activation(cv[:, j % 2, 0:n_tok], p_of(2 * j), ACT.Copy, scale=tap(1, j)).then_inc(sem("own"), 1)
                        for s in range(3):
                            split_hi(act, sem, rings, s)
                        own(0)
                        for j in range(FT):
                            for s in (2 * j + 3, 2 * j + 4):
                                if s < 2 * FT:
                                    split_hi(act, sem, rings, s)
                            if j + 1 < FT:
                                own(j + 1)
                            act.wait_ge(sem("conv"), j + 1)
                            act.activation(cv[:, j % 2, 0:n_tok], cv[:, j % 2, 0:n_tok], ACT.Gelu,
                                           bias=pb[l][:, PB["conv_b"] + j:PB["conv_b"] + j + 1]).then_inc(sem("gelu"), 1)

                    @block.gpsimd
                    def _(pool):
                        for s in range(2 * FT):
                            split_lo(pool, sem, rings, s)

                    @block.vector
                    def _(dve):
                        def conv(j):
                            dve.wait_ge(sem("own"), j + 1)
                            for i, (at, n) in enumerate(seqs):
                                o, p = cv[:, j % 2, at:at + n], p_of(2 * j)[:, at:at + n]
                                dve.scalar_tensor_tensor(o[:, 1:n], p[:, 0:n - 1], tap(0, j), o[:, 1:n], ALU.mult, ALU.add).then_inc(sem(f"prev{i}"), 1)
                            for i, (at, n) in enumerate(seqs):
                                o, p = cv[:, j % 2, at:at + n], p_of(2 * j)[:, at:at + n]
                                dve.wait_ge(sem(f"prev{i}"), j + 1)
                                m = dve.scalar_tensor_tensor(o[:, 0:n - 1], p[:, 1:n], tap(2, j), o[:, 0:n - 1], ALU.mult, ALU.add)
                            m.then_inc(sem("conv"), 1)
                        conv(0)
                        for j in range(FT):
                            dve.wait_ge(sem("gelu"), j + 1)
                            dve.wait_ge(sem("w_used"), 2 * j + 2)
                            dve.tensor_tensor(hf[:, j, :], cv[:, j % 2, 0:n_tok], p_of(2 * j + 1), ALU.mult).then_inc(sem("hf"), 1)
                            if j + 1 < FT:
                                conv(j + 1)

        def ffn_down(l, hf, last):
            nt = LT if last else NT
            with ExitStack() as sc:
                gate = gate_rows(sc, 5, 1 if last else 2)
                with stage(nc) as (block, sem):
                    KG, SL = 2, 8
                    ring = sb(sc, "w_down", [P, SL, KG, 512])
                    lg = sb(sc, "ln_g", [P, D_MODEL])
                    lb = sb(sc, "ln_b", [P, D_MODEL])
                    part = sb(sc, "part", [P, 2, 512])
                    src = A["ffn_down"][l].rearrange("(g k p) n -> g p k n", p=P, k=KG)
                    NG = FT // KG
                    st = sb(sc, "stats", [P, NT, 2, 6])
                    mv = sb(sc, "mean_var", [P, NT, 2])
                    rs = sb(sc, "rstd", [P, NT])

                    @block.sync
                    def _(sp):
                        sp.dma_start(lg[:, :], A["ln2_g"][l].partition_broadcast(P)).then_inc(sem("ln"), 16)
                        sp.dma_start(lb[:, :], A["ln2_b"][l].partition_broadcast(P)).then_inc(sem("ln"), 16)
                        for n in range(2):
                            for g in range(NG):
                                i = n * NG + g
                                if i >= SL:
                                    sp.wait_ge(sem("w_used"), i - SL + 1)
                                sp.dma_start(ring[:, i % SL, :, :], src[g, :, :, n * 512:(n + 1) * 512]).then_inc(sem(f"w_in{i % SL}"), 16)

                    @block.tensor
                    def _(pe):
                        for n in range(2):
                            for g in range(NG):
                                i = n * NG + g
                                pe.wait_ge(sem(f"w_in{i % SL}"), 16 * (i // SL + 1))
                                for t in range(nt):
                                    if n and g == 0:
                                        pe.wait_ge(sem("z1"), t + 1)
                                    for k in range(KG):
                                        m = pe.matmul(bank(t), hf[:, g * KG + k, t * P:(t + 1) * P], ring[:, i % SL, k, :],
                                                      start=g == 0 and k == 0, stop=g == NG - 1 and k == KG - 1)
                                    if g == NG - 1 and t < nt - 1:
                                        m.then_inc(sem("mm"), 1)
                                if g == NG - 1:
                                    m.then_inc(sem("mm"), 1)
                                else:
                                    m.then_inc(sem("w_used"), 1)

                    @block.vector
                    def _(dve):
                        dve.wait_ge(sem("ln"), 32)
                        for n in range(2):
                            c = slice(n * 512, (n + 1) * 512)
                            for t in range(nt):
                                i = n * nt + t
                                dve.wait_ge(sem("mm"), i + 1)
                                if i >= 2:
                                    dve.wait_ge(sem("z2"), i - 1)
                                dve.tensor_tensor(part[:, i % 2, :], bank(t), gate[:, t // LT, c], ALU.mult).then_inc(sem("z1"), 1)
                                dve.wait_ge(sem("z1"), i + 1)
                                dve.scalar_tensor_tensor(x[:, t, c], x[:, t, c], ALPHA, part[:, i % 2, :], ALU.mult, ALU.add).then_inc(sem("z2"), 1)
                                dve.wait_ge(sem("z2"), i + 1)
                                dve.bn_stats(st[:, t, n, :], x[:, t, c]).then_inc(sem("st"), 1)
                        for t in range(nt):
                            dve.wait_ge(sem("st"), nt + t + 1)
                            m = dve.bn_aggr(mv[:, t, :], st[:, t, :, :])
                        m.then_inc(sem("mv"), 1)
                        dve.wait_ge(sem("mv"), 1)
                        dve.tensor_scalar(rs[:, 0:nt], mv[:, 0:nt, 1], LN_EPS, None, ALU.add).then_inc(sem("var"), 1)
                        dve.wait_ge(sem("std"), 1)
                        dve.reciprocal(rs[:, 0:nt], rs[:, 0:nt]).then_inc(sem("rstd"), 1)
                        dve.wait_ge(sem("rstd"), 1)
                        for t in range(nt):
                            dve.tensor_scalar(x[:, t, :], x[:, t, :], mv[:, t, 0:1], rs[:, t:t + 1], ALU.subtract, ALU.mult).then_inc(sem("xn"), 1)
                            dve.wait_ge(sem("xn"), t + 1)
                            dve.tensor_tensor(x[:, t, :], x[:, t, :], lg[:, :], ALU.mult).then_inc(sem("xg"), 1)

                    @block.scalar
                    def _(act):
                        act.wait_ge(sem("var"), 1)
                        act.activation(rs[:, 0:nt], rs[:, 0:nt], ACT.Sqrt).then_inc(sem("std"), 1)

                    @block.gpsimd
                    def _(pool):
                        for t in range(nt):
                            pool.wait_ge(sem("xg"), t + 1)
                            pool.tensor_tensor(x[:, t, :], x[:, t, :], lb[:, :], ALU.add)

        def keep_x():
            with stage(nc) as (block, sem):
                @block.sync
                def _(sp):
                    sp.dma_start(x_keep, x[:, :, :]).then_inc(sem("kept"), 16)
                    sp.wait_ge(sem("kept"), 16)

        for l in range(DEPTH):
            last = l == DEPTH - 1
            modulation(l)
            with ExitStack() as sc:
                oc = sb(sc, "oc", [P, CTILES, TOK])
                with ExitStack() as s2:
                    raw = sb(s2, "raw", [P, 15, TOK])
                    kk = sb(s2, "kk", [P, CTILES, TOK])
                    rkd = sb(s2, "rkd", [P, CTILES, TOK])
                    with ExitStack() as s3:
                        h = activation_pair(s3)
                        norm(l, 0, 1, NT, h)
                        keep_x()
                        rwkv_inputs(l, h, raw, kk, rkd, oc, last)
                        project_rest(l, h, last)
                    kf, vf, wd, ad, rf, gd = raw[:, 0:4], raw[:, 4:8], raw[:, 8], raw[:, 9], raw[:, 10:14], raw[:, 14]
                    with ExitStack() as s3:
                        rwkv_scan(l, s3, oc, rkd, kf, vf, wd, ad, rf, kk, last)
                    rwkv_output(l, oc, rkd, vf, gd, last)
                y = sb(sc, "y", [P, KT, TOK])
                with ExitStack() as s2:
                    oa = sb(s2, "oa", [P, HA, TOK])
                    attention(l, oa, last)
                    merge(l, 0, "w_pa", oa, HA, y, last)
                with ExitStack() as s2:
                    of = sb(s2, "of", [P, F_GROUPS, TOK])
                    fourier(l, of, last)
                    merge(l, 1, "w_pf", of, F_GROUPS, y, last)
                merge(l, 2, "w_pc", oc, CTILES, y, last)
                out_proj(l, y, last)
            with ExitStack() as sc:
                hf = sb(sc, "hf", [P, FT, SEQ if last else TOK])
                with ExitStack() as s2:
                    h = activation_pair(s2)
                    norm(l, 3, 4, LT if last else NT, h)
                    ffn(l, hf, h, last)
                ffn_down(l, hf, last)
        with stage(nc) as (block, sem):
            @block.sync
            def _(sp):
                sp.dma_start(out.rearrange("b (t p) d -> p (b t) d", p=P), x[:, 0:LT, :]).then_inc(sem("out"), 16)
                sp.wait_ge(sem("out"), 16)


_INS = ["x", "c", "ctx", "c_ctx", "ada_w", "ada_b", "w_in", "lam_qk", "subln_g", "tshift_mu", "rw_w0", "rw_w2", "rw_a0",
        "rw_a2", "rw_g2", "rw_kk", "rw_ka", "rw_rk", "rw_lnw", "rw_lnb", "w_pa", "w_pf", "w_pc", "w_o", "ln1_g", "ln1_b",
        "ffn_up", "ffn_conv", "ffn_conv_b", "ffn_down", "ln2_g", "ln2_b"]


def kernel(**inputs):
    import numpy as _np
    import concourse.bacc as _bacc
    from concourse import mybir as _mybir
    from concourse.bass_utils import run_bass_kernel_spmd as _run

    nc = _bacc.Bacc("TRN2", target_bir_lowering=False, num_devices=1)
    arrays, aps = {}, {}
    for name, a in [(n, inputs[n]) for n in _INS] + list(tables().items()):
        a = _np.ascontiguousarray(a)
        arrays[f"in_{name}"] = a
        aps[name] = nc.dram_tensor(f"in_{name}", a.shape, _mybir.dt.from_np(a.dtype), kind="ExternalInput").ap()
    out = nc.dram_tensor("out_0", (1, SEQ, D_MODEL), _mybir.dt.float32, kind="ExternalOutput").ap()
    program(nc, aps, out)
    r = _run(nc, [arrays], core_ids=[0])
    return r.results[0]["out_0"]
```

```python
import math
from contextlib import ExitStack, contextmanager

import numpy as np
import concourse.bass as bass
from concourse import mybir

F32 = mybir.dt.float32
I32 = mybir.dt.int32
F32R = mybir.dt.float32r
ALU = mybir.AluOpType
ACT = mybir.ActivationFunctionType
AX = mybir.AxisListType

P = 128
D_MODEL, SEQ, CTX_LEN, DEPTH, GRID_W = 1024, 512, 256, 2, 64
TOK = SEQ + CTX_LEN
KT = D_MODEL // P
LT, CT = SEQ // P, CTX_LEN // P
NT = LT + CT
HA, DH_A, DV = 8, 64, 128
F_GROUPS, F_GROUP_W = 4, 128
D_F = F_GROUPS * F_GROUP_W
HC, HS_C = 8, 64
D_C = HC * HS_C
CTILES = D_C // P
LORA_G = 128
D_CS = 2 * D_C + 4 * 64
D_CO = D_C + LORA_G
D_FF = 2816
FT = D_FF // P
LN_EPS, GN_EPS, HEAD_EPS = 1e-5, HS_C * 1e-5, 1e-5
ALPHA = (2.0 * DEPTH) ** 0.25
DECAY = math.exp(-0.5)
OFF_Q, OFF_K, OFF_V = 0, D_MODEL, 2 * D_MODEL
OFF_F = 3 * D_MODEL
OFF_C = OFF_F + D_F
OFF_G = OFF_C + D_CS + D_CO
C = 64
GCOL = CTILES * P

PA = dict(ada_b=0, mu0=48, mu1=63, w0=78, a0=86, kk=94, ka=98, rk=102, lnw=106, lnb=110, subln=114, end=115)
PB = dict(conv=0, conv_b=3 * FT, c=4 * FT, c_ctx=4 * FT + KT, end=4 * FT + 2 * KT)
R_K, R_V, R_W, R_A, R_R, R_G, R_KK, N_RAW = 0, 4, 8, 9, 10, 14, 15, 19
J_V, J_F, J_G, J_Q, J_K, N_PROJ = 0, 8, 12, 36, 44, 52
FILLERS = (((J_V, OFF_V, 4), (J_F, OFF_F, 2), (J_G, OFF_G, 2)),
           ((J_Q, OFF_Q, 2), (J_K, OFF_K, 2), (J_G + 4, OFF_G + 4 * P, 5)))
LEVELS = (1, 2, 4, 8, 16, 32)
(M_ID, M_LO, M_UP, M_LOI, M_UPI, M_LO1, M_UP1) = range(7)


def tables():
    t = {}
    t["ident"] = np.eye(P, dtype=np.float32)
    blk = np.zeros((P, P), np.float32)
    blk[:64, :64] = blk[64:, 64:] = 1.0
    t["blkones"] = blk
    i = np.arange(C)
    row, col = np.meshgrid(i, i, indexing="ij")
    low = lambda b: (row // b == col // b + 1) & (row // b % 2 == 1)
    m = [row == col, row > col, row < col, row >= col, row <= col, low(1), low(1).T]
    t["masks"] = np.ascontiguousarray(np.concatenate([np.stack(m, 1)] * 2, 0).astype(np.float32))
    lv = [low(b) for b in LEVELS[1:]] + [low(b).T for b in LEVELS[1:]]
    t["lvmasks"] = np.ascontiguousarray(np.concatenate([np.stack(lv, 1)] * 2, 0).astype(np.int32))
    n_freq = DH_A // 4
    inv = (np.float32(10000.0) ** (-np.arange(n_freq, dtype=np.float32) / n_freq)).astype(np.float32)
    tok = np.arange(SEQ)
    pos = np.stack([tok // GRID_W, tok % GRID_W]).astype(np.float32)
    d = np.arange(P) % DH_A
    ang = pos[d // 32] * inv[d % 16][:, None]
    sign = np.where(d % 32 < 16, -1.0, 1.0)[:, None]
    t["rope"] = np.stack([np.cos(ang), np.sin(ang) * sign], 1).astype(np.float32)
    w = np.arange(F_GROUP_W)
    aw = 2 * np.pi * (np.outer(w, w) % F_GROUP_W) / F_GROUP_W
    t["dft_w"] = np.concatenate([np.cos(aw), np.sin(aw)], 1).astype(np.float32)
    for name, n in (("dft_lat", SEQ), ("dft_ctx", CTX_LEN)):
        k = np.arange(n)
        at = 2 * np.pi * (np.outer(k, k) % n) / n
        s = 1.0 / math.sqrt(n * F_GROUP_W)
        both = np.stack([np.cos(at) * s, -np.sin(at) * s])
        t[name] = np.ascontiguousarray(both.reshape(2, n // P, P, n).transpose(2, 0, 1, 3).astype(np.float32))
    return t


@contextmanager
def stage(nc, done=None):
    sems = {}

    def sem(name):
        if name not in sems:
            sems[name] = nc.alloc_semaphore(nc.get_next_instruction_name() + "_" + name)
        return sems[name]

    with nc.Block(no_gpsimd_drain=True) as block:
        yield block, sem
    if sems:
        nc.clear_and_free_semaphores(list(sems.values()))
        nc.all_engine_barrier(sem_only=True)


def bc(ap, n, axis=1):
    v = ap.unsqueeze(axis)
    shape = list(v.shape)
    shape[axis] = n
    return v.to_broadcast(shape)


def program(nc, A, out):
    with ExitStack() as top:
        def sb(scope, name, shape, dt=F32):
            return scope.enter_context(nc.sbuf_tensor(nc.get_next_instruction_name() + "_" + name, shape, dt))

        ps = top.enter_context(nc.psum_tensor("ps", [P, 4096], F32))
        bank = lambda b, n=512, o=0: ps[:, b * 512 + o:b * 512 + o + n]
        x_keep = nc.dram_tensor("x_keep", [P, NT, D_MODEL], F32).ap()
        raw_d = nc.dram_tensor("raw_d", [P, N_RAW, TOK], F32).ap()
        y_d = nc.dram_tensor("y_d", [P, 2, CTILES, TOK], F32).ap()
        rk_d = nc.dram_tensor("rk_d", [P, 2, CTILES, TOK], F32).ap()
        proj_d = nc.dram_tensor("proj_d", [N_PROJ, P, TOK], F32).ap()

        x = sb(top, "x", [P, NT, D_MODEL])
        ident = sb(top, "ident", [P, P])
        ones = sb(top, "ones", [P, P])
        blkones = sb(top, "blkones", [P, P])
        pa = [sb(top, f"pa{l}", [P, PA["end"]]) for l in range(DEPTH)]
        pb = [sb(top, f"pb{l}", [P, PB["end"]]) for l in range(DEPTH)]
        mu_own = [sb(top, f"mu_own{l}", [P, 15]) for l in range(DEPTH)]
        nlam = [sb(top, f"nlam{l}", [P, 1]) for l in range(DEPTH)]
        subln = [sb(top, f"subln{l}", [P, 1]) for l in range(DEPTH)]
        mod = sb(top, "mod", [P, 48, 2])

        with ExitStack() as sc, stage(nc) as (block, sem):
            rows = [sb(sc, f"rows{i}", [P, P]) for i in range(2 * DEPTH)]
            lqk = sb(sc, "lqk", [P, DEPTH, 4, 64])
            lpr = sb(sc, "lpr", [P, DEPTH, 2, 64])
            ldot = sb(sc, "ldot", [P, DEPTH, 2])
            lexp = sb(sc, "lexp", [P, DEPTH, 2])
            row_src = []
            for l in range(DEPTH):
                ra, rb = rows[2 * l], rows[2 * l + 1]
                r = lambda ap: ap.rearrange("(t p) -> t p", p=P)
                r2 = lambda ap: ap.rearrange("a (t p) -> (a t) p", p=P)
                row_src += [
                    (ra, PA["ada_b"], 48, r(A["ada_b"][l])), (ra, PA["mu0"], 30, r2(A["tshift_mu"][l])),
                    (ra, PA["w0"], 8, r2(A["rw_w0"][l])), (ra, PA["a0"], 8, r2(A["rw_a0"][l])),
                    (ra, PA["kk"], 4, r(A["rw_kk"][l])), (ra, PA["ka"], 4, r(A["rw_ka"][l])),
                    (ra, PA["rk"], 4, A["rw_rk"][l].rearrange("(t a) k -> t (a k)", a=2)),
                    (ra, PA["lnw"], 4, r(A["rw_lnw"][l])), (ra, PA["lnb"], 4, r(A["rw_lnb"][l])),
                    (ra, PA["subln"], 1, r(A["subln_g"][l])),
                    (rb, PB["conv"], 3 * FT, r2(A["ffn_conv"][l])), (rb, PB["conv_b"], FT, r(A["ffn_conv_b"][l])),
                    (rb, PB["c"], KT, r2(A["c"])), (rb, PB["c_ctx"], KT, r(A["c_ctx"])),
                ]

            @block.sync
            def _(sp):
                for dst, at, n, src in row_src:
                    sp.dma_start(dst[at:at + n, :], src).then_inc(sem("rows_in"), 16)
                sp.dma_start(x[:, 0:LT, :], A["x"].rearrange("b (t p) d -> p (b t) d", p=P)).then_inc(sem("x_in"), 16)
                sp.dma_start(x[:, LT:NT, :], A["ctx"].rearrange("b (t p) d -> p (b t) d", p=P)).then_inc(sem("x_in"), 16)
                sp.wait_ge(sem("x_in"), 32)

            @block.scalar
            def _(act):
                act.dma_start(ident[:, :], A["ident"]).then_inc(sem("const_in"), 16)
                act.dma_start(blkones[:, :], A["blkones"]).then_inc(sem("const_in"), 16)
                act.dma_start(lqk[:, :, :, :], A["lam_qk"].partition_broadcast(P)).then_inc(sem("const_in"), 16)
                act.wait_ge(sem("dots"), 1)
                act.activation(lexp[:, :, :], ldot[:, :, :], ACT.Exp).then_inc(sem("lexp"), 1)

            @block.tensor
            def _(pe):
                pe.wait_ge(sem("rows_in"), 16 * len(row_src))
                pe.wait_ge(sem("const_in"), 48)
                for i, src in enumerate(rows):
                    n = (PA, PB)[i % 2]["end"]
                    pe.transpose(bank(i, n), src[0:n, :], ident[0:n, 0:n]).then_inc(sem("columns"), 1)

            @block.gpsimd
            def _(pool):
                pool.memset(ones[:, :], 1.0)

            @block.vector
            def _(dve):
                dve.wait_ge(sem("const_in"), 48)
                dve.tensor_tensor(lpr[:, :, :, :], lqk[:, :, 0:4:2, :], lqk[:, :, 1:4:2, :], ALU.mult).then_inc(sem("dve"), 1)
                dve.wait_ge(sem("dve"), 1)
                dve.reduce_sum(ldot[:, :, :], lpr[:, :, :, :], AX.X).then_inc(sem("dots"), 1)
                for i in range(2 * DEPTH):
                    dst, n = (pa, pb)[i % 2][i // 2], (PA, PB)[i % 2]["end"]
                    dve.wait_ge(sem("columns"), i + 1)
                    dve.tensor_copy(dst[:, :], bank(i, n)).then_inc(sem("dve"), 1)
                dve.wait_ge(sem("dve"), 1 + 2 * DEPTH)
                dve.wait_ge(sem("lexp"), 1)
                for l in range(DEPTH):
                    lam_init = 0.8 - 0.6 * math.exp(-0.3 * l)
                    a = pa[l]
                    dve.tensor_scalar(subln[l][:, :], a[:, PA["subln"]:PA["subln"] + 1], 1.0 - lam_init, None, ALU.mult)
                    dve.tensor_tensor(nlam[l][:, :], lexp[:, l, 1:2], lexp[:, l, 0:1], ALU.subtract).then_inc(sem("half"), 1)
                    dve.tensor_tensor(mu_own[l][:, :], a[:, PA["mu0"]:PA["mu0"] + 15], a[:, PA["mu1"]:PA["mu1"] + 15],
                                      ALU.add).then_inc(sem("half"), 1)
                    dve.wait_ge(sem("half"), 2 * l + 2)
                    dve.tensor_scalar(nlam[l][:, :], nlam[l][:, :], -lam_init, None, ALU.add)
                    dve.tensor_scalar(mu_own[l][:, :], mu_own[l][:, :], -1.0, 1.0, ALU.mult, ALU.add)

        def modulation(l):
            with ExitStack() as sc, stage(nc) as (block, sem):
                NC, SL = 12, 4
                w = sb(sc, "ada_w", [P, SL, KT, 512])
                sg = sb(sc, "sig_c", [P, 2, KT])
                cc = sb(sc, "silu_c", [P, KT, 2])
                row = sb(sc, "mod_row", [2, NC, 512])
                raw = pb[l][:, PB["c"]:PB["end"]].rearrange("p (s k) -> p s k", s=2)
                src = A["ada_w"][l].rearrange("(k p) n -> p k n", p=P)

                @block.sync
                def _(sp):
                    for n in range(NC):
                        if n >= SL:
                            sp.wait_ge(sem("w_used"), n - SL + 1)
                        sp.dma_start(w[:, n % SL, :, :], src[:, :, n * 512:(n + 1) * 512]).then_inc(sem(f"w_in{n % SL}"), 16)

                @block.scalar
                def _(act):
                    act.activation(sg[:, :, :], raw, ACT.Sigmoid).then_inc(sem("sig"), 1)
                    for n in range(NC):
                        act.wait_ge(sem("w_used"), n + 1)
                        act.activation(row[:, n, :], ps[0:2, (n % 4) * 512:(n % 4 + 1) * 512], ACT.Copy).then_inc(sem("row"), 1)

                @block.vector
                def _(dve):
                    dve.wait_ge(sem("sig"), 1)
                    dve.tensor_tensor(cc[:, :, :].rearrange("p k s -> p s k"), raw, sg[:, :, :], ALU.mult).then_inc(sem("silu"), 1)
                    dve.wait_ge(sem("column"), 1)
                    b = pa[l][:, PA["ada_b"]:PA["ada_b"] + 48]
                    dve.tensor_tensor(mod[:, :, :], bank(4, 96).rearrange("p (n s) -> p n s", s=2),
                                      bc(b, 2, 2), ALU.add).then_inc(sem("mod"), 1)
                    dve.wait_ge(sem("mod"), 1)
                    for i in (1, 4):
                        dve.tensor_scalar(mod[:, 8 * i:8 * i + 8, :], mod[:, 8 * i:8 * i + 8, :], 1.0, None, ALU.add)

                @block.tensor
                def _(pe):
                    pe.wait_ge(sem("silu"), 1)
                    for n in range(NC):
                        pe.wait_ge(sem(f"w_in{n % SL}"), 16 * (n // SL + 1))
                        if n >= 4:
                            pe.wait_ge(sem("row"), n - 3)
                        for k in range(KT):
                            m = pe.matmul(ps[0:2, (n % 4) * 512:(n % 4 + 1) * 512], cc[:, k, :], w[:, n % SL, k, :],
                                          start=k == 0, stop=k == KT - 1)
                        m.then_inc(sem("w_used"), 1)
                    pe.wait_ge(sem("row"), NC)
                    for n in range(48):
                        m = pe.transpose(bank(4, 2, 2 * n), row[:, n // 4, (n % 4) * P:(n % 4 + 1) * P], ident[0:2, 0:2])
                    m.then_inc(sem("column"), 1)

        def norm(l, i_shift, i_scale, nt, h):
            lat, ctx = LT, nt - LT
            n_tok = nt * P
            with ExitStack() as sc, stage(nc) as (block, sem):
                xn = sb(sc, "xn", [P, NT, D_MODEL])
                hf = sb(sc, "h_f32", [P, 3, TOK])
                st = sb(sc, "stats", [P, NT, 2, 6])
                mv = sb(sc, "mean_var", [P, NT, 2])
                rs = sb(sc, "rstd", [P, NT])
                sh = lambda j, s: mod[:, 8 * i_shift + j, s:s + 1]
                sl = lambda j, s: mod[:, 8 * i_scale + j, s:s + 1]

                @block.vector
                def _(dve):
                    for t in range(nt):
                        for f in range(2):
                            i = dve.bn_stats(st[:, t, f, :], x[:, t, f * 512:(f + 1) * 512])
                        i.then_inc(sem("stats"), 1)
                    for t in range(nt):
                        dve.wait_ge(sem("stats"), t + 1)
                        i = dve.bn_aggr(mv[:, t, :], st[:, t, :, :])
                    i.then_inc(sem("mv"), 1)
                    dve.wait_ge(sem("mv"), 1)
                    dve.tensor_scalar(rs[:, 0:nt], mv[:, 0:nt, 1], LN_EPS, None, ALU.add).then_inc(sem("var"), 1)
                    dve.wait_ge(sem("std"), 1)
                    dve.reciprocal(rs[:, 0:nt], rs[:, 0:nt]).then_inc(sem("rstd"), 1)
                    dve.wait_ge(sem("rstd"), 1)
                    for t in range(nt):
                        dve.tensor_scalar(xn[:, t, :], x[:, t, :], mv[:, t, 0:1], rs[:, t:t + 1],
                                          ALU.subtract, ALU.mult).then_inc(sem("xn"), 1)
                    for j in range(KT):
                        dve.wait_ge(sem("hi"), j + 1)
                        dve.tensor_tensor(h[1][:, j, 0:n_tok], hf[:, j % 3, 0:n_tok], h[0][:, j, 0:n_tok].bitcast(F32),
                                          ALU.subtract).then_inc(sem("lo"), 1)

                @block.tensor
                def _(pe):
                    pe.wait_ge(sem("xn"), nt)
                    for j in range(KT):
                        if j >= 4:
                            pe.wait_ge(sem("h"), j - 3)
                        for t in range(nt):
                            m = pe.transpose(bank(2 * (j % 4), P, t * P), xn[:, t, j * P:(j + 1) * P], ident[:, :])
                        m.then_inc(sem("T"), 1)

                @block.scalar
                def _(act):
                    act.wait_ge(sem("var"), 1)
                    act.activation(rs[:, 0:nt], rs[:, 0:nt], ACT.Sqrt).then_inc(sem("std"), 1)
                    for j in range(KT):
                        act.wait_ge(sem("T"), j + 1)
                        if j >= 3:
                            act.wait_ge(sem("lo"), j - 2)
                        for s, (at, n) in enumerate(BOTH if ctx else LAT):
                            m = act.activation(hf[:, j % 3, at:at + n], bank(2 * (j % 4), n, at), ACT.Identity, bias=sh(j, s), scale=sl(j, s))
                        m.then_inc(sem("h"), 1)

                @block.gpsimd
                def _(pool):
                    for j in range(KT):
                        pool.wait_ge(sem("h"), j + 1)
                        pool.tensor_copy(h[0][:, j, 0:n_tok], hf[:, j % 3, 0:n_tok]).then_inc(sem("hi"), 1)

        def weight_rings(sc, n_raw, n_split):
            return (sb(sc, "w_raw", [P, n_raw, KT, P]), sb(sc, "w_hi", [P, n_split, KT, P], F32R),
                    sb(sc, "w_lo", [P, n_split, KT, P], F32R))

        def activation_pair(sc):
            return sb(sc, "h_hi", [P, KT, TOK], F32R), sb(sc, "h_lo", [P, KT, TOK], F32R)

        def load_weights(sp, sem, rings, n, src):
            n_raw = rings[0].shape[1]
            if n >= n_raw:
                sp.wait_ge(sem("w_lo"), n - n_raw + 1)
            sp.dma_start(rings[0][:, n % n_raw, 0:src.shape[1], :], src).then_inc(sem(f"w_in{n % n_raw}"), 16)

        def split_hi(act, sem, rings, n, kt=KT):
            n_raw, n_split = rings[0].shape[1], rings[1].shape[1]
            act.wait_ge(sem(f"w_in{n % n_raw}"), 16 * (n // n_raw + 1))
            if n >= n_split:
                act.wait_ge(sem("w_used"), n - n_split + 1)
            act.activation(rings[1][:, n % n_split, 0:kt, :], rings[0][:, n % n_raw, 0:kt, :], ACT.Copy).then_inc(sem("w_hi"), 1)

        def split_lo(eng, sem, rings, n, kt=KT):
            n_raw, n_split = rings[0].shape[1], rings[1].shape[1]
            eng.wait_ge(sem("w_hi"), n + 1)
            eng.tensor_tensor(rings[2][:, n % n_split, 0:kt, :], rings[0][:, n % n_raw, 0:kt, :],
                              rings[1][:, n % n_split, 0:kt, :].bitcast(F32), ALU.subtract).then_inc(sem("w_lo"), 1)

        def fm_product(pe, dst, w, a, ks, kt, widths):
            for k in ks:
                for i, (wi, ai) in enumerate(((0, 0), (0, 1), (1, 0))):
                    for at, n in widths:
                        m = pe.matmul(dst[:, at:at + n], w[wi][:, k, :], a[ai][:, k, at:at + n],
                                      start=k == 0 and i == 0, stop=k == kt - 1 and i == 2)
            return m

        def slot(rings, n):
            n_split = rings[1].shape[1]
            return rings[1][:, n % n_split], rings[2][:, n % n_split]

        BOTH = ((0, SEQ), (SEQ, CTX_LEN))
        LAT = ((0, SEQ),)

        def rwkv_inputs(l, h, last):
            with ExitStack() as s2, stage(nc) as (block, sem):
                raw = sb(s2, "raw", [P, R_KK, TOK])
                kk = sb(s2, "kk", [P, CTILES, TOK])
                kf, wd, gd = raw[:, R_K:R_V], raw[:, R_W], raw[:, R_G]
                rings = weight_rings(s2, 3, 2)
                sq = sb(s2, "sq", [P, TOK])
                nrm = sb(s2, "nrm", [P, 2, TOK])
                src = A["w_in"][l].rearrange("(k p) n -> p k n", p=P)
                p_of = lambda t: ps[:, (t % 4) * 1024:(t % 4) * 1024 + TOK]
                seqs = lambda t: LAT if (last and t >= 10) else BOTH
                col = lambda name, t: pa[l][:, PA[name] + t:PA[name] + t + 1]

                @block.sync
                def _(sp):
                    def store(t):
                        if t not in (R_W, R_G):
                            n = sum(w for _, w in seqs(t))
                            sp.wait_ge(sem("shifted"), t + 1)
                            sp.dma_start(raw_d[:, t, 0:n], raw[:, t, 0:n]).then_inc(sem("raw_out"), 16)
                    for t in range(15):
                        load_weights(sp, sem, rings, t, src[:, :, OFF_C + t * P:OFF_C + (t + 1) * P])
                        if t >= 3:
                            store(t - 3)
                        if t == 5:
                            sp.dma_start(x_keep, x[:, :, :]).then_inc(sem("kept"), 16)
                    for t in (12, 13):
                        store(t)
                    sp.wait_ge(sem("lora_act"), 2)
                    for t in (R_W, R_G):
                        n = sum(w for _, w in seqs(t))
                        sp.dma_start(raw_d[:, t, 0:n], raw[:, t, 0:n]).then_inc(sem("raw_out"), 16)
                    for t in range(CTILES):
                        sp.wait_ge(sem("kk_done"), t + 1)
                        sp.dma_start(raw_d[:, R_KK + t, :], kk[:, t, :]).then_inc(sem("raw_out"), 16)
                    sp.wait_ge(sem("raw_out"), 16 * N_RAW)
                    sp.wait_ge(sem("kept"), 16)

                @block.tensor
                def _(pe):
                    for t in range(15):
                        pe.wait_ge(sem("w_lo"), t + 1)
                        if t >= 4:
                            pe.wait_ge(sem("shifted"), t - 3)
                        fm_product(pe, p_of(t), slot(rings, t), h, range(KT), KT, seqs(t)).then_inc(sem("w_used"), 1)
                    for t in range(CTILES):
                        pe.wait_ge(sem("kk_sq"), t + 1)
                        if t == 0:
                            pe.wait_ge(sem("shifted"), 15)
                        elif t >= 2:
                            pe.wait_ge(sem("norm"), t - 1)
                        for at, n in BOTH:
                            m = pe.matmul(p_of(t % 2)[:, at:at + n], blkones[:, :], sq[:, at:at + n], start=True, stop=True)
                        m.then_inc(sem("kk_ss"), 1)

                @block.scalar
                def _(act):
                    split_hi(act, sem, rings, 0)
                    for t in range(15):
                        if t + 1 < 15:
                            split_hi(act, sem, rings, t + 1)
                        act.wait_ge(sem("w_used"), t + 1)
                        n = sum(w for _, w in seqs(t))
                        act.activation(raw[:, t, 0:n], p_of(t)[:, 0:n], ACT.Copy, scale=mu_own[l][:, t:t + 1]).then_inc(sem("own"), 1)
                    act.wait_ge(sem("shifted"), 15)
                    act.activation(wd, wd, ACT.Tanh).then_inc(sem("lora_act"), 1)
                    act.activation(gd[:, 0:n], gd[:, 0:n], ACT.Sigmoid).then_inc(sem("lora_act"), 1)
                    for t in range(CTILES):
                        act.wait_ge(sem("kk_raw"), t + 1)
                        if t:
                            act.wait_ge(sem("kk_ss"), t)
                        act.activation(sq[:, :], kk[:, t, :], ACT.Square).then_inc(sem("kk_sq"), 1)
                        act.wait_ge(sem("kk_ss"), t + 1)
                        if t >= 2:
                            act.wait_ge(sem("kk_done"), t - 1)
                        act.activation(nrm[:, t % 2, :], p_of(t % 2), ACT.Sqrt).then_inc(sem("norm"), 1)

                @block.gpsimd
                def _(pool):
                    for t in range(15):
                        split_lo(pool, sem, rings, t)

                @block.vector
                def _(dve):
                    for t in range(15):
                        dve.wait_ge(sem("own"), t + 1)
                        for i, (at, n) in enumerate(seqs(t)):
                            o, p = raw[:, t, at:at + n], p_of(t)[:, at:at + n]
                            dve.scalar_tensor_tensor(o[:, 1:n], p[:, 0:n - 1], pa[l][:, PA["mu0"] + t:PA["mu0"] + t + 1],
                                                     o[:, 1:n], ALU.mult, ALU.add).then_inc(sem(f"prev{i}"), 1)
                        for i, (at, n) in enumerate(seqs(t)):
                            o, p = raw[:, t, at:at + n], p_of(t)[:, at:at + n]
                            dve.wait_ge(sem(f"prev{i}"), t + 1)
                            m = dve.scalar_tensor_tensor(o[:, 0:n - 1], p[:, 1:n], pa[l][:, PA["mu1"] + t:PA["mu1"] + t + 1],
                                                         o[:, 0:n - 1], ALU.mult, ALU.add)
                        m.then_inc(sem("shifted"), 1)
                    dve.wait_ge(sem("shifted"), 15)
                    for t in range(CTILES):
                        dve.tensor_scalar(kk[:, t, :], kf[:, t, :], col("kk", t), None, ALU.mult).then_inc(sem("kk_raw"), 1)
                    for t in range(CTILES):
                        n = nrm[:, t % 2, :]
                        dve.wait_ge(sem("norm"), t + 1)
                        dve.tensor_scalar(n, n, 1e-12, None, ALU.max).then_inc(sem("kk_n"), 1)
                        dve.wait_ge(sem("kk_n"), 2 * t + 1)
                        dve.reciprocal(n, n).then_inc(sem("kk_n"), 1)
                        dve.wait_ge(sem("kk_n"), 2 * t + 2)
                        dve.tensor_tensor(kk[:, t, :], kk[:, t, :], n, ALU.mult).then_inc(sem("kk_done"), 1)

        def rwkv_scan(l, s2, h, last):
            G = [P, GCOL]
            two = lambda name: [sb(s2, f"{name}{d}", G) for d in range(2)]
            masks = sb(s2, "masks", [P, 7, C])
            lvm = sb(s2, "lvmasks", [P, 10, C], I32)
            reset = sb(s2, "reset", [P, 2, GCOL])
            w2 = sb(s2, "w2", [P, 2, D_C])
            a2 = sb(s2, "a2", [P, 2, D_C])
            S = [sb(s2, f"S{i}", G) for i in range(3)]
            PC = sb(s2, "PC", [P, 2, 2, CTILES])
            W1T, Btm, Ktm, Vtm, QB, QK = (two(n) for n in ("W1T", "Btm", "Ktm", "Vtm", "QB", "QK"))
            spare = x[:, :, :].rearrange("p t d -> p (t d)")
            Kttm, NAT, T, TT, Y, MT = ([spare[:, (2 * i + d) * GCOL:(2 * i + d + 1) * GCOL] for d in range(2)] for i in range(6))
            MV, U, W2s = Y, T, NAT
            sg, Lr, EN, a, Bh, Bp = (two(n) for n in ("sg", "Lr", "EN", "a", "Bh", "Bp"))
            L, Lx = sb(s2, "L", G), sb(s2, "Lx", G)
            g3 = lambda ap: ap.rearrange("p (t c) -> p t c", t=CTILES)
            g8 = lambda ap: ap.rearrange("p (g c) -> p g c", c=C)
            kI, vI, rI, kkI = (two(n) for n in ("k_in", "v_in", "r_in", "kk_in"))
            kd, Kt, Rt = kI, kkI, rI
            loraI = sb(s2, "lora_in", [P, 2, 2, P])
            rings = weight_rings(s2, 3, 2)
            res = sb(s2, "result", [P, 2, TOK])
            w_src = A["w_in"][l].rearrange("(k p) n -> p k n", p=P)
            cols = lambda name, d: pa[l][:, PA[name] + 4 * d:PA[name] + 4 * d + 4]

            with stage(nc) as (block, sem):
                @block.sync
                def _(sp):
                    sp.dma_start(masks[:, :, :], A["masks"]).then_inc(sem("in"), 16)
                    sp.dma_start(lvm[:, :, :], A["lvmasks"]).then_inc(sem("in"), 16)
                    sp.wait_ge(sem("zero"), 1)
                    for d in range(2):
                        sp.dma_start(w2[64 * d:64 * d + 64, d, :], A["rw_w2"][l, d]).then_inc(sem("in"), 16)
                        sp.dma_start(a2[64 * d:64 * d + 64, d, :], A["rw_a2"][l, d]).then_inc(sem("in"), 16)
                    sp.wait_ge(sem("in"), 96)

                @block.gpsimd
                def _(pool):
                    pool.memset(w2[:, :, :], 0.0)
                    pool.memset(a2[:, :, :], 0.0).then_inc(sem("zero"), 1)
                    pool.memset(S[0][:, :], 0.0)

                @block.vector
                def _(dve):
                    dve.memset(reset[:, :, :], 1.0).then_inc(sem("one"), 1)
                    dve.wait_ge(sem("one"), 1)
                    dve.memset(g8(reset[:, 0, :])[:, :, 0:1], 0.0)
                    dve.memset(g8(reset[:, 1, :])[:, :, C - 1:C], 0.0)

            def groups(base, n, want_y, fillers):
                slots = [(j + i, c + i * P, per, LAT if last and j not in (J_V, J_K) else BOTH)
                         for j, c, per in fillers for i in range(per)]
                pieces = [(s, w) for s, (_, _, _, widths) in enumerate(slots) for w in widths]
                ends = [sum(p <= s for p, _ in pieces) for s in range(len(slots))]
                parts = []
                for i, (s, w) in enumerate(pieces):
                    parts += [(i, s, w, range(0, 4)), (i, s, w, range(4, 8))] if w == BOTH[0] else [(i, s, w, range(8))]
                lv = 3 if len(parts) > 22 else 2
                counts = [("z", 3), ("prod0", 2), ("prod1", 1)] + [(f"level{n}", lv) for n in range(5)]
                counts += [(p, 1) for p in ("W2", "U0", "S0", "U1", "YR0")] + [("end", len(parts))]
                span, first = {}, 0
                for p, n_parts in counts:
                    span[p] = (first, min(first + n_parts, len(parts)))
                    first = span[p][1]
                n_fm, n_pr = (6, 5) if want_y else (5, 3)
                with nc.Fori(0, n) as g, stage(nc) as (block, sem):
                    at = (base + g * P, base + (n - 1) * P - g * P)
                    raw_of = lambda r, d: raw_d[:, r:r + CTILES, bass.ds(at[d], P)]
                    chunk_of = lambda d, q: q if d == 0 else 1 - q
                    HT = [(hh, t) for t in range(CTILES) for hh in range(2)]
                    hc = lambda hh, t: (hh * CTILES + t) * C
                    tc = lambda t, i: t * P + i * C
                    rows = lambda i: slice(64 * i, 64 * i + 64)

                    @block.sync
                    def _(sp):
                        def load(s):
                            _, c, per, _ = slots[s]
                            load_weights(sp, sem, rings, s, w_src[:, :, bass.ds(g * (per * P) + c, P)])
                        def load_in(d, name, dst, src):
                            sp.dma_start(dst, src).then_inc(sem(f"{name}{d}"), 16)
                        for d in range(2):
                            load_in(d, "lora", loraI[:, d, :, :], raw_d[:, R_W:R_A + 1, bass.ds(at[d], P)])
                        for d in range(2):
                            load_in(d, "k", g3(kI[d][:, :]), raw_of(R_K, d))
                            load_in(d, "kk", g3(kkI[d][:, :]), raw_of(R_KK, d))
                            load(d)
                            if want_y:
                                load_in(d, "r", g3(rI[d][:, :]), raw_of(R_R, d))
                            load_in(d, "v", g3(vI[d][:, :]), raw_of(R_V, d))
                        load(2)
                        for s, (j, _, per, widths) in enumerate(slots):
                            if s + 3 < len(slots):
                                load(s + 3)
                            w = sum(w for _, w in widths)
                            sp.wait_ge(sem("result"), ends[s])
                            sp.dma_start(proj_d[bass.ds(g * per + j, 1), :, 0:w].rearrange("j p n -> p (j n)"),
                                         res[:, s % 2, 0:w]).then_inc(sem(f"stored{s % 2}"), 16)
                        if want_y:
                            for d in range(2):
                                sp.wait_ge(sem("Ysum"), d + 1)
                                sp.dma_start(y_d[:, d, :, bass.ds(at[d], P)], g3(sg[d][:, :])).then_inc(sem("y_out"), 16)
                            sp.wait_ge(sem("y_out"), 32)
                            for d in range(2):
                                sp.wait_ge(sem(f"rk_out{d}"), 16)
                        for s in range(len(slots) - 2, len(slots)):
                            sp.wait_ge(sem(f"stored{s % 2}"), 16 * (s // 2 + 1))

                    @block.gpsimd
                    def _(pool):
                        def split(s):
                            pool.wait_ge(sem(f"w_in{s % 3}"), 16 * (s // 3 + 1))
                            pool.tensor_copy(rings[1][:, s % 2, :, :], rings[0][:, s % 3, :, :]).then_inc(sem("w_hi"), 1)
                            split_lo(pool, sem, rings, s)
                        split(0)
                        split(1)
                        for s in range(2, len(slots)):
                            pool.wait_ge(sem("piece"), ends[s - 2])
                            split(s)

                    @block.tensor
                    def _(pe):
                        def fill(point, i0=0, n=None):
                            a0, a1 = span[point]
                            for i, s, (c0, n_c), ks in parts[a0 + i0:a1 if n is None else min(a0 + i0 + n, a1)]:
                                if ks[0] == 0:
                                    pe.wait_ge(sem("w_lo"), s + 1)
                                    if i >= 2:
                                        pe.wait_ge(sem("result"), i - 1)
                                whi, wlo = slot(rings, s)
                                for k in ks:
                                    for v, (w, hv) in enumerate(((whi, h[0]), (whi, h[1]), (wlo, h[0]))):
                                        m = pe.matmul(bank(6 + i % 2, n_c), w[:, k, :], hv[:, k, c0:c0 + n_c],
                                                      start=k == 0 and v == 0, stop=k == KT - 1 and v == 2)
                                if ks[-1] == KT - 1:
                                    m.then_inc(sem("piece"), 1)

                        for d in range(2):
                            pe.wait_ge(sem(f"lora{d}"), 16)
                            for i, w in enumerate((w2, a2)):
                                for t in range(CTILES):
                                    m = pe.matmul(bank((4, 0)[d] + i, P, t * P), w[:, d, t * P:(t + 1) * P], loraI[:, d, i, :],
                                                  start=True, stop=True)
                            m.then_inc(sem("z"), 1)
                        fill("z")
                        for d in range(2):
                            pe.wait_ge(sem("fm"), n_fm * (d + 1))
                            if d:
                                pe.wait_ge(sem("tm"), 4 * d)
                            else:
                                pe.wait_ge(sem("sig"), 2)

                            def product(b, o, stat, mov):
                                for t in range(CTILES):
                                    for i in range(2):
                                        for hh in range(2):
                                            m = pe.matmul(ps[rows(i), (b + hh) * 512 + o + t * C:(b + hh) * 512 + o + (t + 1) * C],
                                                          stat[rows(hh), tc(t, i):tc(t, i) + C], mov[rows(hh), tc(t, i):tc(t, i) + C],
                                                          start=True, stop=True)
                                m.then_inc(sem("pmm"), 1)
                            product(0, 0, Bh[d], Kt[d])
                            product(0, 256, Kt[d], Bh[d])
                            product(2, 0, EN[d], Kt[d])
                            if want_y:
                                product(2, 256, Bh[d], Rt[d])
                                if d:
                                    pe.wait_ge(sem("prod"), n_pr * d)
                                product(4, 0, EN[d], Rt[d])
                            fill(f"prod{d}")
                            pe.wait_ge(sem(f"v{d}"), 16)
                            pe.wait_ge(sem("prod"), n_pr * (d + 1))
                            for b, src in ((0, Kt[d]), (1, Bp[d]), (2, Lr[d]), (3, vI[d])):
                                for t in range(CTILES):
                                    m = pe.transpose(bank(b, P, t * P), src[:, t * P:(t + 1) * P], ident[:, :])
                                m.then_inc(sem("tmm"), 1)
                        def diag(b, stat, mov, name):
                            for hh, t in HT:
                                for i in range(2):
                                    c0 = hc(hh, t)
                                    m = pe.matmul(ps[rows(i), b * 512 + c0:b * 512 + c0 + C], stat[rows(i), c0:c0 + C],
                                                  mov[rows(i), c0:c0 + C], start=True, stop=True)
                            m.then_inc(sem(name), 1)
                        pe.wait_ge(sem("tm"), 8)
                        for n_lv in range(5):
                            for d in range(2):
                                pe.wait_ge(sem(f"T{d}"), n_lv + 1)
                                diag(4 + d, NAT[d], T[d], f"Ymm{d}")
                            fill(f"level{n_lv}", 0, lv - 2)
                            for d in range(2):
                                pe.wait_ge(sem(f"Y{d}"), n_lv + 1)
                                if n_lv < 4:
                                    diag(0 + d, TT[d], Y[d], f"off{d}")
                                diag(2 + d, Y[d], TT[d], f"offT{d}")
                                fill(f"level{n_lv}", lv - 2 + d, 1)
                        for d in range(2):
                            for hh, t in HT:
                                for i in range(2):
                                    m = pe.matmul(ps[rows(i), d * 512 + hc(hh, t):d * 512 + hc(hh, t) + C],
                                                  MT[d][rows(i), hc(hh, t):hc(hh, t) + C],
                                                  Vtm[d][rows(i), tc(t, hh):tc(t, hh) + C], start=True, stop=True)
                            m.then_inc(sem("MVmm"), 1)
                        for d in range(2):
                            pe.wait_ge(sem(f"T{d}"), 6)
                        for d in range(2):
                            if d:
                                pe.wait_ge(sem("W1"), d)
                            for t in range(CTILES):
                                for i in range(2):
                                    for hh in range(2):
                                        m = pe.matmul(ps[rows(hh), (2 + i) * 512 + t * C:(2 + i) * 512 + (t + 1) * C],
                                                      Kttm[d][rows(i), tc(t, hh):tc(t, hh) + C],
                                                      TT[d][rows(i), hc(hh, t):hc(hh, t) + C], start=True, stop=True)
                            m.then_inc(sem("W1mm"), 1)
                        for d in range(2):
                            pe.wait_ge(sem("MV"), d + 1)
                            diag(4 + d, TT[d], MV[d], "W2mm")
                        fill("W2")
                        for q in range(2):
                            if q == 0:
                                pe.wait_ge(sem("W1"), 2)
                                pe.wait_ge(sem("W2"), 4)
                            else:
                                pe.wait_ge(sem("S"), 1)
                            for t in range(CTILES):
                                for d in range(2):
                                    i = chunk_of(d, q)
                                    for hh in range(2):
                                        m = pe.matmul(ps[rows(i), hh * 512 + t * C:hh * 512 + (t + 1) * C],
                                                      W1T[d][rows(hh), tc(t, i):tc(t, i) + C],
                                                      S[q][rows(hh), (d * CTILES + t) * C:(d * CTILES + t + 1) * C], start=True, stop=True)
                            m.then_inc(sem("Umm"), 1)
                            fill(f"U{q}")
                            pe.wait_ge(sem("U"), q + 1)
                            for t in range(CTILES):
                                for d in range(2):
                                    i = chunk_of(d, q)
                                    for hh in range(2):
                                        o = ps[rows(hh), (2 + d) * 512 + t * C:(2 + d) * 512 + (t + 1) * C]
                                        pe.matmul(o, Btm[d][rows(i), tc(t, hh):tc(t, hh) + C],
                                                  U[q][rows(i), hc(hh, t):hc(hh, t) + C], start=True, stop=False)
                                        m = pe.matmul(o, Ktm[d][rows(i), tc(t, hh):tc(t, hh) + C],
                                                      Vtm[d][rows(i), tc(t, hh):tc(t, hh) + C], start=False, stop=True)
                            m.then_inc(sem("Smm"), 1)
                            if q == 0:
                                fill("S0")
                        if want_y:
                            for d in range(2):
                                for t in range(CTILES):
                                    for i in range(2):
                                        q = chunk_of(d, i)
                                        for hh in range(2):
                                            m = pe.matmul(ps[rows(hh), (4 + d) * 512 + tc(t, i):(4 + d) * 512 + tc(t, i) + C],
                                                          S[q][rows(hh), (d * CTILES + t) * C:(d * CTILES + t + 1) * C],
                                                          Rt[d][rows(hh), tc(t, i):tc(t, i) + C], start=True, stop=True)
                                m.then_inc(sem("YRmm"), 1)
                                if d == 0:
                                    fill("YR0")
                                if d:
                                    pe.wait_ge(sem("S"), 2)
                                for t in range(CTILES):
                                    for i in range(2):
                                        q = chunk_of(d, i)
                                        for hh in range(2):
                                            o = ps[rows(hh), (2 * d + i) * 512 + t * C:(2 * d + i) * 512 + (t + 1) * C]
                                            c0 = hc(hh, t)
                                            pe.matmul(o, U[q][rows(i), c0:c0 + C], QB[d][rows(i), c0:c0 + C], start=True, stop=False)
                                            m = pe.matmul(o, Vtm[d][rows(i), tc(t, hh):tc(t, hh) + C],
                                                          QK[d][rows(i), c0:c0 + C], start=False, stop=True)
                                m.then_inc(sem("YUmm"), 1)
                        if not want_y:
                            fill("YR0")
                        fill("end")

                    @block.scalar
                    def _(act):
                        def copy_pieces(*points):
                            for p in points:
                                for i, s, (c0, n_c), ks in parts[span[p][0]:span[p][1]]:
                                    if ks[-1] == KT - 1:
                                        if s >= 2:
                                            act.wait_ge(sem(f"stored{s % 2}"), 16 * (s // 2))
                                        act.wait_ge(sem("piece"), i + 1)
                                        act.activation(res[:, s % 2, c0:c0 + n_c], bank(6 + i % 2, n_c), ACT.Copy).then_inc(sem("result"), 1)

                        for d in range(2):
                            act.wait_ge(sem("z"), d + 1)
                            for b, name, dst in (((4, 0)[d], "w0", sg), ((5, 1)[d], "a0", a)):
                                for t in range(CTILES):
                                    m = act.activation(dst[d][:, t * P:(t + 1) * P], bank(b, P, t * P), ACT.Sigmoid,
                                                       bias=cols(name, d)[:, t:t + 1])
                            m.then_inc(sem("sig"), 1)
                        for d in range(2):
                            act.wait_ge(sem("sums"), 3 * d + 3)
                            act.activation(Lx[:, :], Lx[:, :], ACT.Exp, scale=-DECAY).then_inc(sem("exp"), 1)
                            act.activation(EN[d][:, :], L[:, :], ACT.Exp, scale=DECAY).then_inc(sem("exp"), 1)
                            last_t = C - 1 if d == 0 else 0
                            for q in range(2):
                                i = chunk_of(d, q)
                                act.activation(PC[:, q, d, :], g3(L[:, :])[:, :, i * C + last_t], ACT.Exp, scale=-DECAY)
                            act.activation(Lr[d][:, :], Lr[d][:, :], ACT.Exp, scale=-DECAY).then_inc(sem("exp"), 1)
                            act.wait_ge(sem("exp"), 4 * d + 3)
                            act.activation(L[:, :], L[:, :], ACT.Exp, scale=-DECAY).then_inc(sem("exp"), 1)
                        copy_pieces("z")
                        for d in range(2):
                            for n_tm, (b, dst) in enumerate(((0, Kttm), (1, Btm), (2, Ktm), (3, Vtm))):
                                act.wait_ge(sem("tmm"), 4 * d + n_tm + 1)
                                act.activation(dst[d][:, :], bank(b), ACT.Copy).then_inc(sem("tm"), 1)
                            if want_y:
                                act.wait_ge(sem("rk"), d + 1)
                                act.dma_start(rk_d[:, d, :, bass.ds(at[d], P)], g3(Y[d][:, :])).then_inc(sem(f"rk_out{d}"), 16)
                            copy_pieces(f"prod{d}")
                        for n_lv in range(5):
                            for d in range(2):
                                act.wait_ge(sem(f"Ymm{d}"), n_lv + 1)
                                if n_lv:
                                    act.wait_ge(sem(f"offT{d}"), n_lv)
                                elif want_y:
                                    act.wait_ge(sem(f"rk_out{d}"), 16)
                                act.activation(Y[d][:, :], bank(4 + d), ACT.Copy).then_inc(sem(f"Y{d}"), 1)
                            copy_pieces(f"level{n_lv}")
                        for d in range(2):
                            act.wait_ge(sem("MVmm"), d + 1)
                            act.activation(MV[d][:, :], bank(d), ACT.Copy).then_inc(sem("MV"), 1)
                        for d in range(2):
                            act.wait_ge(sem("W2mm"), d + 1)
                            for q in range(2):
                                r = rows(chunk_of(d, q))
                                act.activation(W2s[q][r, :], ps[r, (4 + d) * 512:(5 + d) * 512], ACT.Copy).then_inc(sem("W2"), 1)
                        copy_pieces("W2", "U0", "S0")
                        if want_y:
                            for d in range(2):
                                act.wait_ge(sem("YRmm"), d + 1)
                                act.activation(sg[d][:, :], bank(4 + d), ACT.Copy).then_inc(sem("YR"), 1)
                        copy_pieces("U1", "YR0", "end")

                    @block.vector
                    def _(dve):
                        for d in range(2):
                            rev = slice(None, None, -1) if d else slice(None)
                            tl = 0 if d else C - 1
                            dve.wait_ge(sem("sig"), d + 1)
                            if d:
                                dve.wait_ge(sem("fm"), n_fm * d)
                                dve.wait_ge(sem("exp"), 4 * d)
                            dve.tensor_tensor_scan(L[:, rev], reset[:, d, rev], sg[d][:, rev], 0.0, ALU.mult, ALU.add).then_inc(sem("sums"), 1)
                            dve.wait_ge(sem("sums"), 3 * d + 1)
                            dve.tensor_tensor(Lx[:, :], L[:, :], sg[d][:, :], ALU.subtract).then_inc(sem("sums"), 1)
                            dve.tensor_tensor(g8(Lr[d][:, :]), g8(L[:, :])[:, :, tl:tl + 1].to_broadcast([P, 8, C]), g8(L[:, :]),
                                              ALU.subtract).then_inc(sem("sums"), 1)
                            dve.scalar_tensor_tensor(g3(Bp[d][:, :]), g3(a[d][:, :]), -1.0, bc(pa[l][:, PA["ka"]:PA["ka"] + 4], P, 2),
                                                     ALU.add, ALU.mult).then_inc(sem("kd"), 1)
                            dve.wait_ge(sem("kd"), 2 * d + 1)
                            dve.wait_ge(sem(f"k{d}"), 16)
                            dve.scalar_tensor_tensor(kd[d][:, :], Bp[d][:, :], 1.0, kI[d][:, :], ALU.add, ALU.mult).then_inc(sem("kd"), 1)
                            dve.wait_ge(sem(f"kk{d}"), 16)
                            dve.scalar_tensor_tensor(a[d][:, :], kkI[d][:, :], -1.0, a[d][:, :], ALU.mult, ALU.mult).then_inc(sem("b"), 1)
                            dve.wait_ge(sem("exp"), 4 * d + 1)
                            dve.wait_ge(sem("b"), d + 1)
                            dve.tensor_tensor(Kt[d][:, :], kkI[d][:, :], Lx[:, :], ALU.mult).then_inc(sem("fm"), 1)
                            dve.wait_ge(sem("exp"), 4 * d + 2)
                            dve.tensor_tensor(Bh[d][:, :], a[d][:, :], EN[d][:, :], ALU.mult).then_inc(sem("fm"), 1)
                            dve.wait_ge(sem("kd"), 2 * d + 2)
                            dve.tensor_tensor(EN[d][:, :], kd[d][:, :], EN[d][:, :], ALU.mult).then_inc(sem("fm"), 1)
                            dve.wait_ge(sem("exp"), 4 * d + 3)
                            dve.tensor_tensor(Bp[d][:, :], a[d][:, :], Lr[d][:, :], ALU.mult).then_inc(sem("fm"), 1)
                            dve.tensor_tensor(Lr[d][:, :], kd[d][:, :], Lr[d][:, :], ALU.mult).then_inc(sem("fm"), 1)
                            if want_y:
                                dve.wait_ge(sem("exp"), 4 * d + 4)
                                dve.wait_ge(sem(f"r{d}"), 16)
                                dve.tensor_tensor(Y[d][:, :], rI[d][:, :], kd[d][:, :], ALU.mult).then_inc(sem("rk"), 1)
                                dve.wait_ge(sem("rk"), d + 1)
                                dve.tensor_tensor(Rt[d][:, :], rI[d][:, :], L[:, :], ALU.mult).then_inc(sem("fm"), 1)
                        for d in range(2):
                            pv = lambda b, o: ps[:, b * 512:(b + 2) * 512].rearrange("p (h c) -> p h c", h=2)[:, :, o:o + 256]\
                                .rearrange("p h (t c) -> p h t c", t=CTILES)
                            o4 = lambda ap: ap.rearrange("p (h t c) -> p h t c", h=2, t=CTILES)
                            mk = lambda m: masks[:, m, :].unsqueeze(1).unsqueeze(1).to_broadcast([P, 2, CTILES, C])
                            strict, incl = ((M_UP, M_UPI), (M_LO, M_LOI))[d]
                            lo1, up1 = ((M_LO1, M_UP1), (M_UP1, M_LO1))[d]
                            dve.wait_ge(sem("pmm"), n_pr * d + 2)
                            dve.tensor_tensor(o4(NAT[d][:, :]), pv(0, 0), mk(strict), ALU.mult).then_inc(sem("prod"), 1)
                            dve.tensor_tensor(o4(T[d][:, :]), pv(0, 256), mk(lo1), ALU.mult).then_inc(sem("prod"), 1)
                            dve.wait_ge(sem("pmm"), n_pr * d + min(n_pr, 4))
                            dve.tensor_tensor(o4(MT[d][:, :]), pv(2, 0), mk(strict), ALU.mult).then_inc(sem("prod"), 1)
                            if want_y:
                                dve.tensor_tensor(o4(QB[d][:, :]), pv(2, 256), mk(incl), ALU.mult).then_inc(sem("prod"), 1)
                                dve.wait_ge(sem("pmm"), n_pr * d + 5)
                                dve.tensor_tensor(o4(QK[d][:, :]), pv(4, 0), mk(incl), ALU.mult).then_inc(sem("prod"), 1)
                            m8 = lambda m: masks[:, m, :].unsqueeze(1).to_broadcast([P, 8, C])
                            dve.wait_ge(sem("prod"), n_pr * d + 2)
                            dve.tensor_tensor(g8(T[d][:, :]), g8(T[d][:, :]), m8(M_ID), ALU.add)
                            dve.tensor_tensor(g8(TT[d][:, :]), g8(NAT[d][:, :]), m8(up1), ALU.mult).then_inc(sem("TT1"), 1)
                            dve.wait_ge(sem("TT1"), d + 1)
                            dve.tensor_tensor(g8(TT[d][:, :]), g8(TT[d][:, :]), m8(M_ID), ALU.add).then_inc(sem(f"T{d}"), 1)
                        for n_lv in range(5):
                            for d in range(2):
                                lo, up = (n_lv, 5 + n_lv) if d == 0 else (5 + n_lv, n_lv)
                                lm = lambda m: lvm[:, m, :].unsqueeze(1).to_broadcast([P, 8, C])
                                if n_lv < 4:
                                    dve.wait_ge(sem(f"off{d}"), n_lv + 1)
                                    dve.copy_predicated(g8(T[d][:, :]), lm(lo), g8(bank(d)))
                                dve.wait_ge(sem(f"offT{d}"), n_lv + 1)
                                dve.copy_predicated(g8(TT[d][:, :]), lm(up), g8(bank(2 + d))).then_inc(sem(f"T{d}"), 1)
                        for d in range(2):
                            dve.wait_ge(sem("W1mm"), d + 1)
                            dve.tensor_copy(W1T[d][:, :].rearrange("p (t i c) -> p i t c", t=CTILES, i=2),
                                            ps[:, 1024:2048].rearrange("p (i c) -> p i c", i=2)[:, :, 0:256]
                                            .rearrange("p i (t c) -> p i t c", t=CTILES)).then_inc(sem("W1"), 1)
                        half = lambda b: ps[:, b * 512:(b + 2) * 512].rearrange("p (b c) -> p b c", b=2)[:, :, 0:256]
                        for q in range(2):
                            if q:
                                dve.wait_ge(sem("S"), q)
                            else:
                                dve.wait_ge(sem("exp"), 8)
                            dve.tensor_tensor(S[q + 1][:, :].rearrange("p (g v) -> p g v", v=C),
                                              S[q][:, :].rearrange("p (g v) -> p g v", v=C),
                                              bc(PC[:, q].rearrange("p d t -> p (d t)"), C, 2), ALU.mult).then_inc(sem("SP"), 1)
                            dve.wait_ge(sem("Umm"), q + 1)
                            if q == 0:
                                dve.wait_ge(sem("W2"), 4)
                            dve.tensor_tensor(U[q][:, :].rearrange("p (b c) -> p b c", b=2), half(0),
                                              W2s[q][:, :].rearrange("p (b c) -> p b c", b=2), ALU.add).then_inc(sem("U"), 1)
                            dve.wait_ge(sem("Smm"), q + 1)
                            dve.wait_ge(sem("SP"), q + 1)
                            s_n = S[q + 1][:, :].rearrange("p (b c) -> p b c", b=2)
                            dve.tensor_tensor(s_n, s_n, half(2), ALU.add).then_inc(sem("S"), 1)
                        if want_y:
                            for d in range(2):
                                dve.wait_ge(sem("YUmm"), d + 1)
                                dve.wait_ge(sem("YR"), d + 1)
                                y = sg[d][:, :].rearrange("p (t i c) -> p t i c", t=CTILES, i=2)
                                dve.tensor_tensor(y, y, half(2 * d).rearrange("p i (t c) -> p t i c", t=CTILES), ALU.add).then_inc(sem("Ysum"), 1)
                            dve.wait_ge(sem("YRmm"), 2)
                        else:
                            dve.wait_ge(sem("Umm"), 2)
                        dve.wait_ge(sem("S"), 2)
                        dve.tensor_copy(S[0][:, :], S[2][:, :])

            groups(SEQ, CTX_LEN // P, not last, FILLERS[0])
            groups(0, SEQ // P, True, FILLERS[1])

        def rwkv_output(l, oc, last):
            seqs = LAT if last else BOTH
            n_tok = SEQ if last else TOK
            with ExitStack() as sc, stage(nc) as (block, sem):
                g2 = sb(sc, "g2", [P, D_C])
                yd = sb(sc, "y_dirs", [P, 2, CTILES, TOK])
                rkd = sb(sc, "rk_dirs", [P, 2, CTILES, TOK])
                vf = sb(sc, "v", [P, CTILES, TOK])
                gd = sb(sc, "g_lora", [P, TOK])
                yc = sb(sc, "yc", [P, 2, TOK])
                sq = sb(sc, "ysq", [P, 2, TOK])
                pr = lambda i: ps[:, i * 1024:i * 1024 + n_tok]
                col = lambda name, t: pa[l][:, PA[name] + t:PA[name] + t + 1]

                @block.sync
                def _(sp):
                    sp.dma_start(g2[:, :], A["rw_g2"][l]).then_inc(sem("g2"), 16)
                    sp.dma_start(gd[:, 0:n_tok], raw_d[:, R_G, 0:n_tok]).then_inc(sem("g2"), 16)
                    for t in range(CTILES):
                        sp.dma_start(yd[:, :, t, 0:n_tok], y_d[:, :, t, 0:n_tok]).then_inc(sem(f"in{t}"), 16)
                        sp.dma_start(rkd[:, :, t, 0:n_tok], rk_d[:, :, t, 0:n_tok]).then_inc(sem(f"in{t}"), 16)
                        sp.dma_start(vf[:, t, 0:n_tok], raw_d[:, R_V + t, 0:n_tok]).then_inc(sem(f"in{t}"), 16)

                @block.gpsimd
                def _(pool):
                    for t in range(CTILES):
                        pool.wait_ge(sem(f"in{t}"), 48)
                        pool.tensor_tensor(oc[:, t, 0:n_tok], yd[:, 0, t, 0:n_tok], yd[:, 1, t, 0:n_tok], ALU.add).then_inc(sem("y"), 1)
                        r = rkd[:, 0, t, 0:n_tok]
                        pool.tensor_tensor(r, r, rkd[:, 1, t, 0:n_tok], ALU.add).then_inc(sem("rk_sum"), 1)
                        pool.wait_ge(sem("rk_sum"), t + 1)
                        pool.tensor_scalar(r, r, col("rk", t), None, ALU.mult).then_inc(sem("rk"), 1)

                @block.tensor
                def _(pe):
                    pe.wait_ge(sem("g2"), 32)
                    for t in range(CTILES):
                        def by(dst, stat, mov, name):
                            for at, n in seqs:
                                m = pe.matmul(dst[:, at:at + n], stat, mov[:, at:at + n], start=True, stop=True)
                            m.then_inc(sem(name), 1)
                        if t:
                            pe.wait_ge(sem("done"), t)
                        pe.wait_ge(sem("y"), t + 1)
                        by(pr(0), blkones[:, :], oc[:, t, :], "mean")
                        by(pr(1), g2[:, t * P:(t + 1) * P], gd, "gate")
                        pe.wait_ge(sem("rk"), t + 1)
                        by(pr(2), blkones[:, :], rkd[:, 0, t, :], "bonus")
                        pe.wait_ge(sem("sq"), t + 1)
                        by(pr(3), blkones[:, :], sq[:, t % 2, :], "var")

                @block.scalar
                def _(act):
                    for t in range(CTILES):
                        act.wait_ge(sem("yc"), t + 1)
                        act.activation(sq[:, t % 2, 0:n_tok], yc[:, t % 2, 0:n_tok], ACT.Square).then_inc(sem("sq"), 1)
                        act.wait_ge(sem("v"), t + 1)
                        act.activation(sq[:, t % 2, 0:n_tok], sq[:, t % 2, 0:n_tok], ACT.Sqrt).then_inc(sem("std"), 1)
                        act.wait_ge(sem("yn"), t + 1)
                        act.activation(yc[:, t % 2, 0:n_tok], yc[:, t % 2, 0:n_tok], ACT.Identity, bias=col("lnb", t),
                                       scale=col("lnw", t)).then_inc(sem("yl"), 1)

                @block.vector
                def _(dve):
                    steps = [0]

                    def link(ins):
                        steps[0] += 1
                        ins.then_inc(sem("dve"), 1)
                        dve.wait_ge(sem("dve"), steps[0])
                    for t in range(CTILES):
                        c, s, y = yc[:, t % 2, 0:n_tok], sq[:, t % 2, 0:n_tok], oc[:, t, 0:n_tok]
                        dve.wait_ge(sem("mean"), t + 1)
                        dve.scalar_tensor_tensor(c, pr(0), -1.0 / HS_C, y, ALU.mult, ALU.add).then_inc(sem("yc"), 1)
                        dve.wait_ge(sem("bonus"), t + 1)
                        dve.wait_ge(sem("yc"), t + 1)
                        link(dve.tensor_tensor(y, pr(2), vf[:, t, 0:n_tok], ALU.mult))
                        dve.wait_ge(sem("var"), t + 1)
                        dve.tensor_scalar(s, pr(3), 1.0 / HS_C, GN_EPS, ALU.mult, ALU.add).then_inc(sem("v"), 1)
                        dve.wait_ge(sem("std"), t + 1)
                        link(dve.reciprocal(s, s))
                        dve.tensor_tensor(c, c, s, ALU.mult).then_inc(sem("yn"), 1)
                        dve.wait_ge(sem("yl"), t + 1)
                        link(dve.tensor_tensor(y, y, c, ALU.add))
                        dve.wait_ge(sem("gate"), t + 1)
                        dve.tensor_tensor(y, y, pr(1), ALU.mult).then_inc(sem("done"), 1)

        def attention(l, oa, last):
            nq = LT if last else NT
            q_seqs = LAT if last else BOTH
            q_tok = SEQ if last else TOK
            units = [(j, u) for j in range(HA) for u in range(nq)]
            N = len(units)
            users = []
            for n, (j, u) in enumerate(units):
                if u == 0:
                    users.append(("v", j))
                users += [("s", n, 0), ("s", n, 1)]
            place = {who: i for i, who in enumerate(users)}
            buf = lambda who, w: ps[:, (place[who] % 3) * 1024:(place[who] % 3) * 1024 + w]
            with ExitStack() as sc, stage(nc) as (block, sem):
                rope = sb(sc, "rope", [P, 2, SEQ])
                qp = sb(sc, "q_plain", [P, 2, TOK])
                kp = sb(sc, "k_plain", [P, 2, TOK])
                vp = sb(sc, "v_fm", [P, 2, TOK])
                qr = sb(sc, "q_rot", [P, 2, SEQ])
                kr = sb(sc, "k_rot", [P, 2, SEQ])
                vt = sb(sc, "v_tm", [P, 2, NT, P])
                shuf = sb(sc, "shuf", [P, 2, SEQ])
                rcos = sb(sc, "rcos", [P, 2, SEQ])
                E = sb(sc, "E", [P, 3, 2, TOK])
                mx = sb(sc, "mx", [P, 3, 2])
                sm = sb(sc, "sm", [P, 3, 2])
                ratio = sb(sc, "ratio", [P, 3])
                diag = sb(sc, "diag", [P, 3, P])
                at = sb(sc, "a_T", [P, 2, TOK])
                swap = list(range(16, 32)) + list(range(16))
                n_keys = lambda u: TOK if u < LT else CTX_LEN
                k_tiles = lambda u: range(NT) if u < LT else range(LT, NT)

                def wait_free(pe, who):
                    i = place[who] - 3
                    if i >= 0:
                        if users[i][0] == "v":
                            pe.wait_ge(sem("vt"), users[i][1] + 1)
                        else:
                            pe.wait_ge(sem(f"exp{users[i][2]}"), users[i][1] + 1)

                @block.sync
                def _(sp):
                    sp.dma_start(rope[:, :, :], A["rope"]).then_inc(sem("rope"), 16)
                    for j in range(HA):
                        if j >= 2:
                            sp.wait_ge(sem("s1_mm"), (j - 1) * nq)
                            sp.wait_ge(sem("v_mm"), j - 1)
                            sp.wait_ge(sem("rot"), 2 * (j - 1))
                        sp.dma_start(vp[:, j % 2, :], proj_d[J_V + j]).then_inc(sem(f"v_in{j % 2}"), 16)
                        sp.dma_start(qp[:, j % 2, 0:q_tok], proj_d[J_Q + j, :, 0:q_tok]).then_inc(sem(f"q_in{j % 2}"), 16)
                        sp.dma_start(kp[:, j % 2, :], proj_d[J_K + j]).then_inc(sem(f"k_in{j % 2}"), 16)

                @block.tensor
                def _(pe):
                    def scores(n):
                        j, u = units[n]
                        if u == 0:
                            pe.wait_ge(sem(f"v_in{j % 2}"), 16 * (j // 2 + 1))
                            wait_free(pe, ("v", j))
                            for t in range(NT):
                                m = pe.transpose(buf(("v", j), TOK)[:, t * P:(t + 1) * P], vp[:, j % 2, t * P:(t + 1) * P], ident[:, :])
                            m.then_inc(sem("v_mm"), 1)
                            pe.wait_ge(sem("rot"), 2 * j + 2)
                            pe.wait_ge(sem(f"q_in{j % 2}"), 16 * (j // 2 + 1))
                            pe.wait_ge(sem(f"k_in{j % 2}"), 16 * (j // 2 + 1))
                        qs = slice(u * P, (u + 1) * P)
                        for c in range(2):
                            wait_free(pe, ("s", n, c))
                            o = buf(("s", n, c), TOK)
                            r = slice(c * DH_A, (c + 1) * DH_A)
                            k0 = 0
                            if u < LT:
                                pe.matmul(o[:, 0:SEQ], qr[r, j % 2, qs], kr[r, j % 2, :], start=True, stop=True)
                                k0 = SEQ
                            pe.matmul(o[:, k0:k0 + CTX_LEN], qp[r, j % 2, qs], kp[r, j % 2, SEQ:TOK],
                                      start=True, stop=True).then_inc(sem(f"s{c}_mm"), 1)

                    def turn(n):
                        j, u = units[n]
                        pe.wait_ge(sem("a"), n + 1)
                        pe.wait_ge(sem("diag"), n + 1)
                        if n:
                            pe.wait_ge(sem("o_read"), n)
                        for i in range(len(k_tiles(u))):
                            m = pe.matmul(ps[:, 3072 + i * P:3072 + (i + 1) * P], E[:, n % 3, 1, i * P:(i + 1) * P], diag[:, n % 3, :],
                                          start=True, stop=True)
                        m.then_inc(sem("aT_mm"), 1)

                    def values(n):
                        j, u = units[n]
                        kts = k_tiles(u)
                        pe.wait_ge(sem("aT"), n + 1)
                        for i, kt in enumerate(kts):
                            m = pe.matmul(bank(7, P, 384), vt[:, j % 2, kt, :], at[:, n % 2, i * P:(i + 1) * P],
                                          start=i == 0, stop=i == len(kts) - 1)
                        m.then_inc(sem("o"), 1)

                    pe.wait_ge(sem("rope"), 16)
                    scores(0)
                    scores(1)
                    for n in range(N):
                        turn(n)
                        if n + 2 < N:
                            scores(n + 2)
                        values(n)

                @block.scalar
                def _(act):
                    def soft(n):
                        j, u = units[n]
                        if u == 0:
                            act.wait_ge(sem("v_mm"), j + 1)
                            if j >= 2:
                                act.wait_ge(sem("o"), (j - 1) * nq)
                            act.activation(vt[:, j % 2, :, :].rearrange("p t d -> p (t d)"), buf(("v", j), TOK), ACT.Copy).then_inc(sem("vt"), 1)
                        w = n_keys(u)
                        if n >= 3:
                            act.wait_ge(sem("aT_mm"), n - 2)
                            act.wait_ge(sem("rec"), n - 2)
                        for c in range(2):
                            act.wait_ge(sem(f"max{c}"), n + 1)
                            act.activation(E[:, n % 3, c, 0:w], buf(("s", n, c), w), ACT.Exp, bias=mx[:, n % 3, c:c + 1],
                                           scale=DH_A ** -0.5, accum_out=sm[:, n % 3, c:c + 1]).then_inc(sem(f"exp{c}"), 1)
                    soft(0)
                    soft(1)
                    for n, (j, u) in enumerate(units):
                        w = n_keys(u)
                        act.wait_ge(sem("aT_mm"), n + 1)
                        if n >= 2:
                            act.wait_ge(sem("o"), n - 1)
                        act.activation(at[:, n % 2, 0:w], ps[:, 3072:3072 + w], ACT.Copy).then_inc(sem("aT"), 1)
                        act.wait_ge(sem("o"), n + 1)
                        act.activation(oa[:, j, u * P:(u + 1) * P], bank(7, P, 384), ACT.Copy).then_inc(sem("o_read"), 1)
                        if n + 2 < N:
                            soft(n + 2)

                @block.gpsimd
                def _(pool):
                    pool.wait_ge(sem("rope"), 16)
                    for j in range(HA):
                        for i in range(2):
                            n = 2 * j + i
                            pool.wait_ge(sem(f"{'qk'[i]}_in{j % 2}"), 16 * (j // 2 + 1))
                            if n >= 2:
                                pool.wait_ge(sem("rot"), n - 1)
                            pool.tensor_tensor(rcos[:, i, :], (qp, kp)[i][:, j % 2, 0:SEQ], rope[:, 0, :], ALU.mult).then_inc(sem("rcos"), 1)
                            pool.wait_ge(sem("rcos"), n + 1)
                            pool.wait_ge(sem("shuf"), n + 1)
                            pool.tensor_tensor(shuf[:, i, :], shuf[:, i, :], rope[:, 1, :], ALU.mult).then_inc(sem("rsin"), 1)
                            pool.wait_ge(sem("rsin"), n + 1)
                            if j >= 2:
                                pool.wait_ge(sem("s1_mm"), (j - 1) * nq)
                            pool.tensor_tensor((qr, kr)[i][:, j % 2, :], shuf[:, i, :], rcos[:, i, :], ALU.add).then_inc(sem("rot"), 1)

                @block.vector
                def _(dve):
                    def shuffle(j):
                        for i in range(2):
                            n = 2 * j + i
                            dve.wait_ge(sem(f"{'qk'[i]}_in{j % 2}"), 16 * (j // 2 + 1))
                            if n >= 2:
                                dve.wait_ge(sem("rot"), n - 1)
                            dve.stream_shuffle(shuf[:, i, :], (qp, kp)[i][:, j % 2, 0:SEQ], swap).then_inc(sem("shuf"), 1)

                    def maxima(n):
                        w = n_keys(units[n][1])
                        if n >= 3:
                            dve.wait_ge(sem("exp1"), n - 2)
                        for c in range(2):
                            m = mx[:, n % 3, c:c + 1]
                            dve.wait_ge(sem(f"s{c}_mm"), n + 1)
                            dve.tensor_reduce(m, buf(("s", n, c), w), AX.X, ALU.max).then_inc(sem(f"mraw{c}"), 1)
                            dve.wait_ge(sem(f"mraw{c}"), n + 1)
                            dve.tensor_scalar(m, m, -DH_A ** -0.5, None, ALU.mult).then_inc(sem(f"max{c}"), 1)

                    def combine(n):
                        w = n_keys(units[n][1])
                        s, q = sm[:, n % 3, :], ratio[:, n % 3:n % 3 + 1]
                        dve.wait_ge(sem("exp0"), n + 1)
                        dve.wait_ge(sem("exp1"), n + 1)
                        if n >= 3:
                            dve.wait_ge(sem("aT_mm"), n - 2)
                        dve.tensor_tensor(q, s[:, 0:1], nlam[l][:, :], ALU.mult).then_inc(sem("q"), 1)
                        dve.wait_ge(sem("q"), 2 * n + 1)
                        dve.reciprocal(s, s).then_inc(sem("rec"), 1)
                        dve.wait_ge(sem("rec"), n + 1)
                        dve.tensor_tensor(q, q, s[:, 1:2], ALU.mult).then_inc(sem("q"), 1)
                        dve.tensor_scalar(diag[:, n % 3, :], ident[:, :], s[:, 0:1], None, ALU.mult).then_inc(sem("diag"), 1)
                        dve.wait_ge(sem("q"), 2 * n + 2)
                        dve.scalar_tensor_tensor(E[:, n % 3, 1, 0:w], E[:, n % 3, 1, 0:w], q, E[:, n % 3, 0, 0:w],
                                                 ALU.mult, ALU.add).then_inc(sem("a"), 1)

                    dve.wait_ge(sem("rope"), 16)
                    shuffle(0)
                    maxima(0)
                    maxima(1)
                    combine(0)
                    for n in range(N):
                        if n + 1 < N:
                            combine(n + 1)
                        if units[n][1] == 0 and units[n][0] + 1 < HA:
                            shuffle(units[n][0] + 1)
                        if n + 2 < N:
                            maxima(n + 2)

            with ExitStack() as sc, stage(nc) as (block, sem):
                sq = sb(sc, "osq", [P, 2, TOK])
                rr = sb(sc, "orr", [P, 2, TOK])
                p_of = lambda j: ps[:, (j % 2) * 1024:(j % 2) * 1024 + q_tok]

                @block.scalar
                def _(act):
                    for j in range(HA):
                        if j >= 2:
                            act.wait_ge(sem("ss"), j - 1)
                        act.activation(sq[:, j % 2, 0:q_tok], oa[:, j, 0:q_tok], ACT.Square).then_inc(sem("sq"), 1)
                        if j:
                            act.wait_ge(sem("ms"), j)
                            act.activation(rr[:, (j - 1) % 2, 0:q_tok], rr[:, (j - 1) % 2, 0:q_tok], ACT.Sqrt).then_inc(sem("std"), 1)
                    act.wait_ge(sem("ms"), HA)
                    act.activation(rr[:, (HA - 1) % 2, 0:q_tok], rr[:, (HA - 1) % 2, 0:q_tok], ACT.Sqrt).then_inc(sem("std"), 1)

                @block.tensor
                def _(pe):
                    for j in range(HA):
                        pe.wait_ge(sem("sq"), j + 1)
                        if j >= 2:
                            pe.wait_ge(sem("ms"), j - 1)
                        for at_, n in q_seqs:
                            m = pe.matmul(p_of(j)[:, at_:at_ + n], ones[:, :], sq[:, j % 2, at_:at_ + n], start=True, stop=True)
                        m.then_inc(sem("ss"), 1)

                @block.vector
                def _(dve):
                    def mean(j):
                        dve.wait_ge(sem("ss"), j + 1)
                        dve.tensor_scalar(rr[:, j % 2, 0:q_tok], p_of(j), 1.0 / DV, HEAD_EPS, ALU.mult, ALU.add).then_inc(sem("ms"), 1)
                    mean(0)
                    for j in range(HA):
                        if j + 1 < HA:
                            mean(j + 1)
                        r = rr[:, j % 2, 0:q_tok]
                        dve.wait_ge(sem("std"), j + 1)
                        dve.reciprocal(r, r).then_inc(sem("rec"), 1)
                        dve.wait_ge(sem("rec"), j + 1)
                        dve.scalar_tensor_tensor(oa[:, j, 0:q_tok], oa[:, j, 0:q_tok], subln[l][:, :], r, ALU.mult, ALU.mult).then_inc(sem("oa"), 1)
                        dve.wait_ge(sem("oa"), j + 1)

        def fourier(l, of, last):
            seqs = LAT if last else BOTH
            n_tok = SEQ if last else TOK
            nt = n_tok // P
            with ExitStack() as sc, stage(nc) as (block, sem):
                dw = sb(sc, "dft_w", [P, 2 * P])
                dl = sb(sc, "dft_lat", [P, 2, LT, SEQ])
                dc = sb(sc, "dft_ctx", [P, 2, CT, CTX_LEN])
                f = sb(sc, "f", [P, F_GROUPS, TOK])
                z = sb(sc, "z", [P, 2, NT, 2 * P])

                @block.sync
                def _(sp):
                    sp.dma_start(f[:, :, 0:n_tok], proj_d[J_F:J_F + F_GROUPS, :, 0:n_tok].rearrange("j p n -> p j n")).then_inc(sem("f"), 16)
                    sp.dma_start(dw[:, :], A["dft_w"]).then_inc(sem("dft"), 16)
                    sp.dma_start(dl[:, :, :, :], A["dft_lat"]).then_inc(sem("dft"), 16)
                    sp.dma_start(dc[:, :, :, :], A["dft_ctx"]).then_inc(sem("dft"), 16)

                @block.tensor
                def _(pe):
                    pe.wait_ge(sem("f"), 16)
                    pe.wait_ge(sem("dft"), 48)
                    for j in range(F_GROUPS):
                        for t in range(nt):
                            if j and t % 2 == 0:
                                pe.wait_ge(sem("z"), 3 * (j - 1) + t // 2 + 1 if nt == 6 else 2 * (j - 1) + t // 2 + 1)
                            m = pe.matmul(ps[:, 1024 + t * 256:1280 + t * 256], f[:, j, t * P:(t + 1) * P], dw[:, :],
                                          start=True, stop=True)
                            if t % 2:
                                m.then_inc(sem("zmm"), 1)
                        pe.wait_ge(sem("z"), (nt // 2) * (j + 1))
                        if j:
                            pe.wait_ge(sem("of"), j)
                        for i in range(2 * LT):
                            m = pe.matmul(bank(6), z[:, j % 2, i % LT, (i // LT) * P:(i // LT + 1) * P], dl[:, i // LT, i % LT, :],
                                          start=i == 0, stop=i == 2 * LT - 1)
                        if not last:
                            for i in range(2 * CT):
                                m = pe.matmul(bank(7, 256), z[:, j % 2, LT + i % CT, (i // CT) * P:(i // CT + 1) * P], dc[:, i // CT, i % CT, :],
                                              start=i == 0, stop=i == 2 * CT - 1)
                        m.then_inc(sem("ofmm"), 1)

                @block.vector
                def _(dve):
                    for j in range(F_GROUPS):
                        for i in range(nt // 2):
                            dve.wait_ge(sem("zmm"), j * (nt // 2) + i + 1)
                            if j >= 2:
                                dve.wait_ge(sem("ofmm"), j - 1)
                            dve.tensor_copy(z[:, j % 2, 2 * i:2 * i + 2, :].rearrange("p a b -> p (a b)"), bank(2 + i)).then_inc(sem("z"), 1)

                @block.scalar
                def _(act):
                    for j in range(F_GROUPS):
                        act.wait_ge(sem("ofmm"), j + 1)
                        act.activation(of[:, j, 0:n_tok], ps[:, 3072:3072 + n_tok], ACT.Copy).then_inc(sem("of"), 1)

        def merge(l, b, w_name, o, kt, y, last):
            seqs = LAT if last else BOTH
            n_tok = SEQ if last else TOK
            with ExitStack() as sc, stage(nc) as (block, sem):
                rings = weight_rings(sc, 3, 2)
                pair = sb(sc, "o_hi", [P, kt, TOK], F32R), sb(sc, "o_lo", [P, kt, TOK], F32R)
                gt = sb(sc, "gate", [P, 3, TOK])
                pr = sb(sc, "gated", [P, 2, TOK])
                src = A[w_name][l].rearrange("(k p) n -> p k n", p=P)
                p_of = lambda j: ps[:, (j % 4) * 1024:(j % 4) * 1024 + n_tok]
                out_of = (lambda j: y[:, j, 0:n_tok]) if b == 0 else (lambda j: pr[:, j % 2, 0:n_tok])

                @block.sync
                def _(sp):
                    for j in range(KT):
                        load_weights(sp, sem, rings, j, src[:, :, j * P:(j + 1) * P])
                        if j >= 3:
                            sp.wait_ge(sem("gated"), j - 2)
                        sp.dma_start(gt[:, j % 3, 0:n_tok], proj_d[J_G + b * KT + j, :, 0:n_tok]).then_inc(sem(f"gate_in{j % 3}"), 16)

                @block.tensor
                def _(pe):
                    for j in range(KT):
                        pe.wait_ge(sem("w_lo"), j + 1)
                        if j >= 4:
                            pe.wait_ge(sem("gated"), j - 3)
                        for k in range(kt):
                            if j == 0:
                                pe.wait_ge(sem("o_lo"), k + 1)
                            m = fm_product(pe, p_of(j), slot(rings, j), pair, (k,), kt, seqs)
                        m.then_inc(sem("w_used"), 1)

                @block.scalar
                def _(act):
                    split_hi(act, sem, rings, 0, kt)
                    for k in range(kt):
                        act.activation(pair[0][:, k, 0:n_tok], o[:, k, 0:n_tok], ACT.Copy).then_inc(sem("o_hi"), 1)
                    for j in range(KT):
                        if j + 1 < KT:
                            split_hi(act, sem, rings, j + 1, kt)
                        act.wait_ge(sem(f"gate_in{j % 3}"), 16 * (j // 3 + 1))
                        g = gt[:, j % 3, 0:n_tok]
                        act.activation(g, g, ACT.Sigmoid).then_inc(sem("gate"), 1)

                @block.vector
                def _(dve):
                    for k in range(kt):
                        dve.wait_ge(sem("o_hi"), k + 1)
                        dve.tensor_tensor(pair[1][:, k, 0:n_tok], o[:, k, 0:n_tok], pair[0][:, k, 0:n_tok].bitcast(F32),
                                          ALU.subtract).then_inc(sem("o_lo"), 1)
                    for j in range(KT):
                        dve.wait_ge(sem("w_used"), j + 1)
                        dve.wait_ge(sem("gate"), j + 1)
                        if b and j >= 2:
                            dve.wait_ge(sem("sum"), j - 1)
                        dve.tensor_tensor(out_of(j), gt[:, j % 3, 0:n_tok], p_of(j), ALU.mult).then_inc(sem("gated"), 1)
                        if b:
                            dve.wait_ge(sem("gated"), j + 1)
                            dve.tensor_tensor(y[:, j, 0:n_tok], y[:, j, 0:n_tok], out_of(j), ALU.add).then_inc(sem("sum"), 1)

                @block.gpsimd
                def _(pool):
                    for j in range(KT):
                        split_lo(pool, sem, rings, j, kt)

        def gate_rows(sc, i_mod, streams):
            g = sb(sc, "gate_row", [P, 2, D_MODEL])
            with ExitStack() as s2, stage(nc) as (block, sem):
                diag = sb(s2, "diag", [P, 2 * KT, P])

                @block.vector
                def _(dve):
                    for s in range(streams):
                        for j in range(KT):
                            m = dve.tensor_scalar(diag[:, s * KT + j, :], ident[:, :], mod[:, 8 * i_mod + j, s:s + 1], None, ALU.mult)
                        m.then_inc(sem("diag"), 1)

                @block.tensor
                def _(pe):
                    for s in range(streams):
                        pe.wait_ge(sem("diag"), s + 1)
                        for j in range(0, KT, 4):
                            m = pe.matmul(bank(2 * s + j // 4), ones[:, :], diag[:, s * KT + j:s * KT + j + 4, :].rearrange("p a b -> p (a b)"),
                                          start=True, stop=True)
                        m.then_inc(sem("row"), 1)

                @block.scalar
                def _(act):
                    for s in range(streams):
                        act.wait_ge(sem("row"), s + 1)
                        act.activation(g[:, s, :], ps[:, s * 1024:(s + 1) * 1024], ACT.Copy)
            return g

        def out_proj(l, y, last):
            nt = LT if last else NT
            with ExitStack() as sc:
                gate = gate_rows(sc, 2, 1 if last else 2)
                with stage(nc) as (block, sem):
                    w = sb(sc, "w_o", [P, KT, D_MODEL])
                    lg = sb(sc, "ln_g", [P, D_MODEL])
                    lb = sb(sc, "ln_b", [P, D_MODEL])
                    tmp = sb(sc, "tmp", [P, 2, D_MODEL])

                    @block.sync
                    def _(sp):
                        sp.dma_start(w[:, :, :], A["w_o"][l].rearrange("(k p) n -> p k n", p=P)).then_inc(sem("w"), 16)
                        sp.dma_start(x[:, :, :], x_keep).then_inc(sem("x_back"), 16)
                        sp.dma_start(lg[:, :], A["ln1_g"][l].partition_broadcast(P)).then_inc(sem("ln"), 16)
                        sp.dma_start(lb[:, :], A["ln1_b"][l].partition_broadcast(P)).then_inc(sem("ln"), 16)

                    @block.tensor
                    def _(pe):
                        pe.wait_ge(sem("w"), 16)
                        for t in range(nt):
                            if t >= 4:
                                pe.wait_ge(sem("z1"), t - 3)
                            for n in range(2):
                                for k in range(KT):
                                    m = pe.matmul(bank(2 * (t % 4) + n), y[:, k, t * P:(t + 1) * P], w[:, k, n * 512:(n + 1) * 512],
                                                  start=k == 0, stop=k == KT - 1)
                            m.then_inc(sem("mm"), 1)

                    norm_tail(block, sem, sc, nt, lambda t: ps[:, (t % 4) * 1024:(t % 4) * 1024 + 1024], gate, tmp, lg, lb, "x_back")

        def norm_tail(block, sem, sc, nt, p_of, gate, tmp, lg, lb, wait_x):
            st = sb(sc, "stats", [P, NT, 2, 6])
            mv = sb(sc, "mean_var", [P, NT, 2])
            rs = sb(sc, "rstd", [P, NT])

            @block.vector
            def _(dve):
                if wait_x:
                    dve.wait_ge(sem(wait_x), 16)
                dve.wait_ge(sem("ln"), 32)

                def first(t):
                    dve.wait_ge(sem("mm"), t + 1)
                    if t >= 2:
                        dve.wait_ge(sem("z2"), t - 1)
                    dve.tensor_tensor(tmp[:, t % 2, :], p_of(t), gate[:, t // LT, :], ALU.mult).then_inc(sem("z1"), 1)
                    dve.wait_ge(sem("z1"), t + 1)
                    dve.scalar_tensor_tensor(x[:, t, :], x[:, t, :], ALPHA, tmp[:, t % 2, :], ALU.mult, ALU.add).then_inc(sem("z2"), 1)
                    dve.wait_ge(sem("z2"), t + 1)
                    for f in range(2):
                        i = dve.bn_stats(st[:, t, f, :], x[:, t, f * 512:(f + 1) * 512])
                    i.then_inc(sem("st"), 1)
                    dve.wait_ge(sem("st"), t + 1)
                    dve.bn_aggr(mv[:, t, :], st[:, t, :, :]).then_inc(sem("mv"), 1)
                    dve.wait_ge(sem("mv"), t + 1)
                    dve.tensor_scalar(rs[:, t:t + 1], mv[:, t, 1:2], LN_EPS, None, ALU.add).then_inc(sem("var"), 1)

                def second(t):
                    dve.wait_ge(sem("std"), t + 1)
                    dve.reciprocal(rs[:, t:t + 1], rs[:, t:t + 1]).then_inc(sem("rstd"), 1)
                    dve.wait_ge(sem("rstd"), t + 1)
                    dve.tensor_scalar(x[:, t, :], x[:, t, :], mv[:, t, 0:1], rs[:, t:t + 1], ALU.subtract, ALU.mult).then_inc(sem("xn"), 1)
                    dve.wait_ge(sem("xn"), t + 1)
                    dve.tensor_tensor(x[:, t, :], x[:, t, :], lg[:, :], ALU.mult).then_inc(sem("xg"), 1)

                first(0)
                for t in range(nt):
                    if t + 1 < nt:
                        first(t + 1)
                    second(t)

            @block.gpsimd
            def _(pool):
                for t in range(nt):
                    pool.wait_ge(sem("xg"), t + 1)
                    pool.tensor_tensor(x[:, t, :], x[:, t, :], lb[:, :], ALU.add)

            @block.scalar
            def _(act):
                for t in range(nt):
                    act.wait_ge(sem("var"), t + 1)
                    act.activation(rs[:, t:t + 1], rs[:, t:t + 1], ACT.Sqrt).then_inc(sem("std"), 1)

        def ffn(l, hf, h, last):
            seqs = LAT if last else BOTH
            n_tok = SEQ if last else TOK
            nt = n_tok // P
            with ExitStack() as s2, stage(nc) as (block, sem):
                rings = weight_rings(s2, 3, 2)
                cv = sb(s2, "conv", [P, 2, TOK])
                src = A["ffn_up"][l].rearrange("(k p) n -> p k n", p=P)
                p_of = lambda s: ps[:, (s % 4) * 1024:(s % 4) * 1024 + n_tok]
                tap = lambda i, j: pb[l][:, PB["conv"] + i * FT + j:PB["conv"] + i * FT + j + 1]

                @block.sync
                def _(sp):
                    for s in range(2 * FT):
                        o = (D_FF, 0)[s % 2] + s // 2 * P
                        load_weights(sp, sem, rings, s, src[:, :, o:o + P])

                @block.tensor
                def _(pe):
                    for s in range(2 * FT):
                        pe.wait_ge(sem("w_lo"), s + 1)
                        if s >= 4:
                            pe.wait_ge(sem("hf"), s // 2 - 1)
                        fm_product(pe, p_of(s), slot(rings, s), h, range(KT), KT, seqs).then_inc(sem("w_used"), 1)

                @block.scalar
                def _(act):
                    def own(j):
                        act.wait_ge(sem("w_used"), 2 * j + 1)
                        if j >= 2:
                            act.wait_ge(sem("hf"), j - 1)
                        act.activation(cv[:, j % 2, 0:n_tok], p_of(2 * j), ACT.Copy, scale=tap(1, j)).then_inc(sem("own"), 1)
                    for s in range(3):
                        split_hi(act, sem, rings, s)
                    own(0)
                    for j in range(FT):
                        for s in (2 * j + 3, 2 * j + 4):
                            if s < 2 * FT:
                                split_hi(act, sem, rings, s)
                        if j + 1 < FT:
                            own(j + 1)
                        act.wait_ge(sem("conv"), j + 1)
                        act.activation(cv[:, j % 2, 0:n_tok], cv[:, j % 2, 0:n_tok], ACT.Gelu,
                                       bias=pb[l][:, PB["conv_b"] + j:PB["conv_b"] + j + 1]).then_inc(sem("gelu"), 1)

                @block.gpsimd
                def _(pool):
                    for s in range(2 * FT):
                        split_lo(pool, sem, rings, s)

                @block.vector
                def _(dve):
                    def conv(j):
                        dve.wait_ge(sem("own"), j + 1)
                        for i, (at, n) in enumerate(seqs):
                            o, p = cv[:, j % 2, at:at + n], p_of(2 * j)[:, at:at + n]
                            dve.scalar_tensor_tensor(o[:, 1:n], p[:, 0:n - 1], tap(0, j), o[:, 1:n], ALU.mult, ALU.add).then_inc(sem(f"prev{i}"), 1)
                        for i, (at, n) in enumerate(seqs):
                            o, p = cv[:, j % 2, at:at + n], p_of(2 * j)[:, at:at + n]
                            dve.wait_ge(sem(f"prev{i}"), j + 1)
                            m = dve.scalar_tensor_tensor(o[:, 0:n - 1], p[:, 1:n], tap(2, j), o[:, 0:n - 1], ALU.mult, ALU.add)
                        m.then_inc(sem("conv"), 1)
                    conv(0)
                    for j in range(FT):
                        dve.wait_ge(sem("gelu"), j + 1)
                        dve.wait_ge(sem("w_used"), 2 * j + 2)
                        dve.tensor_tensor(hf[:, j, :], cv[:, j % 2, 0:n_tok], p_of(2 * j + 1), ALU.mult).then_inc(sem("hf"), 1)
                        if j + 1 < FT:
                            conv(j + 1)

        def ffn_down(l, hf, last):
            nt = LT if last else NT
            with ExitStack() as sc:
                gate = gate_rows(sc, 5, 1 if last else 2)
                with stage(nc) as (block, sem):
                    KG, SL = 2, 8
                    ring = sb(sc, "w_down", [P, SL, KG, 512])
                    lg = sb(sc, "ln_g", [P, D_MODEL])
                    lb = sb(sc, "ln_b", [P, D_MODEL])
                    part = sb(sc, "part", [P, 2, 512])
                    src = A["ffn_down"][l].rearrange("(g k p) n -> g p k n", p=P, k=KG)
                    NG = FT // KG
                    st = sb(sc, "stats", [P, NT, 2, 6])
                    mv = sb(sc, "mean_var", [P, NT, 2])
                    rs = sb(sc, "rstd", [P, NT])

                    @block.sync
                    def _(sp):
                        sp.dma_start(lg[:, :], A["ln2_g"][l].partition_broadcast(P)).then_inc(sem("ln"), 16)
                        sp.dma_start(lb[:, :], A["ln2_b"][l].partition_broadcast(P)).then_inc(sem("ln"), 16)
                        for n in range(2):
                            for g in range(NG):
                                i = n * NG + g
                                if i >= SL:
                                    sp.wait_ge(sem("w_used"), i - SL + 1)
                                sp.dma_start(ring[:, i % SL, :, :], src[g, :, :, n * 512:(n + 1) * 512]).then_inc(sem(f"w_in{i % SL}"), 16)

                    @block.tensor
                    def _(pe):
                        for n in range(2):
                            for g in range(NG):
                                i = n * NG + g
                                pe.wait_ge(sem(f"w_in{i % SL}"), 16 * (i // SL + 1))
                                for t in range(nt):
                                    if n and g == 0:
                                        pe.wait_ge(sem("z1"), t + 1)
                                    for k in range(KG):
                                        m = pe.matmul(bank(t), hf[:, g * KG + k, t * P:(t + 1) * P], ring[:, i % SL, k, :],
                                                      start=g == 0 and k == 0, stop=g == NG - 1 and k == KG - 1)
                                    if g == NG - 1 and t < nt - 1:
                                        m.then_inc(sem("mm"), 1)
                                if g == NG - 1:
                                    m.then_inc(sem("mm"), 1)
                                else:
                                    m.then_inc(sem("w_used"), 1)

                    @block.vector
                    def _(dve):
                        dve.wait_ge(sem("ln"), 32)
                        for n in range(2):
                            c = slice(n * 512, (n + 1) * 512)
                            for t in range(nt):
                                i = n * nt + t
                                dve.wait_ge(sem("mm"), i + 1)
                                if i >= 2:
                                    dve.wait_ge(sem("z2"), i - 1)
                                dve.tensor_tensor(part[:, i % 2, :], bank(t), gate[:, t // LT, c], ALU.mult).then_inc(sem("z1"), 1)
                                dve.wait_ge(sem("z1"), i + 1)
                                dve.scalar_tensor_tensor(x[:, t, c], x[:, t, c], ALPHA, part[:, i % 2, :], ALU.mult, ALU.add).then_inc(sem("z2"), 1)
                                dve.wait_ge(sem("z2"), i + 1)
                                dve.bn_stats(st[:, t, n, :], x[:, t, c]).then_inc(sem("st"), 1)
                        for t in range(nt):
                            dve.wait_ge(sem("st"), nt + t + 1)
                            m = dve.bn_aggr(mv[:, t, :], st[:, t, :, :])
                        m.then_inc(sem("mv"), 1)
                        dve.wait_ge(sem("mv"), 1)
                        dve.tensor_scalar(rs[:, 0:nt], mv[:, 0:nt, 1], LN_EPS, None, ALU.add).then_inc(sem("var"), 1)
                        dve.wait_ge(sem("std"), 1)
                        dve.reciprocal(rs[:, 0:nt], rs[:, 0:nt]).then_inc(sem("rstd"), 1)
                        dve.wait_ge(sem("rstd"), 1)
                        for t in range(nt):
                            dve.tensor_scalar(x[:, t, :], x[:, t, :], mv[:, t, 0:1], rs[:, t:t + 1], ALU.subtract, ALU.mult).then_inc(sem("xn"), 1)
                            dve.wait_ge(sem("xn"), t + 1)
                            dve.tensor_tensor(x[:, t, :], x[:, t, :], lg[:, :], ALU.mult).then_inc(sem("xg"), 1)

                    @block.scalar
                    def _(act):
                        act.wait_ge(sem("var"), 1)
                        act.activation(rs[:, 0:nt], rs[:, 0:nt], ACT.Sqrt).then_inc(sem("std"), 1)

                    @block.gpsimd
                    def _(pool):
                        for t in range(nt):
                            pool.wait_ge(sem("xg"), t + 1)
                            pool.tensor_tensor(x[:, t, :], x[:, t, :], lb[:, :], ALU.add)

        for l in range(DEPTH):
            last = l == DEPTH - 1
            modulation(l)
            with ExitStack() as sc:
                with ExitStack() as s2:
                    h = activation_pair(s2)
                    norm(l, 0, 1, NT, h)
                    rwkv_inputs(l, h, last)
                    with ExitStack() as s3:
                        rwkv_scan(l, s3, h, last)
                oc = sb(sc, "oc", [P, CTILES, TOK])
                rwkv_output(l, oc, last)
                y = sb(sc, "y", [P, KT, TOK])
                with ExitStack() as s2:
                    oa = sb(s2, "oa", [P, HA, TOK])
                    attention(l, oa, last)
                    merge(l, 0, "w_pa", oa, HA, y, last)
                with ExitStack() as s2:
                    of = sb(s2, "of", [P, F_GROUPS, TOK])
                    fourier(l, of, last)
                    merge(l, 1, "w_pf", of, F_GROUPS, y, last)
                merge(l, 2, "w_pc", oc, CTILES, y, last)
                out_proj(l, y, last)
            with ExitStack() as sc:
                hf = sb(sc, "hf", [P, FT, SEQ if last else TOK])
                with ExitStack() as s2:
                    h = activation_pair(s2)
                    norm(l, 3, 4, LT if last else NT, h)
                    ffn(l, hf, h, last)
                ffn_down(l, hf, last)
        with stage(nc) as (block, sem):
            @block.sync
            def _(sp):
                sp.dma_start(out.rearrange("b (t p) d -> p (b t) d", p=P), x[:, 0:LT, :]).then_inc(sem("out"), 16)
                sp.wait_ge(sem("out"), 16)


_INS = ["x", "c", "ctx", "c_ctx", "ada_w", "ada_b", "w_in", "lam_qk", "subln_g", "tshift_mu", "rw_w0", "rw_w2", "rw_a0",
        "rw_a2", "rw_g2", "rw_kk", "rw_ka", "rw_rk", "rw_lnw", "rw_lnb", "w_pa", "w_pf", "w_pc", "w_o", "ln1_g", "ln1_b",
        "ffn_up", "ffn_conv", "ffn_conv_b", "ffn_down", "ln2_g", "ln2_b"]


def kernel(**inputs):
    import numpy as _np
    import concourse.bacc as _bacc
    from concourse import mybir as _mybir
    from concourse.bass_utils import run_bass_kernel_spmd as _run

    nc = _bacc.Bacc("TRN2", target_bir_lowering=False, num_devices=1)
    arrays, aps = {}, {}
    for name, a in [(n, inputs[n]) for n in _INS] + list(tables().items()):
        a = _np.ascontiguousarray(a)
        arrays[f"in_{name}"] = a
        aps[name] = nc.dram_tensor(f"in_{name}", a.shape, _mybir.dt.from_np(a.dtype), kind="ExternalInput").ap()
    out = nc.dram_tensor("out_0", (1, SEQ, D_MODEL), _mybir.dt.float32, kind="ExternalOutput").ap()
    program(nc, aps, out)
    r = _run(nc, [arrays], core_ids=[0])
    return r.results[0]["out_0"]
```
